# Optimizing a Trainium2 kernel written in Bass

```python
import functools
import jax
import jax.numpy as jnp
from jax import lax
import numpy as np

D_MODEL = 1024
BATCH = 1
SEQ = 512
DEPTH = 2
DEC_BATCH = 8
DEC_SEQ = 4
PAST_LEN = 256
PAGE_SIZE = 128

M_HEADS = 4
M_WIDTH = D_MODEL // 2
M_HEAD_DIM = M_WIDTH // M_HEADS
M_CONV = 4
M_CHUNK = 64
HEAD_DIM = 64
N_WIDTH = D_MODEL // 2
N_HEADS = N_WIDTH // HEAD_DIM
N_KV = 2
KV_W = N_KV * HEAD_DIM
CMP_STRIDE = 16
CMP_LEN = 2 * CMP_STRIDE
CMP_HID = 128
SEL_BLOCK = 64
SEL_TOP = 16
WINDOW = 512
Q_BLOCK = 128
ROT_DIM = HEAD_DIM // 4
ROPE_THETA = 500000.0
D_FF = -(-8 * D_MODEL // (3 * 256)) * 256
EPS = 1e-6
NEG = -1e30
TINY = 1e-30
FORCE_SCORE = 1e9
SPLIT_SIZES = (M_WIDTH, M_WIDTH, M_WIDTH, M_HEADS, M_HEADS, N_WIDTH, 6 * KV_W, 3 * N_HEADS, D_MODEL, D_MODEL)
IN_WIDTH = sum(SPLIT_SIZES)

kernel_name = 'hybrid_mlstm_nsa_decoder_step'

def rmsnorm(x, g):
    xf = x.astype(jnp.float32)
    y = xf * lax.rsqrt(jnp.mean(xf * xf, axis=-1, keepdims=True) + EPS) * g.astype(jnp.float32)
    return y.astype(x.dtype)

def split_cols(z):
    pts = [int(p) for p in np.cumsum(SPLIT_SIZES)[:-1]]
    return jnp.split(z, pts, axis=-1)

def rope_partial(x, pos):
    half = ROT_DIM // 2
    inv = ROPE_THETA ** (-jnp.arange(half, dtype=jnp.float32) / half)
    ang = pos.astype(jnp.float32)[:, None] * inv[None, :]
    cos = jnp.cos(ang)[None, :, None, :]
    sin = jnp.sin(ang)[None, :, None, :]
    xf = x.astype(jnp.float32)
    x1 = xf[..., :half]
    x2 = xf[..., half:ROT_DIM]
    out = jnp.concatenate([x1 * cos - x2 * sin, x2 * cos + x1 * sin, xf[..., ROT_DIM:]], axis=-1)
    return out.astype(x.dtype)

def masked_softmax(s, mask):
    s = jnp.where(mask, s.astype(jnp.float32), NEG)
    p = jnp.exp(s - jnp.max(s, axis=-1, keepdims=True)) * mask
    return p / jnp.maximum(jnp.sum(p, axis=-1, keepdims=True), TINY)

def causal_conv(u, buf, w, b):
    T = u.shape[1]
    xp = jnp.concatenate([buf.astype(u.dtype), u], axis=1)
    y = b + sum(xp[:, j:j + T] * w[j] for j in range(M_CONV))
    return jax.nn.silu(y), xp[:, T:]

def mlstm_chunkwise(q, k, v, i_pre, log_f, C0, n0, m0):
    B, T, H, _ = q.shape
    cs = T if T <= M_CHUNK else M_CHUNK
    nc = T // cs

    def to_chunks(a):
        a = a.astype(jnp.float32).reshape((B, nc, cs, H) + a.shape[3:])
        return jnp.moveaxis(a, (1, 3), (0, 2))

    tril = jnp.tril(jnp.ones((cs, cs), dtype=bool))

    def step(carry, inp):
        C, n, m = carry
        qc, kc, vc, ic, fc = inp
        F = jnp.cumsum(fc, axis=-1)
        a = ic - F
        mt = F + jnp.maximum(m[..., None], lax.cummax(a, axis=a.ndim - 1))
        logD = jnp.where(tril, a[..., None, :] + (F - mt)[..., :, None], -jnp.inf)
        S = jnp.einsum('bhtd,bhsd->bhts', qc, kc) * jnp.exp(logD)
        inter = jnp.exp(m[..., None] + F - mt)
        num = jnp.einsum('bhts,bhse->bhte', S, vc) + inter[..., None] * jnp.einsum('bhtd,bhde->bhte', qc, C)
        den = jnp.sum(S, axis=-1) + inter * jnp.einsum('bhtd,bhd->bht', qc, n)
        h = num / jnp.maximum(jnp.abs(den), jnp.exp(-mt))[..., None]
        m_new = mt[..., -1]
        w = jnp.exp(a + (F[..., -1] - m_new)[..., None])
        decay = jnp.exp(m + F[..., -1] - m_new)
        C_new = decay[..., None, None] * C + jnp.einsum('bhs,bhsd,bhse->bhde', w, kc, vc)
        n_new = decay[..., None] * n + jnp.einsum('bhs,bhsd->bhd', w, kc)
        return (C_new, n_new, m_new), h

    init = (C0.astype(jnp.float32), n0.astype(jnp.float32), m0.astype(jnp.float32))
    (C, n, m), h = lax.scan(step, init, (to_chunks(q), to_chunks(k), to_chunks(v), to_chunks(i_pre), to_chunks(log_f)))
    h = jnp.moveaxis(h, (0, 2), (1, 3)).reshape(B, T, H, v.shape[-1])
    return h, C, n, m

def mlstm_branch(u, v, o, ig, fg, conv_buf, C0, n0, m0, conv_w, conv_b, w_mq, w_mk, b_gates, norm_g):
    B, T, _ = u.shape
    c, conv_new = causal_conv(u, conv_buf, conv_w, conv_b)
    c = c.reshape(B, T, M_HEADS, M_HEAD_DIM)
    q = jnp.einsum('bthd,hde->bthe', c, w_mq)
    k = jnp.einsum('bthd,hde->bthe', c, w_mk) * (M_HEAD_DIM ** -0.5)
    v = v.reshape(B, T, M_HEADS, M_HEAD_DIM)
    pre = jnp.concatenate([ig, fg], axis=-1).astype(jnp.float32) + b_gates.astype(jnp.float32)
    i_pre = pre[..., :M_HEADS]
    log_f = jax.nn.log_sigmoid(pre[..., M_HEADS:])
    h, C, n, m = mlstm_chunkwise(q, k, v, i_pre, log_f, C0, n0, m0)
    h = h * lax.rsqrt(jnp.mean(h * h, axis=-1, keepdims=True) + EPS) * norm_g.astype(jnp.float32).reshape(M_HEADS, M_HEAD_DIM)
    out = h.reshape(B, T, M_WIDTH) * jax.nn.sigmoid(o.astype(jnp.float32))
    return out.astype(u.dtype), conv_new, C, n, m

def compress(raw, pe, w1, w2):
    B, L = raw.shape[:2]
    n_chunk = L // CMP_STRIDE
    ch = raw[:, :n_chunk * CMP_STRIDE].reshape(B, n_chunk, CMP_STRIDE, N_KV, HEAD_DIM)
    blocks = jnp.concatenate([ch[:, :-1], ch[:, 1:]], axis=2) + pe[None, None, :, None, :]
    hid = jax.nn.gelu(jnp.einsum('bnlgd,lde->bnge', blocks, w1))
    return jnp.einsum('bnge,ef->bngf', hid, w2)

def sel_overlap(n_cmp, n_blk):
    start = np.arange(n_cmp) * CMP_STRIDE
    bs = np.arange(n_blk) * SEL_BLOCK
    ov = np.minimum(start[:, None] + CMP_LEN, bs[None, :] + SEL_BLOCK) - np.maximum(start[:, None], bs[None, :])
    return jnp.asarray(np.clip(ov, 0, None) / CMP_LEN, dtype=jnp.float32)

def gather_rows(kv, idx):
    return jax.vmap(jax.vmap(lambda a, i: a[i]))(kv, idx)

def nsa_core(q, q_rot, qpos, kc, vc, cmp_end, k_sel, v_sel, kw, vw, kwpos, gates):
    B, Q = q.shape[:2]
    L = k_sel.shape[1]
    R = N_HEADS // N_KV
    scale = HEAD_DIM ** -0.5
    qp = q.reshape(B, Q, N_KV, R, HEAD_DIM)
    qr = q_rot.reshape(B, Q, N_KV, R, HEAD_DIM)
    p_c = masked_softmax(jnp.einsum('bqgrd,bngd->bgrqn', qp, kc) * scale, cmp_end[None, :] <= qpos[:, None])
    o_c = jnp.einsum('bgrqn,bngd->bqgrd', p_c, vc)
    n_blk = -(-L // SEL_BLOCK)
    imp = jnp.einsum('bgrqn,nj->bgqj', p_c, sel_overlap(kc.shape[1], n_blk))
    blk = jnp.arange(n_blk)[None, :]
    cur = (qpos // SEL_BLOCK)[:, None]
    forced = (blk == 0) | (blk == cur) | (blk == cur - 1)
    score = jnp.where(blk <= cur, jnp.where(forced, FORCE_SCORE, imp), -1.0)
    _, top = lax.top_k(score, min(SEL_TOP, n_blk))
    tok = (top[..., None] * SEL_BLOCK + jnp.arange(SEL_BLOCK)).reshape(B, N_KV, Q, -1)
    idx = jnp.minimum(tok, L - 1)
    ks = gather_rows(jnp.swapaxes(k_sel, 1, 2), idx)
    vs = gather_rows(jnp.swapaxes(v_sel, 1, 2), idx)
    p_s = masked_softmax(jnp.einsum('bqgrd,bgqnd->bgrqn', qr, ks) * scale, (tok <= qpos[:, None])[:, :, None])
    o_s = jnp.einsum('bgrqn,bgqnd->bqgrd', p_s, vs)
    dpos = qpos[:, None] - kwpos[None, :]
    mask_w = (dpos >= 0) & (dpos < WINDOW) & (kwpos[None, :] >= 0)
    p_w = masked_softmax(jnp.einsum('bqgrd,bkgd->bgrqk', qr, kw) * scale, mask_w)
    o_w = jnp.einsum('bgrqk,bkgd->bqgrd', p_w, vw)
    g = gates.reshape(B, Q, N_KV, R, 3)
    out = g[..., 0:1] * o_c + g[..., 1:2] * o_s + g[..., 2:3] * o_w
    return out.reshape(B, Q, N_WIDTH).astype(q.dtype)

def nsa_prompt(q, q_rot, pos, k_cmp, v_cmp, k_sel, v_sel, k_win, v_win, gates, cmp):
    pe_k, pe_v, w1_k, w2_k, w1_v, w2_v = cmp
    B, T = q.shape[:2]
    kc = compress(k_cmp, pe_k, w1_k, w2_k)
    vc = compress(v_cmp, pe_v, w1_v, w2_v)
    cmp_end = jnp.arange(kc.shape[1]) * CMP_STRIDE + (CMP_LEN - 1)
    pad = ((0, 0), (WINDOW, 0), (0, 0), (0, 0))
    kw_pad = jnp.pad(k_win, pad)
    vw_pad = jnp.pad(v_win, pad)

    def one_block(i):
        s0 = i * Q_BLOCK
        take = lambda a, n: lax.dynamic_slice_in_dim(a, s0, n, axis=1)
        qpos = lax.dynamic_slice_in_dim(pos, s0, Q_BLOCK)
        kwpos = qpos[0] - WINDOW + jnp.arange(WINDOW + Q_BLOCK)
        return nsa_core(take(q, Q_BLOCK), take(q_rot, Q_BLOCK), qpos, kc, vc, cmp_end, k_sel, v_sel,
                        take(kw_pad, WINDOW + Q_BLOCK), take(vw_pad, WINDOW + Q_BLOCK), kwpos, take(gates, Q_BLOCK))

    out = lax.map(one_block, jnp.arange(T // Q_BLOCK))
    out = jnp.moveaxis(out, 0, 1).reshape(B, T, N_WIDTH)
    wp = min(WINDOW, T)
    return out, jnp.stack([k_win[:, -wp:], v_win[:, -wp:]], axis=2)

def nsa_sample(q, q_rot, pos, k_cmp, v_cmp, k_sel, v_sel, k_win, v_win, gates, cmp, past, win_buf):
    pe_k, pe_v, w1_k, w2_k, w1_v, w2_v = cmp
    T = q.shape[1]
    P = past.shape[1]
    WB = win_buf.shape[1]
    full = lambda i, new: jnp.concatenate([past[:, :, i].astype(new.dtype), new], axis=1)
    kc = compress(full(0, k_cmp), pe_k, w1_k, w2_k)
    vc = compress(full(1, v_cmp), pe_v, w1_v, w2_v)
    cmp_end = jnp.arange(kc.shape[1]) * CMP_STRIDE + (CMP_LEN - 1)
    kw = jnp.concatenate([win_buf[:, :, 0].astype(k_win.dtype), k_win], axis=1)
    vw = jnp.concatenate([win_buf[:, :, 1].astype(v_win.dtype), v_win], axis=1)
    kwpos = P - WB + jnp.arange(WB + T)
    out = nsa_core(q, q_rot, pos, kc, vc, cmp_end, full(2, k_sel), full(3, v_sel), kw, vw, kwpos, gates)
    return out, jnp.stack([kw[:, -WB:], vw[:, -WB:]], axis=2)

def layer_step(x, pos, W, l, conv_buf, C0, n0, m0, nsa_fn):
    B, T, _ = x.shape
    h = rmsnorm(x, W['norm1_g'][l])
    u, v, o, ig, fg, q, kv, ng, ga, gb = split_cols(h @ W['w_in'][l])
    h_a, conv_new, C, n, m = mlstm_branch(u, v, o, ig, fg, conv_buf, C0, n0, m0, W['conv_w'][l], W['conv_b'][l],
                                          W['w_mq'][l], W['w_mk'][l], W['b_gates'][l], W['mlstm_norm_g'][l])
    q = q.reshape(B, T, N_HEADS, HEAD_DIM)
    kv = kv.reshape(B, T, 6, N_KV, HEAD_DIM)
    k_cmp, v_cmp, v_sel, v_win = kv[:, :, 0], kv[:, :, 1], kv[:, :, 3], kv[:, :, 5]
    k_sel = rope_partial(kv[:, :, 2], pos)
    k_win = rope_partial(kv[:, :, 4], pos)
    q_rot = rope_partial(q, pos)
    gates = jax.nn.sigmoid(ng.astype(jnp.float32)).reshape(B, T, N_HEADS, 3)
    h_b, win_new = nsa_fn(q, q_rot, pos, k_cmp, v_cmp, k_sel, v_sel, k_win, v_win, gates)
    merged = jax.nn.sigmoid(ga) * (h_a @ W['w_branch_a'][l]) + jax.nn.sigmoid(gb) * (h_b @ W['w_branch_b'][l])
    x = x + merged.astype(x.dtype) @ W['w_out'][l]
    g_ff, u_ff = jnp.split(rmsnorm(x, W['norm2_g'][l]) @ W['w_ffn_up'][l], 2, axis=-1)
    x = x + (jax.nn.silu(g_ff) * u_ff) @ W['w_ffn_down'][l]
    kv_rows = jnp.stack([k_cmp, v_cmp, k_sel, v_sel], axis=2)
    return x, kv_rows, win_new, C, n, m, conv_new

def setup_inputs(seed: int = 0) -> dict:
    key = jax.random.key(seed)
    ks = jax.random.split(key, 40)
    nrm = lambda i, shape, s: s * jax.random.normal(ks[i], shape, dtype=jnp.float32)
    n_pages = PAST_LEN // PAGE_SIZE
    n_used = DEC_BATCH * n_pages
    n_pool = n_used + n_used // 4
    page_table = jax.random.permutation(ks[0], n_pool)[:n_used].reshape(DEC_BATCH, n_pages).astype(jnp.int32)
    wb = min(WINDOW, PAST_LEN)
    b_gates = jnp.concatenate([nrm(1, (DEPTH, M_HEADS), 0.1),
                               jnp.linspace(3.0, 6.0, M_HEADS, dtype=jnp.float32)[None, :] + nrm(2, (DEPTH, M_HEADS), 0.1)], axis=1)
    return {
        'x_prompt': nrm(3, (BATCH, SEQ, D_MODEL), 1.0),
        'x_sample': nrm(4, (DEC_BATCH, DEC_SEQ, D_MODEL), 1.0),
        'cache_kv_pages': nrm(5, (DEPTH, n_pool, PAGE_SIZE, 4, N_KV, HEAD_DIM), 1.0),
        'page_table': page_table,
        'cache_win': nrm(6, (DEPTH, DEC_BATCH, wb, 2, N_KV, HEAD_DIM), 1.0),
        'state_mlstm_C': nrm(7, (DEPTH, DEC_BATCH, M_HEADS, M_HEAD_DIM, M_HEAD_DIM), 0.5),
        'state_mlstm_n': nrm(8, (DEPTH, DEC_BATCH, M_HEADS, M_HEAD_DIM), 0.5),
        'state_mlstm_m': nrm(9, (DEPTH, DEC_BATCH, M_HEADS), 1.0),
        'state_mlstm_conv': nrm(10, (DEPTH, DEC_BATCH, M_CONV - 1, M_WIDTH), 1.0),
        'norm1_g': 1.0 + nrm(11, (DEPTH, D_MODEL), 0.01),
        'w_in': nrm(12, (DEPTH, D_MODEL, IN_WIDTH), D_MODEL ** -0.5),
        'b_gates': b_gates,
        'conv_w': nrm(13, (DEPTH, M_CONV, M_WIDTH), M_CONV ** -0.5),
        'conv_b': nrm(14, (DEPTH, M_WIDTH), 0.01),
        'w_mq': nrm(15, (DEPTH, M_HEADS, M_HEAD_DIM, M_HEAD_DIM), M_HEAD_DIM ** -0.5),
        'w_mk': nrm(16, (DEPTH, M_HEADS, M_HEAD_DIM, M_HEAD_DIM), M_HEAD_DIM ** -0.5),
        'mlstm_norm_g': 1.0 + nrm(17, (DEPTH, M_WIDTH), 0.01),
        'cmp_pe_k': nrm(18, (DEPTH, CMP_LEN, HEAD_DIM), 0.02),
        'cmp_pe_v': nrm(19, (DEPTH, CMP_LEN, HEAD_DIM), 0.02),
        'cmp_w1_k': nrm(20, (DEPTH, CMP_LEN, HEAD_DIM, CMP_HID), (CMP_LEN * HEAD_DIM) ** -0.5),
        'cmp_w2_k': nrm(21, (DEPTH, CMP_HID, HEAD_DIM), CMP_HID ** -0.5),
        'cmp_w1_v': nrm(22, (DEPTH, CMP_LEN, HEAD_DIM, CMP_HID), (CMP_LEN * HEAD_DIM) ** -0.5),
        'cmp_w2_v': nrm(23, (DEPTH, CMP_HID, HEAD_DIM), CMP_HID ** -0.5),
        'w_branch_a': nrm(24, (DEPTH, M_WIDTH, D_MODEL), M_WIDTH ** -0.5),
        'w_branch_b': nrm(25, (DEPTH, N_WIDTH, D_MODEL), N_WIDTH ** -0.5),
        'w_out': nrm(26, (DEPTH, D_MODEL, D_MODEL), D_MODEL ** -0.5),
        'norm2_g': 1.0 + nrm(27, (DEPTH, D_MODEL), 0.01),
        'w_ffn_up': nrm(28, (DEPTH, D_MODEL, 2 * D_FF), D_MODEL ** -0.5),
        'w_ffn_down': nrm(29, (DEPTH, D_FF, D_MODEL), D_FF ** -0.5),
        'final_norm_g': 1.0 + nrm(30, (D_MODEL,), 0.01),
    }

def reference(x_prompt, x_sample, cache_kv_pages, page_table, cache_win, state_mlstm_C, state_mlstm_n, state_mlstm_m,
              state_mlstm_conv, norm1_g, w_in, b_gates, conv_w, conv_b, w_mq, w_mk, mlstm_norm_g, cmp_pe_k, cmp_pe_v,
              cmp_w1_k, cmp_w2_k, cmp_w1_v, cmp_w2_v, w_branch_a, w_branch_b, w_out, norm2_g, w_ffn_up, w_ffn_down,
              final_norm_g):
    W = {'norm1_g': norm1_g, 'w_in': w_in, 'b_gates': b_gates, 'conv_w': conv_w, 'conv_b': conv_b, 'w_mq': w_mq,
         'w_mk': w_mk, 'mlstm_norm_g': mlstm_norm_g, 'w_branch_a': w_branch_a, 'w_branch_b': w_branch_b,
         'w_out': w_out, 'norm2_g': norm2_g, 'w_ffn_up': w_ffn_up, 'w_ffn_down': w_ffn_down}
    Bp, Tp, _ = x_prompt.shape
    Bs, Ts, _ = x_sample.shape
    n_pages = page_table.shape[1]
    past_len = n_pages * cache_kv_pages.shape[2]
    pos_p = jnp.arange(Tp)
    pos_s = past_len + jnp.arange(Ts)

    xp = x_prompt
    xs = x_sample
    p_kv, p_win, p_C, p_n, p_m, p_conv = [], [], [], [], [], []
    s_kv, s_win, s_C, s_n, s_m, s_conv = [], [], [], [], [], []
    for l in range(DEPTH):
        cmp = (cmp_pe_k[l], cmp_pe_v[l], cmp_w1_k[l], cmp_w2_k[l], cmp_w1_v[l], cmp_w2_v[l])
        xp, kv_r, win_r, C, n, m, cv = layer_step(
            xp, pos_p, W, l,
            jnp.zeros((Bp, M_CONV - 1, M_WIDTH), xp.dtype),
            jnp.zeros((Bp, M_HEADS, M_HEAD_DIM, M_HEAD_DIM), jnp.float32),
            jnp.zeros((Bp, M_HEADS, M_HEAD_DIM), jnp.float32),
            jnp.zeros((Bp, M_HEADS), jnp.float32),
            functools.partial(nsa_prompt, cmp=cmp))
        p_kv.append(kv_r); p_win.append(win_r); p_C.append(C); p_n.append(n); p_m.append(m); p_conv.append(cv)
        past = cache_kv_pages[l][page_table].reshape(Bs, past_len, 4, N_KV, HEAD_DIM)
        xs, kv_r, win_r, C, n, m, cv = layer_step(
            xs, pos_s, W, l, state_mlstm_conv[l], state_mlstm_C[l], state_mlstm_n[l], state_mlstm_m[l],
            functools.partial(nsa_sample, cmp=cmp, past=past, win_buf=cache_win[l]))
        s_kv.append(kv_r); s_win.append(win_r); s_C.append(C); s_n.append(n); s_m.append(m); s_conv.append(cv)

    y_prompt = rmsnorm(xp, final_norm_g)
    y_sample = rmsnorm(xs, final_norm_g)
    new_p_kv = jnp.stack(p_kv)
    new_p_win = jnp.stack(p_win)
    new_p_C = jnp.stack(p_C)
    new_p_n = jnp.stack(p_n)
    new_p_m = jnp.stack(p_m)
    new_p_conv = jnp.stack(p_conv)
    new_s_kv = jnp.stack(s_kv)
    new_s_win = jnp.stack(s_win)
    new_s_C = jnp.stack(s_C)
    new_s_n = jnp.stack(s_n)
    new_s_m = jnp.stack(s_m)
    new_s_conv = jnp.stack(s_conv)
    return (y_prompt, y_sample, new_p_kv, new_p_win, new_p_C, new_p_n, new_p_m, new_p_conv,
            new_s_kv, new_s_win, new_s_C, new_s_n, new_s_m, new_s_conv)


_drawn_inputs = setup_inputs


def setup_inputs(seed=0):
    import zlib

    import numpy as np

    out = dict(_drawn_inputs(seed))
    spreads = {}
    factors = {'norm1_g': 2.892,
     'mlstm_norm_g': 8.0,
     'cmp_pe_k': 8.0,
     'cmp_pe_v': 8.0,
     'norm2_g': 5.351,
     'final_norm_g': 5.501}
    for name, (base, spread) in spreads.items():
        noise = np.random.default_rng([zlib.crc32(name.encode()), seed]).standard_normal(out[name].shape)
        drawn = base * np.exp(spread * noise) if base else spread * noise
        out[name] = jnp.asarray(drawn.astype(out[name].dtype))
    for name, factor in factors.items():
        out[name] = (out[name] * factor).astype(out[name].dtype)
    return out
```

```python
from contextlib import ExitStack

import numpy as np

import concourse.bass as bass
from concourse import mybir

ALU = mybir.AluOpType
ACT = mybir.ActivationFunctionType
F32 = mybir.dt.float32
I32 = mybir.dt.int32
AX = mybir.AxisListType

P = 128
DEPTH, D, SEQ, DECB, DECT, PAST, PAGE = 2, 1024, 512, 8, 4, 256, 128
KC = D // P
NS = DECB * DECT
N = SEQ + NS
NHALF = N // 2
MH, MD = 4, 128
NH, NKV, HD = 8, 2, 64
R = NH // NKV
CONV = 4
STRIDE, CLEN, HID = 16, 32, 128
NFF = 2816 // P
TT = SEQ // P
NPG = PAST // PAGE
EPS, NEG, TINY = 1e-6, -1e30, 1e-30
RAW = SEQ + DECB * PAST
NBLK = RAW // STRIDE
NCP = SEQ // STRIDE - 1
PBLK = SEQ // STRIDE
SBLK = PAST // STRIDE
UW = (CONV - 1) + SEQ + DECB * (CONV - 1 + DECT)

UNITS = ([("tm", k) for k in range(KC)] + [("u", m) for m in range(4)] + [("if", 0)]
         + [("o", m) for m in range(4)] + [("q", m) for m in range(4)] + [("k", m) for m in range(4)]
         + [("w1", n) for n in range(8)]
         + [(w, m) for m in range(KC) for w in ("ga", "gb", "ab")]
         + [("out", m) for m in range(KC)]
         + [(w, m) for m in range(NFF) for w in ("fg", "fu")]
         + [("dn", n) for n in range(3 * KC)])
UNIT = {key: n for n, key in enumerate(UNITS)}
RING = 9
UCOLS = 1024
TMC = 512 + 280

GROUPS = ([("n1", 0)] + [("tm", i) for i in range(TT + 1)] + [("u", m) for m in range(4)] + [("if", 0)]
          + [("o", m) for m in range(4)] + [(w, h) for h in range(MH) for w in ("mq", "mk")]
          + [("aw", 0)] + [("kw", i) for i in range(TT + 1)]
          + [("mn", h) for h in range(MH)]
          + [("q", m) for m in range(4)] + [("k", m) for m in range(4)] + [("rope", n) for n in range(6)]
          + [(w, m) for m in range(KC) for w in ("ga", "gb", "a", "b")]
          + [("out", m) for m in range(KC)] + [("n2", 0)]
          + [(w, m) for m in range(NFF) for w in ("fg", "fu")]
          + [("dn", m) for m in range(KC)])
GROUP = {key: n for n, key in enumerate(GROUPS)}
CORE_AT = GROUP[("mn", 0)]
ATTN_AT = GROUP[("ga", 0)]


def columns(spec):
    at, out = 0, {}
    for name, width in spec:
        out[name] = (at, at + width)
        at += width
    return out, at


SMALL, SMALL_W = columns([("n1g", KC), ("n2g", KC), ("mng", MH), ("cw", 4 * CONV), ("cb", 4), ("wmq", MH * MD),
                          ("wmk", MH * MD), ("w2", 2 * HD), ("pe", 2 * CLEN), ("bi", 1), ("bf", 1), ("m0", DECB),
                          ("n0", MH * DECB), ("cs", 4 * DECB * (CONV - 1))])
CONST, CONST_W = columns([("cos", N), ("sin", N), ("rot", P), ("ident", P), ("qneg", P), ("sneg", P),
                          ("cneg", TT * NCP), ("c01", TT * NCP), ("sel4", MH * P), ("m32", NS), ("blk", DECB),
                          ("nneg", 2 * NS), ("kneg", 2 * P), ("tsel", 2 * P), ("rowm", NH), ("fng", KC)])


def arena(spec):
    return columns(spec)


MIX, MIX_W = arena([("upad", 4 * UW), ("cT", 4 * N), ("ctmp", 2 * N), ("qm", MH * N), ("km", MH * N),
                    ("vtm", (TT + 1) * 512), ("kw", (TT + 1) * 512), ("C", 2 * DECB * MD), ("vb", DECB * MD),
                    ("rows", 4 * N + 64)])
CORE, CORE_W = arena([("gbc", 2 * N), ("enm", 2 * N), ("int", 2 * NS), ("E", 2 * 512), ("St", 2 * 512),
                      ("qi", 2 * NS), ("gmask", P), ("pC", MH * MD)])
assert CORE_W <= 4 * UW + 4 * N + 2 * N
NSA, NSA_W = arena([("qT", 4 * N), ("qrT", 4 * N), ("kT", 2 * N), ("raw", 2 * (RAW + NS)), ("selp", DECB * 2 * NPG * P),
                    ("P", 2 * 2 * 512), ("D", 2 * 2 * P), ("PT", 2 * 512), ("qb", 2 * DECB * 32), ("hid", 2 * 2 * NBLK),
                    ("kcT", NBLK), ("vcp", P), ("vcs", P), ("rtmp", 2 * N)])
FFN, FFN_W = arena([("act", NFF * N), ("merged", KC * N), ("sg", 2 * N), ("mt", 2 * N)])
ARENA_W = max(MIX_W, NSA_W, FFN_W)


def build_step(nc, xT_in, W_in, small_in, const_in, c0_in, pages_in, table_in, win_in, cwin_in,
               y_out, fm_out, tm_out, u_out, pC_out, pn_out, m_out, sC_out, oldwin_out):
    with ExitStack() as ctx:
        def sb(name, shape, dt=F32):
            return ctx.enter_context(nc.sbuf_tensor(name, shape, dt))

        def sem(name):
            s = ctx.enter_context(nc.semaphore(name))
            layer_sems.append(s)
            return s

        layer_sems = []
        xT = sb("xT", [P, KC, N])
        hT = sb("hT", [P, KC, N])
        ring = sb("ring", [P, RING, UCOLS])
        const = sb("const", [P, CONST_W])
        small = sb("small", [P, SMALL_W])
        haT = sb("haT", [P, MH, N])
        hbT = sb("hbT", [P, R, N])
        hbrows = hbT
        sq = sb("sq", [P, 2, N])
        rstd = sb("rstd", [P, N])
        vkv = sb("vkv", [P, TT + 1, 2 * P])
        gate = sb("gate", [P, TT + 1, NH * 3])
        ones = sb("ones", [P, P])
        eps = sb("eps", [P, 1])
        awt = sb("awt", [P, TT + 1, 2, MH])
        stat = sb("stat", [P, 16, 2])
        nstat = sb("nstat", [P, MH, 1 + DECB])
        gsel = sb("gsel", [P, 2, 3])
        gtmp = sb("gtmp", [P, 3, NH])
        hbias = sb("hbias", [P, 2])
        table = sb("table", [1, DECB * NPG], I32)
        big = sb("arena", [P, ARENA_W])
        ps = ctx.enter_context(nc.psum_tensor("ps", [P, 8, 512], F32))

        def cut(lay, name, pattern=None, base=None, **k):
            a, b = lay[name]
            v = (big if base is None else base)[:, a:b]
            return v.rearrange(pattern, **k) if pattern else v

        def con(name, pattern=None, **k):
            return cut(CONST, name, pattern, const, **k)

        def sml(name, pattern=None, **k):
            return cut(SMALL, name, pattern, small, **k)

        upad = cut(MIX, "upad", "p (c n) -> p c n", c=4)
        cT = cut(MIX, "cT", "p (c n) -> p c n", c=4)
        ctmp = cut(MIX, "ctmp", "p (c n) -> p c n", c=2)
        qm = cut(MIX, "qm", "p (c n) -> p c n", c=MH)
        km = cut(MIX, "km", "p (c n) -> p c n", c=MH)
        vtm = cut(MIX, "vtm", "p (i n) -> p i n", n=512)
        kw = cut(MIX, "kw", "p (i n) -> p i n", n=512)
        Cst = cut(MIX, "C", "p (a b e) -> p a b e", a=2, b=DECB)
        vb = cut(MIX, "vb", "p (b e) -> p b e", b=DECB)
        rowsx = cut(MIX, "rows")
        pCs = cut(CORE, "pC", "p (h e) -> p h e", h=MH)
        gbc = cut(CORE, "gbc", "p (a n) -> p a n", a=2)
        enm = cut(CORE, "enm", "p (a n) -> p a n", a=2)
        inter = cut(CORE, "int", "p (a n) -> p a n", a=2)
        Et = cut(CORE, "E", "p (a n) -> p a n", a=2)
        St = cut(CORE, "St", "p (a n) -> p a n", a=2)
        qi = cut(CORE, "qi", "p (a n) -> p a n", a=2)
        gmask = cut(CORE, "gmask")
        qT = cut(NSA, "qT", "p (c n) -> p c n", c=4)
        qrT = cut(NSA, "qrT", "p (c n) -> p c n", c=4)
        kT = cut(NSA, "kT", "p (c n) -> p c n", c=2)
        raw = cut(NSA, "raw", "p (c n) -> p c n", c=2)
        winp = cut(NSA, "raw")[:, 0:DECB * 2 * NPG * P].rearrange("p (b v j s) -> p b v j s", b=DECB, v=2, j=NPG)
        selp = cut(NSA, "selp", "p (b j v s) -> p b j v s", b=DECB, j=NPG, v=2)
        Pt = cut(NSA, "P", "p (a r n) -> p a r n", a=2, r=2)
        Dg = cut(NSA, "D", "p (a r n) -> p a r n", a=2, r=2)
        PT = cut(NSA, "PT", "p (a n) -> p a n", a=2)
        qb = cut(NSA, "qb", "p (a b m) -> p a b m", a=2, b=DECB)
        hid = cut(NSA, "hid", "p (v g n) -> p v g n", v=2, g=2)
        kcT = cut(NSA, "kcT")
        vcp = cut(NSA, "vcp")
        vcs = cut(NSA, "vcs")
        rtmp = cut(NSA, "rtmp", "p (a n) -> p a n", a=2)
        act_ = cut(FFN, "act", "p (c n) -> p c n", c=NFF)
        merged = cut(FFN, "merged", "p (c n) -> p c n", c=KC)
        sg = cut(FFN, "sg", "p (a n) -> p a n", a=2)
        mt = cut(FFN, "mt", "p (a n) -> p a n", a=2)

        def row(n):
            if n < 4:
                return hbrows[0:MH, n, :]
            return rowsx[0:MH, (n - 4) * N:(n - 3) * N]

        I_, Z_, L_, F_, M_, A_, G_, W_ = range(8)
        EN_, IN_ = L_, None
        introw = rowsx[0:MH, 4 * N:4 * N + NS]
        tmprow = rowsx[0:MH, 4 * N + NS:4 * N + 2 * NS]

        def per_seq(r):
            return r.rearrange("p (b t) -> p b t", t=DECT)

        def halves(v):
            return v.rearrange("p (a n) -> p a n", a=2)

        def pair(q, cols=NHALF, rows=P):
            s = q % 4
            return ps[0:rows, 2 * s:2 * s + 2, 0:cols]

        def bc(ap, shape):
            return ap.to_broadcast(shape)

        cos, sin, ident = con("cos"), con("sin"), con("ident")
        rot = con("rot")
        sel4 = con("sel4", "p (h n) -> p h n", h=MH)
        cneg = con("cneg", "p (i n) -> p i n", i=TT)
        c01 = con("c01", "p (i n) -> p i n", i=TT)
        nneg = con("nneg", "p (a n) -> p a n", a=2)
        kneg = con("kneg", "p (a n) -> p a n", a=2)
        tsel = con("tsel", "p (a n) -> p a n", a=2)

        unit_landed = [sem(f"unit_landed{s}") for s in range(RING)]
        pair_done = sem("pair_done")
        pair_free = [sem(f"pair_free{s}") for s in range(4)]
        small_landed = sem("small_landed")
        raw_landed = sem("raw_landed")
        sel_landed = sem("sel_landed")
        win_landed = sem("win_landed")
        c0_landed = [sem(f"c0_landed{s}") for s in range(2)]
        stored = sem("stored")
        cstored = sem("cstored")
        history_ready = sem("history_ready")
        tm_used = sem("tm_used")
        w1_used = sem("w1_used")
        dn_used = sem("dn_used")
        u_stored = sem("u_stored")
        mix_stored = sem("mix_stored")
        raw_stored = sem("raw_stored")
        nsa_stored = sem("nsa_stored")
        num_read = sem("num_read")
        pn_ready = sem("pn_ready")
        sq_ready = sem("sq_ready")
        sq_used = sem("sq_used")
        h_ready = sem("h_ready")
        conv_ready = sem("conv_ready")
        c_ready = sem("c_ready")
        ln_ready = sem("ln_ready")
        rows_ready = sem("rows_ready")
        wexp_ready = sem("wexp_ready")
        bc_done = sem("bc_done")
        bc_ready = sem("bc_ready")
        ms_done = sem("ms_done")
        gm_ready = sem("gm_ready")
        e_ready = sem("e_ready")
        st_ready = sem("st_ready")
        nd_done = sem("nd_done")
        head_fin = sem("head_fin")
        qi_ready = sem("qi_ready")
        msq_ready = sem("msq_ready")
        ha_ready = sem("ha_ready")
        vb_ready = sem("vb_ready")
        cs_done = sem("cs_done")
        pc_done = sem("pc_done")
        pc_ready = sem("pc_ready")
        rope_ready = sem("rope_ready")
        hid_ready = sem("hid_ready")
        cmp_done = sem("cmp_done")
        cmp_ready = sem("cmp_ready")
        qb_ready = sem("qb_ready")
        s_done = sem("s_done")
        max_ready = sem("max_ready")
        exp_done = sem("exp_done")
        d_ready = sem("d_ready")
        t_done = sem("t_done")
        t_free = [sem(f"t_free{s}") for s in range(2)]
        o_done = sem("o_done")
        hb_ready = sem("hb_ready")
        gs_done = sem("gs_done")
        merged_ready = sem("merged_ready")
        dve_step = sem("dve_step")
        act_step = sem("act_step")
        pool_step = sem("pool_step")

        first_sems = len(layer_sems)
        start_landed = ctx.enter_context(nc.semaphore("start_landed"))
        start_step = ctx.enter_context(nc.semaphore("start_step"))

        with nc.Block() as block:
            @block.sync
            def _(sp):
                sp.dma_start(const[:, :], const_in).then_inc(start_landed, 16)
                sp.dma_start(xT[:, :, :], xT_in).then_inc(start_landed, 16)
                sp.dma_start(table[:, :], table_in).then_inc(start_landed, 16)
                sp.wait_ge(start_landed, 48)

            @block.vector
            def _(dve):
                dve.memset(ones[:, :], 1.0).then_inc(start_step, 1)
                dve.memset(eps[:, :], EPS).then_inc(start_step, 1)
                dve.wait_ge(start_step, 2)

        STEPS = [(i, g, rp, br) for i in range(TT) for g in range(NKV) for rp in range(2) for br in range(3)]
        CHUNKS = []
        for k, (i, g, rp, br) in enumerate(STEPS):
            for j in range(0, 1 if br == 0 else i + 1, 2):
                CHUNKS.append((k, j, 1 if br == 0 else min(2, i + 1 - j)))
        NPC = len(CHUNKS)
        SSTEPS = [(hb, br) for hb in range(2) for br in range(3)]
        NSTEP = len(STEPS)

        def chunks_of(k):
            return [(x, j, nj) for x, (kk, j, nj) in enumerate(CHUNKS) if kk == k]

        def evac_on_act(x):
            return x >= NPC or CHUNKS[x][1] > 0

        def read_out(eng, key):
            q = GROUP[key]
            eng.wait_ge(pair_free[q % 4], q // 4 + 1)

        def unit_used(eng, n):
            kind, m = UNITS[n]
            if kind == "tm" and m < KC - 1:
                eng.wait_ge(tm_used, m + 1)
            elif kind == "w1":
                eng.wait_ge(w1_used, m + 1)
            elif kind == "dn" and m % 3 < 2:
                eng.wait_ge(dn_used, 2 * (m // 3) + m % 3 + 1)
            else:
                group = {"tm": ("tm", TT), "ab": ("b", m), "dn": ("dn", m // 3)}.get(kind, (kind, m))
                eng.wait_ge(pair_done, GROUP[group] + 1)

        with nc.Fori(0, DEPTH) as layer:
            with nc.Block() as block:
                @block.sync
                def _(sp):
                    sp.dma_start(small[:, :], small_in[bass.ds(layer, 1)].rearrange("l p n -> (l p) n")).then_inc(small_landed, 16)

                    def unit(n):
                        if n >= RING:
                            unit_used(sp, n - RING)
                        sp.dma_start(ring[:, n % RING, :],
                                     W_in[bass.ds(layer, 1), n].rearrange("l p n -> (l p) n")).then_inc(unit_landed[n % RING], 16)

                    for n in range(len(UNITS)):
                        unit(n)
                    sp.wait_ge(stored, 32)
                    sp.wait_ge(u_stored, 16)
                    sp.wait_ge(mix_stored, 32)
                    sp.wait_ge(cstored, 16 * MH)
                    sp.wait_ge(raw_stored, 32)
                    sp.wait_ge(nsa_stored, 48)

                @block.gpsimd
                def _(pool):
                    pool.dma_start(oldwin_out[bass.ds(layer, 1)].rearrange("l b n -> (l b) n"),
                                   cwin_in[bass.ds(layer, 1)].rearrange("l b n -> (l b) n")[:, DECT * 2 * P:PAST * 2 * P]).then_inc(stored, 16)

                    def load_c0(h):
                        pool.dma_start(Cst[:, h % 2, :, :].rearrange("p b e -> p (b e)"),
                                       c0_in[bass.ds(layer, 1), h].rearrange("l p n -> (l p) n")).then_inc(c0_landed[h % 2], 16)

                    load_c0(0)
                    load_c0(1)
                    pool.wait_ge(small_landed, 16)
                    pool.memset(upad[:, :, 0:CONV - 1], 0.0)
                    us = upad[:, :, CONV - 1 + SEQ:UW].rearrange("p c (b t) -> p c b t", b=DECB)
                    cs = sml("cs", "p (c b t) -> p c b t", c=4, b=DECB)
                    for c in range(4):
                        last = pool.tensor_copy(us[:, c, :, 0:CONV - 1], cs[:, c])
                    last.then_inc(history_ready, 1)
                    pool.wait_ge(history_ready, 1)
                    for m in range(4):
                        read_out(pool, ("u", m))
                    pool.dma_start(u_out[bass.ds(layer, 1)].rearrange("l p c n -> (l p) c n"), upad[:, :, SEQ:UW]).then_inc(u_stored, 16)
                    pool.wait_ge(rows_ready, 1)
                    pool.dma_start(m_out[bass.ds(layer, 1)].rearrange("l p n -> (l p) n"), row(M_)).then_inc(mix_stored, 16)
                    for h in range(MH):
                        pool.wait_ge(head_fin, h + 1)
                        pool.dma_start(sC_out[bass.ds(layer, 1), h].rearrange("l p n -> (l p) n"),
                                       Cst[:, h % 2, :, :].rearrange("p b e -> p (b e)")).then_inc(cstored, 16)
                        if h + 2 < MH:
                            pool.wait_ge(cstored, 16 * (h + 1))
                            load_c0(h + 2)
                    pool.wait_ge(cstored, 16 * MH)
                    pool.wait_ge(pc_ready, 1)
                    pool.wait_ge(pn_ready, 1)
                    pool.dma_start(pC_out[bass.ds(layer, 1)].rearrange("l p n -> (l p) n"),
                                   pCs.rearrange("p h e -> p (h e)")).then_inc(mix_stored, 16)
                    pool.dma_start(pn_out[bass.ds(layer, 1)].rearrange("l p n -> (l p) n"),
                                   nstat[:, :, :].rearrange("p h b -> p (h b)")).then_inc(stored, 16)
                    pool.wait_ge(mix_stored, 32)
                    pool.wait_ge(ha_ready, MH)
                    for n in range(DECB * NPG):
                        b, j = divmod(n, NPG)
                        page = pool.value_load(table[0:1, n:n + 1], min_val=0, max_val=pages_in.shape[1] - 1)
                        src = pages_in[bass.ds(layer, 1), bass.ds(page, 1)].rearrange("l a p n -> (l a p) n")
                        at = SEQ + b * PAST + j * PAGE
                        pool.dma_start(raw[:, :, at:at + PAGE],
                                       src[:, 0:2 * PAGE].rearrange("p (v s) -> p v s", v=2)).then_inc(raw_landed, 16)
                        pool.dma_start(selp[:, b, j, :, :],
                                       src[:, 2 * PAGE:4 * PAGE].rearrange("p (v s) -> p v s", v=2)).then_inc(sel_landed, 16)
                    pool.memset(qb[:, :, :, :], 0.0).then_inc(pool_step, 1)
                    pool.wait_ge(w1_used, 8)
                    pool.wait_ge(rope_ready, 6)
                    pool.dma_start(fm_out[bass.ds(layer, 1)].rearrange("l p v n -> (l p) v n")[:, 0:2, 0:SEQ],
                                   raw[:, :, 0:SEQ]).then_inc(raw_stored, 16)
                    pool.dma_start(fm_out[bass.ds(layer, 1)].rearrange("l p v n -> (l p) v n")[:, 0:2, SEQ:N],
                                   raw[:, :, RAW:RAW + NS]).then_inc(raw_stored, 16)
                    pool.wait_ge(raw_stored, 32)
                    pool.dma_start(winp, win_in[bass.ds(layer, 1)].rearrange("l p (b v j s) -> (l p) b v j s", b=DECB, v=2, j=NPG)).then_inc(win_landed, 16)
                    pool.dma_start(fm_out[bass.ds(layer, 1)].rearrange("l p v n -> (l p) v n")[:, 2:4, :], kT).then_inc(nsa_stored, 16)
                    tmo = tm_out[bass.ds(layer, 1)].rearrange("l p i n -> (l p) i n")
                    pool.dma_start(tmo[:, 0:TT, :], vkv[:, 0:TT, :]).then_inc(nsa_stored, 16)
                    pool.dma_start(tmo[0:NS, TT, :], vkv[0:NS, TT, :]).then_inc(nsa_stored, 16)
                    pool.wait_ge(stored, 32)
                    pool.wait_ge(nsa_stored, 48)
                    pool.wait_ge(win_landed, 16)
                    pool.wait_ge(raw_landed, 16 * DECB * NPG)
                    pool.wait_ge(sel_landed, 16 * DECB * NPG)
                    pool.dma_reset()

                @block.tensor
                def _(pe):
                    def landed(key):
                        n = UNIT[key]
                        pe.wait_ge(unit_landed[n % RING], 16 * (n // RING + 1))
                        return ring[:, n % RING, :]

                    def begin(key):
                        q = GROUP[key]
                        if q >= 4:
                            pe.wait_ge(pair_free[q % 4], q // 4)
                        return pair(q)

                    def drained(q):
                        for s in range(4):
                            pe.wait_ge(pair_free[s], (q - s + 3) // 4)

                    def product(key, unit_key, src, kcs, first=0, ready=None):
                        w = landed(unit_key).rearrange("p (k m) -> p k m", m=P)
                        out = begin(key)
                        for k in range(kcs):
                            if ready is not None:
                                pe.wait_ge(ready[0], ready[1] + k + 1)
                            for a in range(2):
                                mm = pe.matmul(out[:, a, :], w[:, first + k, :], src[:, k, a * NHALF:(a + 1) * NHALF],
                                               start=(k == 0), stop=(k == kcs - 1))
                        return mm

                    def norm_sum(key, base):
                        out = begin(key)
                        for k in range(KC):
                            pe.wait_ge(sq_ready, base + k + 1)
                            for a in range(2):
                                mm = pe.matmul(out[:, a, :], ones[:, :], sq[:, k % 2, a * NHALF:(a + 1) * NHALF],
                                               start=(k == 0), stop=(k == KC - 1))
                            if k < KC - 1:
                                mm.then_inc(sq_used, 1)
                        mm.then_inc(pair_done, 1)

                    norm_sum(("n1", 0), 0)
                    for i in range(TT + 1):
                        rows = P if i < TT else NS
                        q = GROUP[("tm", i)]
                        begin(("tm", i))
                        s = 2 * (q % 4)
                        for k in range(KC):
                            if i == 0:
                                pe.wait_ge(h_ready, k + 1)
                            w = landed(("tm", k))
                            x = hT[:, k, i * P:i * P + rows]
                            pe.matmul(ps[0:rows, s, :], x, w[:, 0:512], start=(k == 0), stop=(k == KC - 1))
                            mm = pe.matmul(ps[0:rows, s + 1, 0:280], x, w[:, 512:TMC], start=(k == 0), stop=(k == KC - 1))
                            if i == TT and k < KC - 1:
                                mm.then_inc(tm_used, 1)
                        mm.then_inc(pair_done, 1)

                    def fm(kind, m, src=hT, kcs=KC):
                        product((kind, m), (kind, m), src, kcs).then_inc(pair_done, 1)

                    for m in range(4):
                        fm("u", m)
                    w = landed(("if", 0)).rearrange("p (k m) -> p k m", k=KC)
                    out = begin(("if", 0))
                    for k in range(KC):
                        for a in range(2):
                            mm = pe.matmul(out[0:64, a, :], w[:, k, 0:64], hT[:, k, a * NHALF:(a + 1) * NHALF],
                                           start=(k == 0), stop=(k == KC - 1))
                    mm.then_inc(pair_done, 1)
                    for m in range(4):
                        fm("o", m)
                    pe.wait_ge(small_landed, 16)
                    for h in range(MH):
                        for name in ("mq", "mk"):
                            w = sml("w" + name, "p (h m) -> p h m", h=MH)[:, h, :]
                            out = begin((name, h))
                            pe.wait_ge(c_ready, h + 1)
                            for a in range(2):
                                mm = pe.matmul(out[:, a, :], w, cT[:, h, a * NHALF:(a + 1) * NHALF], start=True, stop=True)
                            mm.then_inc(pair_done, 1)
                    begin(("aw", 0))
                    s = 2 * (GROUP[("aw", 0)] % 4)
                    aw = ps[:, s, 0:(TT + 1) * 2 * MH].rearrange("p (i a h) -> p i a h", i=TT + 1, a=2)
                    pe.wait_ge(wexp_ready, 1)
                    for i in range(TT + 1):
                        rows = P if i < TT else NS
                        for a, r in enumerate((A_, W_)):
                            mm = pe.transpose(aw[0:rows, i, a, :], row(r)[:, i * P:i * P + rows], ident[0:MH, 0:MH])
                    mm.then_inc(pair_done, 1)
                    for i in range(TT + 1):
                        rows = P if i < TT else NS
                        begin(("kw", i))
                        s = 2 * (GROUP[("kw", i)] % 4)
                        wk = sml("wmk", "p (h m) -> p h m", h=MH)
                        for h in range(MH):
                            mm = pe.matmul(ps[0:rows, s, h * MD:(h + 1) * MD], cT[:, h, i * P:i * P + rows], wk[:, h, :],
                                           start=True, stop=True)
                        mm.then_inc(pair_done, 1)
                    drained(CORE_AT)

                    def spread(h, which):
                        x = 2 * h + which
                        if x >= 1:
                            pe.wait_ge(bc_ready, x)
                        r = row(G_) if which == 0 else row(EN_)
                        for a in range(2):
                            mm = pe.matmul(ps[:, 6 + a, 0:NHALF], sel4[0:MH, h, :], r[:, a * NHALF:(a + 1) * NHALF],
                                           start=True, stop=True)
                        if which == 1:
                            mm = pe.matmul(ps[:, 6, NHALF:NHALF + NS], sel4[0:MH, h, :], introw, start=True, stop=True)
                        mm.then_inc(bc_done, 1)

                    def scores(k):
                        h, j = divmod(k, TT + 1)
                        if k >= 2:
                            pe.wait_ge(st_ready, k - 1)
                        if j < TT:
                            mm = pe.matmul(ps[:, k % 2, 0:SEQ - j * P], km[:, h, j * P:(j + 1) * P], qm[:, h, j * P:SEQ],
                                           start=True, stop=True)
                        else:
                            mm = pe.matmul(ps[0:NS, k % 2, 0:NS], km[:, h, SEQ:N], qm[:, h, SEQ:N], start=True, stop=True)
                        mm.then_inc(ms_done, 1)

                    def numden(k):
                        h, j = divmod(k, TT + 1)
                        if j == 0 and h >= 1:
                            pe.wait_ge(num_read, h)
                        pe.wait_ge(st_ready, k + 1)
                        if j < TT:
                            s = St[:, k % 2, 0:SEQ - j * P]
                            pe.matmul(ps[:, 2, j * P:SEQ], vtm[:, j, h * MD:(h + 1) * MD], s, start=(j == 0), stop=(j == TT - 1))
                            mm = pe.matmul(ps[:, 3, j * P:SEQ], ones[:, :], s, start=(j == 0), stop=(j == TT - 1))
                        else:
                            s = St[0:NS, k % 2, 0:NS]
                            pe.matmul(ps[:, 4, 0:NS], vtm[0:NS, TT, h * MD:(h + 1) * MD], s, start=True, stop=False)
                            pe.wait_ge(qi_ready, h + 1)
                            pe.wait_ge(c0_landed[h % 2], 16 * (h // 2 + 1))
                            for b in range(DECB):
                                pe.matmul(ps[:, 4, b * DECT:(b + 1) * DECT], Cst[:, h % 2, b, :], qi[:, 0, b * DECT:(b + 1) * DECT],
                                          start=False, stop=(b == DECB - 1))
                            pe.matmul(ps[:, 4, NS:2 * NS], ones[0:NS, :], s, start=True, stop=False)
                            mm = pe.matmul(ps[:, 4, NS:2 * NS], ones[:, :], qi[:, 1, :], start=False, stop=True)
                        mm.then_inc(nd_done, 1)

                    def new_state(h):
                        pe.wait_ge(vb_ready, h + 1)
                        pe.wait_ge(bc_ready, min(2 * h + 4, 2 * MH))
                        k = kw[0:NS, TT, h * MD:(h + 1) * MD]
                        for a in range(2):
                            pe.matmul(ps[:, 6 + a, :], k, vb[0:NS, 4 * a:4 * a + 4, :], start=True, stop=True)
                        mm = pe.matmul(ps[:, 5, 0:DECB], k, con("blk")[0:NS, :], start=True, stop=True)
                        mm.then_inc(cs_done, 1)

                    nk = MH * (TT + 1)
                    spread(0, 0)
                    spread(0, 1)
                    scores(0)
                    for k in range(nk):
                        h, j = divmod(k, TT + 1)
                        if k + 1 < nk:
                            scores(k + 1)
                        if j == 0 and h + 1 < MH:
                            if h >= 1:
                                pe.wait_ge(head_fin, h)
                            spread(h + 1, 0)
                            spread(h + 1, 1)
                        numden(k)
                        if j == TT:
                            new_state(h)
                    pe.wait_ge(st_ready, nk)
                    for h in range(MH):
                        for what in range(2):
                            for i in range(TT):
                                k = kw[:, i, h * MD:(h + 1) * MD]
                                if what == 0:
                                    mm = pe.matmul(ps[:, 0, h * MD:(h + 1) * MD], k, vtm[:, i, h * MD:(h + 1) * MD],
                                                   start=(i == 0), stop=(i == TT - 1))
                                else:
                                    mm = pe.matmul(ps[:, 1, h:h + 1], k, ones[:, 0:1], start=(i == 0), stop=(i == TT - 1))
                    mm.then_inc(pc_done, 1)
                    pe.wait_ge(head_fin, MH)
                    pe.wait_ge(pc_ready, 1)
                    pe.wait_ge(pn_ready, 1)
                    for h in range(MH):
                        q = GROUP[("mn", h)]
                        begin(("mn", h))
                        pe.wait_ge(msq_ready, h + 1)
                        for a in range(2):
                            mm = pe.matmul(pair(q)[:, a, :], ones[:, :], sq[:, h % 2, a * NHALF:(a + 1) * NHALF], start=True, stop=True)
                        mm.then_inc(pair_done, 1)
                    for m in range(4):
                        fm("q", m)
                    for m in range(4):
                        fm("k", m)
                    for n in range(6):
                        out = begin(("rope", n))
                        src = qT[:, n, :] if n < 4 else kT[:, n - 4, :]
                        read_out(pe, ("q", n) if n < 4 else ("k", n - 2))
                        for a in range(2):
                            mm = pe.matmul(out[:, a, :], rot, src[:, a * NHALF:(a + 1) * NHALF], start=True, stop=True)
                        mm.then_inc(pair_done, 1)
                    drained(ATTN_AT)
                    pe.wait_ge(raw_landed, 16 * DECB * NPG)
                    pes = sml("pe", "p (v l) -> p v l", v=2)
                    for v in range(2):
                        for u in range(4):
                            w = landed(("w1", 4 * v + u)).rearrange("p (l e) -> p l e", e=HID)
                            for l8 in range(8):
                                l = 8 * u + l8
                                for g in range(NKV):
                                    x = raw[g * HD:(g + 1) * HD, v, l:l + STRIDE * (NBLK - 1) + 1:STRIDE]
                                    pe.matmul(ps[:, 3 * v + g, 0:NBLK], w[g * HD:(g + 1) * HD, l8, :], x, start=(l == 0), stop=(l == CLEN - 1))
                                mm = pe.matmul(ps[:, 3 * v + 2, 0:1], w[0:HD, l8, :], pes[0:HD, v, l:l + 1], start=(l == 0), stop=(l == CLEN - 1))
                            mm.then_inc(w1_used, 1)
                    w2 = sml("w2", "p (v f) -> p v f", v=2)
                    pe.wait_ge(hid_ready, 1)
                    for g in range(NKV):
                        pe.matmul(ps[g * HD:(g + 1) * HD, 6, 0:NBLK], w2[:, 0, :], hid[:, 0, g, :], start=True, stop=True)
                    pe.wait_ge(hid_ready, 2)
                    for g in range(NKV):
                        pe.matmul(ps[0:NCP, 7, g * HD:(g + 1) * HD], hid[:, 1, g, 0:NCP], w2[:, 1, :], start=True, stop=True)
                        mm = pe.matmul(ps[:, 7, P + g * HD:P + (g + 1) * HD], hid[:, 1, g, PBLK:NBLK], w2[:, 1, :], start=True, stop=True)
                    mm.then_inc(cmp_done, 1)
                    pe.wait_ge(cmp_ready, 1)

                    def att_scores(k):
                        i, g, rp, br = STEPS[k]
                        if k >= 2:
                            pe.wait_ge(exp_done, k - 1)
                        src = qT if br == 0 else qrT
                        keys = kcT[g * HD:(g + 1) * HD, 0:NCP] if br == 0 else kT[g * HD:(g + 1) * HD, br - 1, 0:(i + 1) * P]
                        width = NCP if br == 0 else (i + 1) * P
                        for r in range(2):
                            mm = pe.matmul(ps[:, 2 * (k % 2) + r, 0:width], src[g * HD:(g + 1) * HD, 2 * rp + r, i * P:(i + 1) * P], keys,
                                           start=True, stop=True)
                        mm.then_inc(s_done, 1)

                    def att_turn(k):
                        i, g, rp, br = STEPS[k]
                        pe.wait_ge(d_ready, k + 1)
                        for x, j0, nj in chunks_of(k):
                            if x >= 2:
                                pe.wait_ge(t_free[x % 2], x // 2)
                            rows = NCP if br == 0 else P
                            for j in range(j0, j0 + nj):
                                for r in range(2):
                                    at = ((j - j0) * 2 + r) * P
                                    mm = pe.matmul(ps[0:rows, 4 + x % 2, at:at + P], Pt[:, k % 2, r, j * P:j * P + rows], Dg[:, k % 2, r, :],
                                                   start=True, stop=True)
                            mm.then_inc(t_done, 1)

                    def att_out(k):
                        i, g, rp, br = STEPS[k]
                        w = k // 3
                        if br == 0 and w >= 2:
                            pe.wait_ge(hb_ready, w - 1)
                        out = ps[g * HD:(g + 1) * HD, 6 + w % 2, 0:2 * P]
                        for x, j0, nj in chunks_of(k):
                            pe.wait_ge(t_free[x % 2], x // 2 + 1)
                            for j in range(j0, j0 + nj):
                                c = (j - j0) * 2 * P
                                if br == 0:
                                    mm = pe.matmul(out, vcp[0:NCP, g * HD:(g + 1) * HD], PT[0:NCP, x % 2, 0:2 * P], start=True, stop=False)
                                else:
                                    mm = pe.matmul(out, vkv[:, j, (br - 1) * P + g * HD:(br - 1) * P + (g + 1) * HD], PT[:, x % 2, c:c + 2 * P],
                                                   start=False, stop=(br == 2 and j == i))
                            mm.then_inc(o_done, 1)

                    att_scores(0)
                    pe.wait_ge(rope_ready, 6)
                    for k in range(NSTEP):
                        if k + 1 < NSTEP:
                            att_scores(k + 1)
                        att_turn(k)
                        att_out(k)
                    pe.wait_ge(hb_ready, NSTEP // 3)
                    pe.wait_ge(exp_done, NSTEP)
                    for hb in range(2):
                        mm = pe.matmul(ps[:, 3, hb * 24:(hb + 1) * 24], tsel[0:NS, hb, :], gate[0:NS, TT, :], start=True, stop=True)
                    mm.then_inc(gs_done, 1)
                    pe.wait_ge(qb_ready, 1)
                    pe.wait_ge(sel_landed, 16 * DECB * NPG)

                    def samp_scores(m):
                        hb, br = SSTEPS[m]
                        if m >= 2:
                            pe.wait_ge(exp_done, NSTEP + m - 1)
                        if br == 2:
                            pe.wait_ge(win_landed, 16)
                        for b4 in range(4):
                            b = 4 * hb + b4
                            o = ps[32 * b4:32 * b4 + 32, m % 2, :]
                            if br == 0:
                                mm = pe.matmul(o[:, 0:P], qb[:, 0, b, :], kcT[:, PBLK:NBLK], start=True, stop=True)
                            else:
                                past = selp[:, b, :, 0, :] if br == 1 else winp[:, b, 0, :, :]
                                pe.matmul(o[:, 0:PAST], qb[:, 1, b, :], past, start=True, stop=True)
                                mm = pe.matmul(o[:, PAST:PAST + NS], qb[:, 1, b, :], kT[:, br - 1, SEQ:N], start=True, stop=True)
                        mm.then_inc(s_done, 1)

                    def samp_turn(m):
                        hb, br = SSTEPS[m]
                        x = NPC + m
                        pe.wait_ge(d_ready, NSTEP + m + 1)
                        pe.wait_ge(t_free[x % 2], x // 2)
                        for j in range(1 if br == 0 else 3):
                            rows = NS if j == 2 else P
                            mm = pe.matmul(ps[0:rows, 4 + x % 2, j * P:(j + 1) * P], Pt[:, m % 2, 0, j * P:j * P + rows], Dg[:, m % 2, 0, :],
                                           start=True, stop=True)
                        mm.then_inc(t_done, 1)

                    def samp_out(m):
                        hb, br = SSTEPS[m]
                        x = NPC + m
                        pe.wait_ge(t_free[x % 2], x // 2 + 1)
                        bank = 6 + hb
                        if br == 0:
                            mm = pe.matmul(ps[:, bank, 0:P], vcs, PT[:, x % 2, 0:P], start=True, stop=False)
                        else:
                            pe.matmul(ps[:, bank, 0:P], vkv[0:NS, TT, (br - 1) * P:br * P], PT[0:NS, x % 2, 2 * P:3 * P], start=False, stop=False)
                            for b4 in range(4):
                                b = 4 * hb + b4
                                for j in range(NPG):
                                    v = selp[:, b, j, 1, :] if br == 1 else winp[:, b, 1, j, :]
                                    mm = pe.matmul(ps[:, bank, 32 * b4:32 * b4 + 32], v, PT[:, x % 2, j * P + 32 * b4:j * P + 32 * b4 + 32],
                                                   start=False, stop=(br == 2 and j == NPG - 1 and b4 == 3))
                        mm.then_inc(o_done, 1)

                    samp_scores(0)
                    for m in range(6):
                        if m + 1 < 6:
                            samp_scores(m + 1)
                        samp_turn(m)
                        samp_out(m)
                    pe.wait_ge(exp_done, NSTEP + 6)
                    pe.wait_ge(hb_ready, NSTEP // 3 + 2)
                    for m in range(KC):
                        product(("ga", m), ("ga", m), hT, KC).then_inc(pair_done, 1)
                        product(("gb", m), ("gb", m), hT, KC).then_inc(pair_done, 1)
                        product(("a", m), ("ab", m), haT, 4).then_inc(pair_done, 1)
                        product(("b", m), ("ab", m), hbT, 4, first=4).then_inc(pair_done, 1)
                    pe.wait_ge(merged_ready, KC)
                    for m in range(KC):
                        product(("out", m), ("out", m), merged, KC).then_inc(pair_done, 1)
                    norm_sum(("n2", 0), KC)
                    pe.wait_ge(h_ready, 2 * KC)
                    for m in range(NFF):
                        fm("fg", m)
                        fm("fu", m)
                    for m in range(KC):
                        out = begin(("dn", m))
                        for k in range(NFF):
                            if m == 0:
                                read_out(pe, ("fu", k))
                            w = landed(("dn", 3 * m + k // 8)).rearrange("p (k m) -> p k m", m=P)
                            for a in range(2):
                                mm = pe.matmul(out[:, a, :], w[:, k % 8, :], act_[:, k, a * NHALF:(a + 1) * NHALF],
                                               start=(k == 0), stop=(k == NFF - 1))
                            if k % 8 == 7:
                                mm.then_inc(dn_used, 1)
                        mm.then_inc(pair_done, 1)

                @block.scalar
                def _(act):
                    steps = [0]

                    def link(ins):
                        steps[0] += 1
                        ins.then_inc(act_step, 1)
                        act.wait_ge(act_step, steps[0])

                    def done(key):
                        q = GROUP[key]
                        act.wait_ge(pair_done, q + 1)
                        return pair(q), pair_free[q % 4]

                    def squares():
                        for k in range(KC):
                            if k >= 2:
                                act.wait_ge(sq_used, k - 1)
                            act.activation(sq[:, k % 2, :], xT[:, k, :], ACT.Square).then_inc(sq_ready, 1)

                    def root(key):
                        out, free = done(key)
                        act.activation(halves(rstd[:, :]), out, ACT.Sqrt, bias=eps[:, :], scale=1.0 / D).then_inc(free, 1)

                    squares()
                    root(("n1", 0))
                    for i in range(TT + 1):
                        rows = P if i < TT else NS
                        done(("tm", i))
                        q = GROUP[("tm", i)]
                        s = 2 * (q % 4)
                        act.activation(gate[0:rows, i, :], ps[0:rows, s + 1, 2 * P:2 * P + 24], ACT.Sigmoid)
                        act.copy(vkv[0:rows, i, :], ps[0:rows, s + 1, 0:2 * P])
                        act.copy(vtm[0:rows, i, :], ps[0:rows, s, :]).then_inc(pair_free[q % 4], 1)
                    for m in range(4):
                        out, free = done(("u", m))
                        act.copy(upad[:, m, 3:3 + NHALF], out[:, 0, :])
                        act.copy(upad[:, m, 3 + NHALF:3 + SEQ], out[:, 1, 0:SEQ - NHALF])
                        us = upad[:, m, 3 + SEQ:UW].rearrange("p (b t) -> p b t", b=DECB)
                        act.copy(us[:, :, 3:7], out[:, 1, SEQ - NHALF:NHALF].rearrange("p (b t) -> p b t", b=DECB)).then_inc(free, 1)
                    out, free = done(("if", 0))
                    act.wait_ge(small_landed, 16)
                    act.activation(halves(row(I_)), out[0:MH], ACT.Identity, bias=sml("bi")[0:MH, :])
                    act.copy(halves(row(A_)), out[32:32 + MH]).then_inc(free, 1)
                    read_out(act, ("if", 0))
                    link(act.activation(row(Z_), row(A_), ACT.Identity, bias=sml("bf")[0:MH, :]))
                    link(act.activation(row(L_), row(Z_), ACT.Abs))
                    link(act.activation(row(A_), row(L_), ACT.Exp, scale=-1.0))
                    act.activation(row(L_), row(A_), ACT.Ln, bias=ones[0:MH, 0:1]).then_inc(ln_ready, 1)
                    for m in range(4):
                        act.wait_ge(conv_ready, m + 1)
                        act.activation(cT[:, m, :], ctmp[:, m % 2, :], ACT.Silu).then_inc(c_ready, 1)
                    for m in range(4):
                        out, free = done(("o", m))
                        act.activation(halves(haT[:, m, :]), out, ACT.Sigmoid).then_inc(free, 1)
                    act.wait_ge(rows_ready, 1)
                    act.activation(row(W_)[:, 0:SEQ], row(A_)[:, 0:SEQ], ACT.Exp, bias=row(G_)[:, SEQ - 1:SEQ])
                    act.activation(row(W_)[:, SEQ:N], tmprow, ACT.Exp)
                    act.activation(row(EN_), row(M_), ACT.Exp, scale=-1.0)
                    act.activation(introw, introw, ACT.Exp).then_inc(wexp_ready, 1)
                    for h in range(MH):
                        for name, dst, scale in (("mq", qm, 1.0), ("mk", km, MD ** -0.5)):
                            out, free = done((name, h))
                            act.activation(halves(dst[:, h, :]), out, ACT.Copy, scale=scale).then_inc(free, 1)
                    act.wait_ge(pair_done, CORE_AT)
                    act.wait_ge(u_stored, 16)
                    read_out(act, ("aw", 0))

                    def spread(h):
                        if h >= 2:
                            act.wait_ge(head_fin, h - 1)
                        act.wait_ge(bc_done, 2 * h + 1)
                        act.copy(halves(gbc[:, h % 2, :]), ps[:, 6:8, 0:NHALF]).then_inc(bc_ready, 1)
                        act.wait_ge(bc_done, 2 * h + 2)
                        act.copy(inter[:, h % 2, :], ps[:, 6, NHALF:NHALF + NS])
                        act.copy(halves(enm[:, h % 2, :]), ps[:, 6:8, 0:NHALF]).then_inc(bc_ready, 1)

                    spread(0)
                    for k in range(MH * (TT + 1)):
                        h, j = divmod(k, TT + 1)
                        if j == 1 and h + 1 < MH:
                            spread(h + 1)
                        if k >= 2:
                            act.wait_ge(st_ready, k - 1)
                        act.wait_ge(gm_ready, k + 1)
                        if j < TT:
                            if j < TT - 1:
                                act.wait_ge(bc_ready, 2 * h + 1)
                                act.activation(Et[:, k % 2, P:SEQ - j * P], gbc[:, h % 2, (j + 1) * P:SEQ], ACT.Exp, bias=awt[:, j, 0, h:h + 1])
                            act.activation(Et[:, k % 2, 0:P], gmask, ACT.Exp, bias=awt[:, j, 0, h:h + 1]).then_inc(e_ready, 1)
                        else:
                            act.activation(Et[0:NS, k % 2, 0:NS], gmask[0:NS, 0:NS], ACT.Exp, bias=awt[0:NS, j, 0, h:h + 1]).then_inc(e_ready, 1)
                    act.wait_ge(pc_done, 1)
                    act.copy(pCs, ps[:, 0, :].rearrange("p (h e) -> p h e", h=MH)).then_inc(pc_ready, 1)
                    for h in range(MH):
                        if h >= 2:
                            act.wait_ge(pair_done, GROUP[("mn", h - 2)] + 1)
                        act.wait_ge(num_read, h + 1)
                        act.activation(sq[:, h % 2, :], qm[:, h, :], ACT.Square).then_inc(msq_ready, 1)
                    for h in range(MH):
                        out, free = done(("mn", h))
                        if h >= 1:
                            act.wait_ge(ha_ready, h)
                        act.activation(halves(rstd[:, :]), out, ACT.Sqrt, bias=eps[:, :], scale=1.0 / MD).then_inc(free, 1)
                    act.wait_ge(ha_ready, MH)
                    act.wait_ge(mix_stored, 32)
                    act.wait_ge(cstored, 16 * MH)
                    for m in range(4):
                        out, free = done(("q", m))
                        act.activation(halves(qT[:, m, :]), out, ACT.Copy, scale=HD ** -0.5).then_inc(free, 1)
                    for m in range(4):
                        out, free = done(("k", m))
                        if m < 2:
                            act.copy(raw[:, m, 0:NHALF], out[:, 0, :])
                            act.copy(raw[:, m, NHALF:SEQ], out[:, 1, 0:SEQ - NHALF])
                            act.copy(raw[:, m, RAW:RAW + NS], out[:, 1, SEQ - NHALF:NHALF]).then_inc(free, 1)
                        else:
                            act.copy(halves(kT[:, m - 2, :]), out).then_inc(free, 1)
                    for v in range(2):
                        act.wait_ge(w1_used, 4 * (v + 1))
                        link(act.copy(hbias[:, v:v + 1], ps[:, 3 * v + 2, 0:1]))
                        for g in range(NKV):
                            ins = act.activation(hid[:, v, g, :], ps[:, 3 * v + g, 0:NBLK], ACT.Gelu_apprx_tanh, bias=hbias[:, v:v + 1])
                        ins.then_inc(hid_ready, 1)
                    act.wait_ge(cmp_done, 1)
                    act.copy(kcT, ps[:, 6, 0:NBLK])
                    act.copy(vcp[0:NCP, :], ps[0:NCP, 7, 0:P])
                    act.copy(vcs, ps[:, 7, P:2 * P]).then_inc(cmp_ready, 1)

                    def att_exp(k):
                        i, g, rp, br = STEPS[k]
                        act.wait_ge(max_ready, k + 1)
                        if k >= 2:
                            act.wait_ge(t_done, chunks_of(k - 2)[-1][0] + 1)
                        width = NCP if br == 0 else (i + 1) * P
                        for r in range(2):
                            ins = act.activation(Pt[:, k % 2, r, 0:width], ps[:, 2 * (k % 2) + r, 0:width], ACT.Exp,
                                                 bias=stat[:, k % 2, r:r + 1],
                                                 accum_out=None if br == 0 else stat[:, 2 + k % 2, r:r + 1])
                        ins.then_inc(exp_done, 1)

                    def evac(x, rows, cols):
                        act.wait_ge(t_done, x + 1)
                        if x >= 2:
                            act.wait_ge(o_done, x - 1)
                        act.copy(PT[0:rows, x % 2, 0:cols], ps[0:rows, 4 + x % 2, 0:cols]).then_inc(t_free[x % 2], 1)

                    att_exp(0)
                    for k in range(NSTEP):
                        i, g, rp, br = STEPS[k]
                        if k + 1 < NSTEP:
                            att_exp(k + 1)
                        for x, j0, nj in chunks_of(k):
                            if evac_on_act(x):
                                evac(x, P, nj * 2 * P)
                        if br == 2:
                            act.wait_ge(o_done, chunks_of(k)[-1][0] + 1)
                            act.copy(hbT[g * HD:(g + 1) * HD, 2 * rp:2 * rp + 2, i * P:(i + 1) * P],
                                     ps[g * HD:(g + 1) * HD, 6 + (k // 3) % 2, 0:2 * P].rearrange("p (r t) -> p r t", r=2)).then_inc(hb_ready, 1)

                    def samp_exp(m):
                        hb, br = SSTEPS[m]
                        act.wait_ge(max_ready, NSTEP + m + 1)
                        if m >= 2:
                            act.wait_ge(t_done, NPC + m - 1)
                        else:
                            act.wait_ge(t_done, NPC)
                        width = P if br == 0 else PAST + NS
                        act.activation(Pt[:, m % 2, 0, 0:width], ps[:, m % 2, 0:width], ACT.Exp, bias=stat[:, m % 2, 0:1],
                                       accum_out=stat[:, 2 + m % 2, 0:1]).then_inc(exp_done, 1)

                    samp_exp(0)
                    for m in range(6):
                        hb, br = SSTEPS[m]
                        if m + 1 < 6:
                            samp_exp(m + 1)
                        x = NPC + m
                        if br == 0:
                            evac(x, P, P)
                        else:
                            act.wait_ge(t_done, x + 1)
                            act.wait_ge(o_done, x - 1)
                            act.copy(PT[:, x % 2, 0:2 * P], ps[:, 4 + x % 2, 0:2 * P])
                            act.copy(PT[0:NS, x % 2, 2 * P:3 * P], ps[0:NS, 4 + x % 2, 2 * P:3 * P]).then_inc(t_free[x % 2], 1)
                        if br == 2:
                            act.wait_ge(o_done, x + 1)
                            for g in range(NKV):
                                o = ps[g * HD:(g + 1) * HD, 6 + hb, 0:P].rearrange("p (b g r t) -> p b g r t", b=4, g=NKV, r=R)
                                d = hbT[g * HD:(g + 1) * HD, :, SEQ + 16 * hb:SEQ + 16 * hb + 16].rearrange("p r (b t) -> p b r t", b=4)
                                for b4 in range(4):
                                    ins = act.copy(d[:, b4], o[:, b4, g])
                            ins.then_inc(hb_ready, 1)
                    for m in range(KC):
                        for n, name in enumerate(("ga", "gb")):
                            out, free = done((name, m))
                            if m >= 1:
                                read_out(act, (("a", "b")[n], m - 1))
                            act.activation(halves(sg[:, n, :]), out, ACT.Sigmoid).then_inc(free, 1)
                    for k in range(KC):
                        read_out(act, ("out", k))
                        if k >= 2:
                            act.wait_ge(sq_used, KC - 1 + k - 1)
                        act.activation(sq[:, k % 2, :], xT[:, k, :], ACT.Square).then_inc(sq_ready, 1)
                    root(("n2", 0))
                    for m in range(NFF):
                        out, free = done(("fg", m))
                        if m >= 2:
                            read_out(act, ("fu", m - 2))
                        act.activation(halves(sg[:, m % 2, :]), out, ACT.Silu).then_inc(free, 1)

                @block.vector
                def _(dve):
                    steps = [0]

                    def link(ins):
                        steps[0] += 1
                        ins.then_inc(dve_step, 1)
                        dve.wait_ge(dve_step, steps[0])

                    def done(key):
                        q = GROUP[key]
                        dve.wait_ge(pair_done, q + 1)
                        return pair(q), pair_free[q % 4]

                    def normed(g, base):
                        link(dve.reciprocal(rstd[:, :], rstd[:, :]))
                        for k in range(KC):
                            dve.scalar_tensor_tensor(out=hT[:, k, :], in0=xT[:, k, :], scalar=g[:, k:k + 1], in1=rstd[:, :],
                                                     op0=ALU.mult, op1=ALU.mult).then_inc(h_ready, 1)

                    dve.wait_ge(small_landed, 16)
                    read_out(dve, ("n1", 0))
                    normed(sml("n1g"), 0)
                    dve.wait_ge(history_ready, 1)
                    cw = sml("cw", "p (c j) -> p c j", c=4)
                    for m in range(4):
                        read_out(dve, ("u", m))
                        if m >= 2:
                            dve.wait_ge(c_ready, m - 1)
                        us = upad[:, m, 3 + SEQ:UW].rearrange("p (b t) -> p b t", b=DECB)
                        up, dp = upad[:, m, 0:3 + SEQ], ctmp[:, m % 2, 0:SEQ]
                        dsm = ctmp[:, m % 2, SEQ:N].rearrange("p (b t) -> p b t", b=DECB)
                        dve.tensor_scalar(dp, up[:, 0:SEQ], cw[:, m, 0:1], sml("cb")[:, m:m + 1], ALU.mult, ALU.add)
                        link(dve.tensor_scalar(dsm, us[:, :, 0:DECT], cw[:, m, 0:1], sml("cb")[:, m:m + 1], ALU.mult, ALU.add))
                        for j in range(1, CONV):
                            dve.scalar_tensor_tensor(out=dp, in0=up[:, j:j + SEQ], scalar=cw[:, m, j:j + 1], in1=dp, op0=ALU.mult, op1=ALU.add)
                            ins = dve.scalar_tensor_tensor(out=dsm, in0=us[:, :, j:j + DECT], scalar=cw[:, m, j:j + 1], in1=dsm,
                                                           op0=ALU.mult, op1=ALU.add)
                            if j < CONV - 1:
                                link(ins)
                            else:
                                ins.then_inc(conv_ready, 1)
                    dve.wait_ge(ln_ready, 1)
                    lf = row(Z_)
                    link(dve.scalar_tensor_tensor(out=lf, in0=row(Z_), scalar=0.0, in1=row(L_), op0=ALU.min, op1=ALU.subtract))
                    dve.memset(row(A_), 1.0)
                    m0 = sml("m0")[0:MH, :]
                    fs, ms, ls, is_ = (per_seq(r[:, SEQ:N]) for r in (row(F_), row(M_), lf, row(I_)))
                    link(dve.tensor_tensor_scan(out=row(M_)[:, 0:SEQ], data0=lf[:, 0:SEQ], data1=row(I_)[:, 0:SEQ], initial=0.0,
                                                op0=ALU.add, op1=ALU.max))
                    dve.tensor_tensor_scan(out=row(F_)[:, 0:SEQ], data0=row(A_)[:, 0:SEQ], data1=lf[:, 0:SEQ], initial=0.0,
                                           op0=ALU.mult, op1=ALU.add)
                    for t in range(DECT):
                        link(dve.tensor_tensor(ms[:, :, t], m0 if t == 0 else ms[:, :, t - 1], ls[:, :, t], ALU.add))
                        dve.tensor_tensor(ms[:, :, t], ms[:, :, t], is_[:, :, t], ALU.max)
                        link(dve.tensor_copy(fs[:, :, t], ls[:, :, t]) if t == 0 else
                             dve.tensor_tensor(fs[:, :, t], fs[:, :, t - 1], ls[:, :, t], ALU.add))
                    dve.tensor_tensor(row(A_), row(I_), row(F_), ALU.subtract)
                    link(dve.tensor_tensor(row(G_), row(F_), row(M_), ALU.subtract))
                    gs = per_seq(row(G_)[:, SEQ:N])
                    dve.tensor_tensor(per_seq(introw), gs, bc(m0.unsqueeze(2), [MH, DECB, DECT]), ALU.add)
                    dve.tensor_tensor(per_seq(tmprow), per_seq(row(A_)[:, SEQ:N]), bc(gs[:, :, DECT - 1:DECT], [MH, DECB, DECT]),
                                      ALU.add).then_inc(rows_ready, 1)
                    q = GROUP[("aw", 0)]
                    done(("aw", 0))
                    dve.tensor_copy(awt[:, 0:TT].rearrange("p i a h -> p (i a h)"), ps[:, 2 * (q % 4), 0:TT * 2 * MH])
                    dve.tensor_copy(awt[0:NS, TT].rearrange("p a h -> p (a h)"),
                                    ps[0:NS, 2 * (q % 4), TT * 2 * MH:(TT + 1) * 2 * MH]).then_inc(pair_free[q % 4], 1)
                    read_out(dve, ("aw", 0))
                    for i in range(TT + 1):
                        rows = P if i < TT else NS
                        done(("kw", i))
                        q = GROUP[("kw", i)]
                        for h in range(MH):
                            ins = dve.tensor_scalar(kw[0:rows, i, h * MD:(h + 1) * MD], ps[0:rows, 2 * (q % 4), h * MD:(h + 1) * MD],
                                                    awt[0:rows, i, 1, h:h + 1], MD ** -0.5, ALU.mult, ALU.mult)
                        ins.then_inc(pair_free[q % 4], 1)
                    for name in ("mq", "mk"):
                        for h in range(MH):
                            read_out(dve, (name, h))

                    def masked(k):
                        h, j = divmod(k, TT + 1)
                        dve.wait_ge(bc_ready, 2 * h + 1)
                        if k >= 1:
                            dve.wait_ge(e_ready, k)
                        if j < TT:
                            dve.tensor_tensor(gmask, gbc[:, h % 2, j * P:(j + 1) * P], con("sneg"), ALU.add).then_inc(gm_ready, 1)
                        else:
                            dve.tensor_tensor(gmask[0:NS, 0:NS], gbc[0:NS, h % 2, SEQ:N], con("m32")[0:NS, :], ALU.add).then_inc(gm_ready, 1)

                    masked(0)
                    for k in range(MH * (TT + 1)):
                        h, j = divmod(k, TT + 1)
                        if j == 0:
                            if h >= 1:
                                dve.wait_ge(nd_done, h * (TT + 1))
                            dve.wait_ge(bc_ready, 2 * h + 2)
                            link(dve.tensor_tensor(qi[:, 0, :], qm[:, h, SEQ:N], inter[:, h % 2, :], ALU.mult))
                            n0 = sml("n0", "p (h b) -> p h b", h=MH)[:, h, :]
                            dve.tensor_tensor(per_seq(qi[:, 1, :]), per_seq(qi[:, 0, :]), bc(n0.unsqueeze(2), [P, DECB, DECT]),
                                              ALU.mult).then_inc(qi_ready, 1)
                        dve.wait_ge(e_ready, k + 1)
                        dve.wait_ge(ms_done, k + 1)
                        if k >= 2:
                            dve.wait_ge(nd_done, k - 1)
                        if j < TT:
                            w = SEQ - j * P
                            dve.tensor_tensor(St[:, k % 2, 0:w], ps[:, k % 2, 0:w], Et[:, k % 2, 0:w], ALU.mult).then_inc(st_ready, 1)
                        else:
                            dve.tensor_tensor(St[0:NS, k % 2, 0:NS], ps[0:NS, k % 2, 0:NS], Et[0:NS, k % 2, 0:NS], ALU.mult).then_inc(st_ready, 1)
                        if k + 1 < MH * (TT + 1):
                            masked(k + 1)
                        if j == TT:
                            if h >= 1:
                                dve.wait_ge(cs_done, h)
                            v = vtm[0:NS, TT, h * MD:(h + 1) * MD]
                            dve.tensor_tensor(vb[0:NS], bc(v.unsqueeze(1), [NS, DECB, MD]), bc(con("blk")[0:NS, :].unsqueeze(2), [NS, DECB, MD]),
                                              ALU.mult).then_inc(vb_ready, 1)
                            dve.wait_ge(nd_done, (h + 1) * (TT + 1))
                            for num, den, en, dst in ((ps[:, 2, :], ps[:, 3, :], enm[:, h % 2, 0:SEQ], qm[:, h, 0:SEQ]),
                                                      (ps[:, 4, 0:NS], ps[:, 4, NS:2 * NS], enm[:, h % 2, SEQ:N], qm[:, h, SEQ:N])):
                                link(dve.scalar_tensor_tensor(out=en, in0=den, scalar=-1.0, in1=en, op0=ALU.mult, op1=ALU.max))
                                link(dve.tensor_tensor(en, den, en, ALU.max))
                                link(dve.reciprocal(en, en))
                                ins = dve.tensor_tensor(dst, num, en, ALU.mult)
                            ins.then_inc(num_read, 1)
                            dve.wait_ge(cs_done, h + 1)
                            dec = per_seq(inter[:, h % 2, :])[:, :, DECT - 1:DECT]
                            C = Cst[:, h % 2]
                            n0 = sml("n0", "p (h b) -> p h b", h=MH)[:, h, :]
                            dve.tensor_tensor(C, C, bc(dec, [P, DECB, MD]), ALU.mult)
                            link(dve.tensor_tensor(nstat[:, h, 1:1 + DECB], n0, dec.rearrange("p b o -> p (b o)"), ALU.mult))
                            dve.tensor_tensor(nstat[:, h, 1:1 + DECB], nstat[:, h, 1:1 + DECB], ps[:, 5, 0:DECB], ALU.add)
                            dve.tensor_tensor(C.rearrange("p (a b) e -> p a (b e)", a=2), C.rearrange("p (a b) e -> p a (b e)", a=2),
                                              ps[:, 6:8, :], ALU.add).then_inc(head_fin, 1)
                    dve.wait_ge(pc_done, 1)
                    dve.tensor_copy(nstat[:, :, 0], ps[:, 1, 0:MH]).then_inc(pn_ready, 1)
                    for h in range(MH):
                        read_out(dve, ("mn", h))
                        link(dve.reciprocal(rstd[:, :], rstd[:, :]))
                        link(dve.scalar_tensor_tensor(out=qm[:, h, :], in0=qm[:, h, :], scalar=sml("mng")[:, h:h + 1], in1=rstd[:, :],
                                                      op0=ALU.mult, op1=ALU.mult))
                        dve.tensor_tensor(haT[:, h, :], haT[:, h, :], qm[:, h, :], ALU.mult).then_inc(ha_ready, 1)
                    for n in range(6):
                        out, free = done(("rope", n))
                        src = qT[:, n, :] if n < 4 else kT[:, n - 4, :]
                        dst = qrT[:, n, :] if n < 4 else kT[:, n - 4, :]
                        if n:
                            dve.wait_ge(rope_ready, n)
                        dve.tensor_tensor(halves(rtmp[:, 0, :]), out, halves(sin), ALU.mult).then_inc(free, 1)
                        link(dve.tensor_tensor(rtmp[:, 1, :], src, cos, ALU.mult))
                        dve.tensor_tensor(dst, rtmp[:, 0, :], rtmp[:, 1, :], ALU.add).then_inc(rope_ready, 1)
                    dve.wait_ge(rope_ready, 4)
                    dve.wait_ge(pool_step, 1)
                    for a, src in enumerate((qT, qrT)):
                        for g in range(NKV):
                            for r in range(R):
                                ins = dve.tensor_copy(qb[g * HD:(g + 1) * HD, a, :, g * 16 + r * 4:g * 16 + r * 4 + 4],
                                                      per_seq(src[g * HD:(g + 1) * HD, r, SEQ:N]))
                    ins.then_inc(qb_ready, 1)

                    def att_max(k):
                        i, g, rp, br = STEPS[k]
                        dve.wait_ge(s_done, k + 1)
                        b = 2 * (k % 2)
                        width = NCP if br == 0 else (i + 1) * P
                        lo = 0 if br == 0 else i * P
                        mask = cneg[:, i, :] if br == 0 else con("qneg")
                        link(dve.tensor_tensor(ps[:, b:b + 2, lo:width], ps[:, b:b + 2, lo:width], bc(mask.unsqueeze(1), [P, 2, width - lo]), ALU.add))
                        dve.tensor_reduce(stat[:, k % 2, :], ps[:, b:b + 2, 0:width], AX.X, ALU.max, negate=True).then_inc(max_ready, 1)

                    def diagonal(k, heads, total, gates):
                        link(dve.tensor_scalar(stat[:, 4, 0:heads], total, TINY, None, ALU.max))
                        link(dve.reciprocal(stat[:, 5, 0:heads], stat[:, 4, 0:heads]))
                        link(dve.tensor_tensor(stat[:, 6, 0:heads], stat[:, 5, 0:heads], gates, ALU.mult))
                        dve.tensor_tensor(Dg[:, k % 2, 0:heads, :], bc(ident.unsqueeze(1), [P, heads, P]),
                                          bc(stat[:, 6, 0:heads].unsqueeze(2), [P, heads, P]), ALU.mult).then_inc(d_ready, 1)

                    def att_diag(k):
                        i, g, rp, br = STEPS[k]
                        dve.wait_ge(exp_done, k + 1)
                        total = stat[:, 2 + k % 2, :]
                        if br == 0:
                            link(dve.tensor_tensor(Pt[:, k % 2, :, 0:NCP], Pt[:, k % 2, :, 0:NCP], bc(c01[:, i, :].unsqueeze(1), [P, 2, NCP]), ALU.mult))
                            link(dve.tensor_reduce(total, Pt[:, k % 2, :, 0:NCP], AX.X, ALU.add))
                        if k >= 2:
                            dve.wait_ge(t_done, chunks_of(k - 2)[-1][0] + 1)
                        gv = gate[:, i, :].rearrange("p (h b) -> p h b", b=3)
                        diagonal(k, 2, total, gv[:, g * R + 2 * rp:g * R + 2 * rp + 2, br])

                    att_max(0)
                    att_diag(0)
                    for k in range(NSTEP):
                        if k + 1 < NSTEP:
                            att_max(k + 1)
                        for x, j0, nj in chunks_of(k):
                            if not evac_on_act(x):
                                rows = NCP if STEPS[k][3] == 0 else P
                                dve.wait_ge(t_done, x + 1)
                                if x >= 2:
                                    dve.wait_ge(o_done, x - 1)
                                dve.tensor_copy(PT[0:rows, x % 2, 0:nj * 2 * P], ps[0:rows, 4 + x % 2, 0:nj * 2 * P]).then_inc(t_free[x % 2], 1)
                        if k + 1 < NSTEP:
                            att_diag(k + 1)
                    dve.wait_ge(gs_done, 1)
                    for hb in range(2):
                        gall = ps[:, 3, hb * 24:(hb + 1) * 24].rearrange("p (h b) -> p b h", b=3)
                        link(dve.tensor_tensor(gtmp[:, :, :], gall, bc(con("rowm").unsqueeze(1), [P, 3, NH]), ALU.mult))
                        link(dve.tensor_reduce(gsel[:, hb, :], gtmp[:, :, :], AX.X, ALU.add))

                    def samp_max(m):
                        hb, br = SSTEPS[m]
                        dve.wait_ge(s_done, NSTEP + m + 1)
                        width = P if br == 0 else PAST + NS
                        lo = 0 if br == 0 else PAST
                        mask = kneg[:, hb, :] if br == 0 else nneg[:, hb, :]
                        link(dve.tensor_tensor(ps[:, m % 2, lo:width], ps[:, m % 2, lo:width], mask, ALU.add))
                        dve.tensor_reduce(stat[:, m % 2, 0:1], ps[:, m % 2, 0:width], AX.X, ALU.max, negate=True).then_inc(max_ready, 1)

                    def samp_diag(m):
                        hb, br = SSTEPS[m]
                        dve.wait_ge(exp_done, NSTEP + m + 1)
                        dve.wait_ge(t_done, NPC + max(m - 1, 0))
                        diagonal(m, 1, stat[:, 2 + m % 2, 0:1], gsel[:, hb, br:br + 1])

                    for m in range(6):
                        samp_max(m)
                        samp_diag(m)
                    dve.wait_ge(hb_ready, NSTEP // 3 + 2)
                    for m in range(KC):
                        if m:
                            dve.wait_ge(merged_ready, m)
                        for n, name in enumerate(("a", "b")):
                            read_out(dve, (("ga", "gb")[n], m))
                            out, free = done((name, m))
                            dve.tensor_tensor(halves(mt[:, n, :]), out, halves(sg[:, n, :]), ALU.mult).then_inc(free, 1)
                        read_out(dve, ("a", m))
                        read_out(dve, ("b", m))
                        dve.tensor_tensor(merged[:, m, :], mt[:, 0, :], mt[:, 1, :], ALU.add).then_inc(merged_ready, 1)
                    for m in range(KC):
                        out, free = done(("out", m))
                        dve.tensor_tensor(halves(xT[:, m, :]), halves(xT[:, m, :]), out, ALU.add).then_inc(free, 1)
                    read_out(dve, ("n2", 0))
                    normed(sml("n2g"), KC)
                    for m in range(NFF):
                        if m == 0:
                            dve.wait_ge(nsa_stored, 48)
                        read_out(dve, ("fg", m))
                        out, free = done(("fu", m))
                        dve.tensor_tensor(halves(act_[:, m, :]), out, halves(sg[:, m % 2, :]), ALU.mult).then_inc(free, 1)
                    for m in range(KC):
                        out, free = done(("dn", m))
                        dve.tensor_tensor(halves(xT[:, m, :]), halves(xT[:, m, :]), out, ALU.add).then_inc(free, 1)

            for s in layer_sems:
                nc.sync.sem_clear(s)
            nc.all_engine_barrier()

        fin_sq = ctx.enter_context(nc.semaphore("fin_sq"))
        fin_sum = ctx.enter_context(nc.semaphore("fin_sum"))
        fin_root = ctx.enter_context(nc.semaphore("fin_root"))
        fin_step = ctx.enter_context(nc.semaphore("fin_step"))
        fin_y = ctx.enter_context(nc.semaphore("fin_y"))
        fin_stored = ctx.enter_context(nc.semaphore("fin_stored"))
        with nc.Block() as block:
            @block.scalar
            def _(act):
                for k in range(KC):
                    if k >= 2:
                        act.wait_ge(fin_sum, k - 1)
                    act.activation(sq[:, k % 2, :], xT[:, k, :], ACT.Square).then_inc(fin_sq, 1)
                act.wait_ge(fin_sum, KC)
                act.activation(halves(rstd[:, :]), ps[:, 0:2, 0:NHALF], ACT.Sqrt, bias=eps[:, :], scale=1.0 / D).then_inc(fin_root, 1)

            @block.tensor
            def _(pe):
                for k in range(KC):
                    pe.wait_ge(fin_sq, k + 1)
                    for a in range(2):
                        mm = pe.matmul(ps[:, a, 0:NHALF], ones[:, :], sq[:, k % 2, a * NHALF:(a + 1) * NHALF],
                                       start=(k == 0), stop=(k == KC - 1))
                    mm.then_inc(fin_sum, 1)

            @block.vector
            def _(dve):
                dve.wait_ge(fin_root, 1)
                dve.reciprocal(rstd[:, :], rstd[:, :]).then_inc(fin_step, 1)
                dve.wait_ge(fin_step, 1)
                fng = con("fng")
                for k in range(KC):
                    dve.scalar_tensor_tensor(out=hT[:, k, :], in0=xT[:, k, :], scalar=fng[:, k:k + 1], in1=rstd[:, :],
                                             op0=ALU.mult, op1=ALU.mult).then_inc(fin_y, 1)

            @block.sync
            def _(sp):
                for k in range(KC):
                    sp.wait_ge(fin_y, k + 1)
                    sp.dma_start(y_out[:, k, :], hT[:, k, :]).then_inc(fin_stored, 16)
                sp.wait_ge(fin_stored, 16 * KC)


def shape_constants():
    c = np.zeros((P, CONST_W), np.float32)

    def put(name, value):
        a, b = CONST[name]
        v = np.asarray(value, np.float32)
        v = v.reshape(v.shape[0], -1)
        c[:v.shape[0], a:b] = v

    pos = np.concatenate([np.arange(SEQ), np.tile(PAST + np.arange(DECT), DECB)]).astype(np.float32)
    half = HD // 8
    inv = (np.float32(500000.0) ** (-np.arange(half, dtype=np.float32) / np.float32(half))).astype(np.float32)
    ang = (pos[None, :] * inv[:, None]).astype(np.float32)
    cos, sin, rot = np.ones((P, N)), np.zeros((P, N)), np.zeros((P, P))
    for g in range(NKV):
        for a in range(2):
            cos[g * HD + a * half:g * HD + (a + 1) * half] = np.cos(ang.astype(np.float64))
            sin[g * HD + a * half:g * HD + (a + 1) * half] = np.sin(ang.astype(np.float64))
        for d in range(half):
            rot[g * HD + half + d, g * HD + d] = -1.0
            rot[g * HD + d, g * HD + half + d] = 1.0
    put("cos", cos)
    put("sin", sin)
    put("rot", rot)
    put("ident", np.eye(P))
    t = np.arange(P)
    put("qneg", np.where(t[None, :] <= t[:, None], 0.0, NEG))
    put("sneg", np.where(t[:, None] <= t[None, :], 0.0, NEG))
    q = t[:, None, None] + P * np.arange(TT)[None, :, None]
    seen = np.arange(NCP)[None, None, :] * STRIDE + CLEN - 1 <= q
    put("cneg", np.where(seen, 0.0, NEG))
    put("c01", seen)
    put("sel4", np.repeat(np.eye(MH)[:, :, None], P, 2))
    s = np.arange(NS)
    same = s[:, None] // DECT == s[None, :] // DECT
    put("m32", np.where(same & (s[:, None] <= s[None, :]), 0.0, NEG))
    put("blk", s[:, None] // DECT == np.arange(DECB)[None, :])
    b4, g, r, tok = t // 32, t // 16 % 2, t // 4 % 4, t % 4
    b = b4[:, None] + 4 * np.arange(2)[None, :]
    put("nneg", np.where((b[:, :, None] == s // DECT) & (s % DECT <= tok[:, None, None]), 0.0, NEG))
    put("kneg", np.where((b[:, :, None] == t // SBLK) & (t % SBLK < SBLK - 1), 0.0, NEG))
    put("tsel", s[:, None, None] == (b * DECT + tok[:, None]).T[None])
    put("rowm", (g * R + r)[:, None] == np.arange(NH)[None, :])
    return c


def chunked(a):
    return a.reshape(-1, P, a.shape[-1]).transpose(1, 0, 2)


def weight_units(l, w):
    w_in = w["w_in"][l]
    at = np.cumsum([0, 512, 512, 512, 4, 4, 512, 768, 24, D, D])
    u, v, o, ig, fg, q, kv, ng, ga, gb = (w_in[:, a:b] for a, b in zip(at[:-1], at[1:]))
    kv = kv.reshape(D, 6, P)
    q = q.reshape(D, NKV, R, HD).transpose(0, 2, 1, 3).reshape(D, 512)
    out = np.zeros((len(UNITS), P, UCOLS), np.float32)

    def put(key, a):
        a = np.ascontiguousarray(a).reshape(P, -1)
        out[UNIT[key], :, :a.shape[1]] = a

    tm = np.concatenate([v, kv[:, 3], kv[:, 5], ng], 1)
    for k in range(KC):
        put(("tm", k), tm[k * P:(k + 1) * P])
    gates = np.zeros((D, P), np.float32)
    gates[:, 0:MH] = ig
    gates[:, 32:32 + MH] = fg
    put(("if", 0), chunked(gates))
    kk = kv[:, [0, 1, 2, 4]].reshape(D, 512)
    for m in range(4):
        for name, a in (("u", u), ("o", o), ("q", q), ("k", kk)):
            put((name, m), chunked(a[:, m * P:(m + 1) * P]))
    for v2, name in enumerate(("cmp_w1_k", "cmp_w1_v")):
        w1 = w[name][l].transpose(1, 0, 2)
        w1 = np.concatenate([w1, w1], 0)
        for n in range(4):
            put(("w1", 4 * v2 + n), w1[:, 8 * n:8 * n + 8])
    wb = w["w_branch_b"][l].reshape(NKV, R, HD, D).transpose(1, 0, 2, 3).reshape(512, D)
    for m in range(KC):
        c = slice(m * P, (m + 1) * P)
        put(("ga", m), chunked(ga[:, c]))
        put(("gb", m), chunked(gb[:, c]))
        put(("ab", m), np.concatenate([chunked(w["w_branch_a"][l][:, c]), chunked(wb[:, c])], 1))
        put(("out", m), chunked(w["w_out"][l][:, c]))
        dn = chunked(w["w_ffn_down"][l][:, c])
        for n in range(3):
            put(("dn", 3 * m + n), dn[:, 8 * n:8 * n + 8])
    for m in range(NFF):
        put(("fg", m), chunked(w["w_ffn_up"][l][:, m * P:(m + 1) * P]))
        put(("fu", m), chunked(w["w_ffn_up"][l][:, (NFF + m) * P:(NFF + m + 1) * P]))
    return out


def small_weights(l, w):
    out = np.zeros((P, SMALL_W), np.float32)

    def put(name, a):
        a = np.ascontiguousarray(a)
        a = a.reshape(a.shape[0], -1)
        lo, hi = SMALL[name]
        out[:a.shape[0], lo:lo + a.shape[1]] = a

    def vec(a):
        return a.reshape(-1, P).T

    put("n1g", vec(w["norm1_g"][l]))
    put("n2g", vec(w["norm2_g"][l]))
    put("mng", vec(w["mlstm_norm_g"][l]))
    put("cw", w["conv_w"][l].reshape(CONV, 4, P).transpose(2, 1, 0))
    put("cb", vec(w["conv_b"][l]))
    put("wmq", w["w_mq"][l].transpose(1, 0, 2))
    put("wmk", w["w_mk"][l].transpose(1, 0, 2))
    put("w2", np.stack([w["cmp_w2_k"][l], w["cmp_w2_v"][l]], 1))
    pe = np.stack([w["cmp_pe_k"][l].T, w["cmp_pe_v"][l].T], 1)
    put("pe", np.concatenate([pe, pe], 0))
    put("bi", w["b_gates"][l][:MH, None])
    put("bf", w["b_gates"][l][MH:, None])
    put("m0", w["state_mlstm_m"][l].T)
    put("n0", w["state_mlstm_n"][l].transpose(2, 1, 0))
    put("cs", w["state_mlstm_conv"][l].reshape(DECB, CONV - 1, 4, P).transpose(3, 2, 0, 1))
    return out


def kernel(**inputs):
    import concourse.bacc as bacc
    from concourse.bass_utils import run_bass_kernel_spmd

    w = {k: np.asarray(v) for k, v in inputs.items()}
    x = np.concatenate([w["x_prompt"].reshape(SEQ, D), w["x_sample"].reshape(NS, D)], 0)
    const = shape_constants()
    a, b = CONST["fng"]
    const[:, a:b] = w["final_norm_g"].reshape(KC, P).T
    pages = w["cache_kv_pages"]
    pool = pages.shape[1]
    pg = pages.reshape(DEPTH, pool, PAGE, 4, P)
    turned = pg[:, :, :, 0:3].transpose(0, 1, 4, 3, 2).reshape(DEPTH, pool, P, 3 * PAGE)
    packed = np.concatenate([turned, pg[:, :, :, 3]], 3)
    cw = w["cache_win"].reshape(DEPTH, DECB, PAST, 2, P)
    wk = cw[:, :, :, 0].transpose(0, 3, 1, 2)
    wv = cw[:, :, :, 1].reshape(DEPTH, DECB, NPG, P, P).transpose(0, 3, 1, 2, 4).reshape(DEPTH, P, DECB, PAST)
    win = np.stack([wk, wv], 3).reshape(DEPTH, P, DECB * 2 * PAST)
    arrays = {
        "xT": chunked(np.ascontiguousarray(x.T)),
        "W": np.stack([weight_units(l, w) for l in range(DEPTH)]),
        "small": np.stack([small_weights(l, w) for l in range(DEPTH)]),
        "consts": const,
        "c0": w["state_mlstm_C"].transpose(0, 2, 3, 1, 4).reshape(DEPTH, MH, P, DECB * MD),
        "pages": packed,
        "table": w["page_table"].reshape(1, -1).astype(np.int32),
        "win": win,
        "cwin": w["cache_win"].reshape(DEPTH, DECB, PAST * 2 * P),
    }
    outs = {
        "y": (P, KC, N), "fm": (DEPTH, P, 4, N), "tm": (DEPTH, P, TT + 1, 2 * P), "u": (DEPTH, P, 4, UW - SEQ),
        "pC": (DEPTH, P, MH * MD), "pn": (DEPTH, P, MH * (1 + DECB)), "m": (DEPTH, MH, N),
        "sC": (DEPTH, MH, P, DECB * MD), "oldwin": (DEPTH, DECB, (PAST - DECT) * 2 * P),
    }
    nc = bacc.Bacc("TRN2", target_bir_lowering=False, num_devices=1)
    ins, args = {}, []
    for name, v in arrays.items():
        v = np.ascontiguousarray(v)
        ins["in_" + name] = v
        args.append(nc.dram_tensor("in_" + name, v.shape, mybir.dt.from_np(v.dtype), kind="ExternalInput").ap())
    oap = {n: nc.dram_tensor("out_" + n, s, F32, kind="ExternalOutput").ap() for n, s in outs.items()}
    build_step(nc, *args, *(oap[n] for n in ("y", "fm", "tm", "u", "pC", "pn", "m", "sC", "oldwin")))
    got = run_bass_kernel_spmd(nc, [ins], core_ids=[0]).results[0]
    o = {n: np.asarray(got["out_" + n]) for n in outs}

    y = o["y"].transpose(2, 1, 0).reshape(N, D)
    fm, tmv = o["fm"], o["tm"]
    kc, vc, ks, kwin = (fm[:, :, n].transpose(0, 2, 1) for n in range(4))
    tok = np.concatenate([tmv[:, :, :TT].transpose(0, 2, 1, 3).reshape(DEPTH, SEQ, 2 * P), tmv[:, :NS, TT]], 1)
    vs, vw = tok[..., :P], tok[..., P:]
    rows = np.stack([kc, vc, ks, vs], 2).reshape(DEPTH, N, 4, NKV, HD)
    wins = np.stack([kwin, vw], 2).reshape(DEPTH, N, 2, NKV, HD)
    old = o["oldwin"].reshape(DEPTH, DECB, PAST - DECT, 2, NKV, HD)
    u = o["u"]
    hist = CONV - 1
    p_conv = u[..., :hist].transpose(0, 3, 2, 1).reshape(DEPTH, 1, hist, 512)
    s_conv = u[..., hist:].reshape(DEPTH, P, 4, DECB, hist + DECT)[..., DECT:].transpose(0, 3, 4, 2, 1).reshape(DEPTH, DECB, hist, 512)
    n_ = o["pn"].reshape(DEPTH, P, MH, 1 + DECB).transpose(0, 3, 2, 1)
    m_ = o["m"]
    got = (
        y[:SEQ].reshape(1, SEQ, D), y[SEQ:].reshape(DECB, DECT, D),
        rows[:, None, :SEQ], wins[:, None, :SEQ],
        o["pC"].reshape(DEPTH, P, MH, MD).transpose(0, 2, 1, 3)[:, None], n_[:, 0:1], m_[:, None, :, SEQ - 1], p_conv,
        rows[:, SEQ:].reshape(DEPTH, DECB, DECT, 4, NKV, HD),
        np.concatenate([old, wins[:, SEQ:].reshape(DEPTH, DECB, DECT, 2, NKV, HD)], 2),
        o["sC"].reshape(DEPTH, MH, P, DECB, MD).transpose(0, 3, 1, 2, 4), n_[:, 1:],
        m_[:, :, SEQ:].reshape(DEPTH, MH, DECB, DECT)[..., -1].transpose(0, 2, 1), s_conv,
    )
    return tuple(np.ascontiguousarray(a) for a in got)
```

```python
from contextlib import ExitStack

import numpy as np

import concourse.bass as bass
from concourse import mybir

ALU = mybir.AluOpType
ACT = mybir.ActivationFunctionType
F32 = mybir.dt.float32
I32 = mybir.dt.int32
F32R = mybir.dt.float32r
AX = mybir.AxisListType

P = 128
DEPTH, D, SEQ, DECB, DECT, PAST, PAGE = 2, 1024, 512, 8, 4, 256, 128
KC = D // P
NS = DECB * DECT
N = SEQ + NS
NHALF = N // 2
MH, MD = 4, 128
NH, NKV, HD = 8, 2, 64
R = NH // NKV
CONV = 4
STRIDE, CLEN, HID = 16, 32, 128
NFF = 2816 // P
TT = SEQ // P
NPG = PAST // PAGE
EPS, NEG, TINY = 1e-6, -1e30, 1e-30
RAW = SEQ + DECB * PAST
NBLK = RAW // STRIDE
RC = NBLK + 2
NCP = SEQ // STRIDE - 1
PBLK = SEQ // STRIDE
SBLK = PAST // STRIDE
UW = (CONV - 1) + SEQ + DECB * (CONV - 1 + DECT)

NFH = NFF // 2

UNITS = ([("tm", k) for k in range(KC)] + [("u", m) for m in range(4)] + [("if", 0)]
         + [("o", m) for m in range(4)] + [("q", m) for m in range(4)] + [("k", m) for m in range(4)]
         + [("w1", n) for n in range(8)]
         + [(w, m) for m in range(KC) for w in ("ga", "gb", "ab")]
         + [("out", m) for m in range(KC)]
         + [u for f in range(2) for u in
            [(w, m) for m in range(f * NFH, (f + 1) * NFH) for w in ("fg", "fu")] + [("dn", n) for n in range(f * NFH, (f + 1) * NFH)]])
UNIT = {key: n for n, key in enumerate(UNITS)}
RING = 8
UCOLS = 1024
TMC = 512 + 280

GROUPS = ([("n1", 0)] + [("tm", i) for i in range(TT + 1)] + [("u", m) for m in range(4)] + [("if", 0)]
          + [("o", m) for m in range(4)] + [(w, h) for h in range(MH) for w in ("mq", "mk")]
          + [("aw", 0)] + [("kw", i) for i in range(TT + 1)]
          + [("mn", h) for h in range(MH)]
          + [("q", m) for m in range(4)] + [("k", m) for m in range(4)] + [("rope", n) for n in range(6)]
          + [(w, m) for m in range(KC) for w in ("ga", "gb", "a", "b")]
          + [("out", m) for m in range(KC)] + [("n2", 0)]
          + [g for f in range(2) for g in
             [(w, m) for m in range(f * NFH, (f + 1) * NFH) for w in ("fg", "fu")] + [("dn", f * KC + m) for m in range(KC)]])
GROUP = {key: n for n, key in enumerate(GROUPS)}
CORE_AT = GROUP[("mn", 0)]
ATTN_AT = GROUP[("ga", 0)]


SPLITS = [key for key in UNITS if key[0] in ("ga", "gb", "out", "fg", "fu", "dn")]
SPLIT = {key: n for n, key in enumerate(SPLITS)}
SRING = 3


def columns(spec):
    at, out = 0, {}
    for name, width in spec:
        out[name] = (at, at + width)
        at += width
    return out, at


SMALL, SMALL_W = columns([("n1g", KC), ("n2g", KC), ("mng", MH), ("cw", 4 * CONV), ("cb", 4), ("wmq", MH * MD),
                          ("wmk", MH * MD), ("w2", 2 * HD), ("pe", 2 * CLEN), ("bi", 1), ("bf", 1), ("m0", DECB),
                          ("n0", MH * DECB), ("cs", 4 * DECB * (CONV - 1))])
CONST, CONST_W = columns([("cos", N), ("sin", N), ("rot", P), ("ident", P), ("qneg", P), ("sneg", P),
                          ("cneg", TT * NCP), ("c01", TT * NCP), ("sel4", MH * P), ("m32", NS), ("blk", DECB),
                          ("nneg", 2 * NS), ("kneg", 2 * P), ("tsel", 2 * P), ("rowm", NH), ("fng", KC)])


def arena(spec):
    return columns(spec)


MIX, MIX_W = arena([("upad", 4 * UW), ("cT", 4 * N), ("ctmp", 2 * N), ("qm", MH * N), ("km", MH * N),
                    ("vtm", (TT + 1) * 512), ("kw", (TT + 1) * 512), ("C", 2 * DECB * MD), ("vb", DECB * MD),
                    ("rows", 4 * N + 64)])
CORE, CORE_W = arena([("gbc", 2 * N), ("enm", 2 * N), ("int", 2 * NS), ("E", 2 * 512), ("St", 2 * 512),
                      ("qi", 2 * NS), ("gmask", P), ("pC", MH * MD)])
assert CORE_W <= 4 * UW + 4 * N + 2 * N
NSA, NSA_W = arena([("qT", 4 * N), ("qrT", 4 * N), ("kT", 2 * N), ("raw", 2 * STRIDE * RC), ("knew", 2 * NS), ("stage", 4 * 2 * PAGE), ("selp", DECB * 2 * NPG * P),
                    ("P", 2 * 2 * 512), ("D", 2 * 2 * P), ("PT", 2 * 512), ("qb", 2 * DECB * 32), ("hid", 2 * 2 * NBLK),
                    ("kcT", NBLK), ("vcp", P), ("vcs", P), ("rtmp", 2 * N)])
MIX_AT = KC * N + MH * N + R * N
LATE, LATE_W = columns([("xl", KC * N), ("skip", 8704 - KC * N), ("mh", KC * N), ("ml", KC * N), ("xh", KC * N),
                        ("wh", SRING * UCOLS), ("wl", SRING * UCOLS), ("sg", 2 * N), ("mt", 2 * N), ("t", 2 * N)])
AH_AT, AL_AT = KC * N, KC * N + NFH * N
assert AL_AT + NFH * N <= LATE["xh"][0] and LATE["mh"][0] == MIX_AT
SLAB_W = max(MIX_AT + max(MIX_W, NSA_W), LATE_W)


def build_step(nc, xT_in, W_in, small_in, const_in, c0_in, pages_in, table_in, win_in, cwin_in,
               y_out, fm_out, raw_out, knew_out, tm_out, u_out, pC_out, pn_out, m_out, sC_out, oldwin_out):
    with ExitStack() as ctx:
        def sb(name, shape, dt=F32):
            return ctx.enter_context(nc.sbuf_tensor(name, shape, dt))

        def sem(name):
            s = ctx.enter_context(nc.semaphore(name))
            layer_sems.append(s)
            return s

        layer_sems = []
        slab_at = -(-nc.sbuf_base // 32) * 32
        slab = sb("slab", [P, SLAB_W])

        def at_slab(name, col, shape):
            return nc.alloc_sbuf_tensor_at(name, shape, F32R, offset=slab_at + 4 * col)

        xT = sb("xT", [P, KC, N])
        hT = slab[:, 0:KC * N].rearrange("p (k n) -> p k n", k=KC)
        haT = slab[:, KC * N:KC * N + MH * N].rearrange("p (k n) -> p k n", k=MH)
        hbT = slab[:, KC * N + MH * N:MIX_AT].rearrange("p (k n) -> p k n", k=R)
        xl = at_slab("xl", LATE["xl"][0], [P, KC, N])
        xh = at_slab("xh", LATE["xh"][0], [P, KC, N])
        mh = at_slab("mh", LATE["mh"][0], [P, KC, N])
        ml = at_slab("ml", LATE["ml"][0], [P, KC, N])
        ah = at_slab("ah", AH_AT, [P, NFH, N])
        al = at_slab("al", AL_AT, [P, NFH, N])
        wh = at_slab("wh", LATE["wh"][0], [P, SRING, UCOLS])
        wl = at_slab("wl", LATE["wl"][0], [P, SRING, UCOLS])
        ring = sb("ring", [P, RING, UCOLS])
        const = sb("const", [P, CONST_W])
        small = sb("small", [P, SMALL_W])
        hbrows = hbT
        sq = sb("sq", [P, 2, N])
        rstd = sb("rstd", [P, N])
        vkv = sb("vkv", [P, TT + 1, 2 * P])
        gate = sb("gate", [P, TT + 1, NH * 3])
        ones = sb("ones", [P, P])
        eps = sb("eps", [P, 1])
        awt = sb("awt", [P, TT + 1, 2, MH])
        stat = sb("stat", [P, 16, 2])
        nstat = sb("nstat", [P, MH, 1 + DECB])
        gsel = sb("gsel", [P, 2, 3])
        gtmp = sb("gtmp", [P, 3, NH])
        hbias = sb("hbias", [P, 2])
        table = sb("table", [1, DECB * NPG], I32)
        big = slab[:, MIX_AT:SLAB_W]
        acc = sb("acc", [P, N])
        ps = ctx.enter_context(nc.psum_tensor("ps", [P, 8, 512], F32))

        def cut(lay, name, pattern=None, base=None, **k):
            a, b = lay[name]
            v = (big if base is None else base)[:, a:b]
            return v.rearrange(pattern, **k) if pattern else v

        def con(name, pattern=None, **k):
            return cut(CONST, name, pattern, const, **k)

        def sml(name, pattern=None, **k):
            return cut(SMALL, name, pattern, small, **k)

        upad = cut(MIX, "upad", "p (c n) -> p c n", c=4)
        cT = cut(MIX, "cT", "p (c n) -> p c n", c=4)
        ctmp = cut(MIX, "ctmp", "p (c n) -> p c n", c=2)
        qm = cut(MIX, "qm", "p (c n) -> p c n", c=MH)
        km = cut(MIX, "km", "p (c n) -> p c n", c=MH)
        vtm = cut(MIX, "vtm", "p (i n) -> p i n", n=512)
        kw = cut(MIX, "kw", "p (i n) -> p i n", n=512)
        Cst = cut(MIX, "C", "p (a b e) -> p a b e", a=2, b=DECB)
        vb = cut(MIX, "vb", "p (b e) -> p b e", b=DECB)
        rowsx = cut(MIX, "rows")
        pCs = cut(CORE, "pC", "p (h e) -> p h e", h=MH)
        gbc = cut(CORE, "gbc", "p (a n) -> p a n", a=2)
        enm = cut(CORE, "enm", "p (a n) -> p a n", a=2)
        inter = cut(CORE, "int", "p (a n) -> p a n", a=2)
        Et = cut(CORE, "E", "p (a n) -> p a n", a=2)
        St = cut(CORE, "St", "p (a n) -> p a n", a=2)
        qi = cut(CORE, "qi", "p (a n) -> p a n", a=2)
        gmask = cut(CORE, "gmask")
        qT = cut(NSA, "qT", "p (c n) -> p c n", c=4)
        qrT = cut(NSA, "qrT", "p (c n) -> p c n", c=4)
        kT = cut(NSA, "kT", "p (c n) -> p c n", c=2)
        raw = cut(NSA, "raw", "p (v l n) -> p v l n", v=2, l=STRIDE)
        knew = cut(NSA, "knew", "p (v n) -> p v n", v=2)
        stage = cut(NSA, "stage", "p (a v n) -> p a v n", a=4, v=2)
        winp = cut(NSA, "raw")[:, 0:DECB * 2 * NPG * P].rearrange("p (b v j s) -> p b v j s", b=DECB, v=2, j=NPG)
        selp = cut(NSA, "selp", "p (b j v s) -> p b j v s", b=DECB, j=NPG, v=2)
        Pt = cut(NSA, "P", "p (a r n) -> p a r n", a=2, r=2)
        Dg = cut(NSA, "D", "p (a r n) -> p a r n", a=2, r=2)
        PT = cut(NSA, "PT", "p (a n) -> p a n", a=2)
        qb = cut(NSA, "qb", "p (a b m) -> p a b m", a=2, b=DECB)
        hid = cut(NSA, "hid", "p (v g n) -> p v g n", v=2, g=2)
        kcT = cut(NSA, "kcT")
        vcp = cut(NSA, "vcp")
        vcs = cut(NSA, "vcs")
        rtmp = cut(NSA, "rtmp", "p (a n) -> p a n", a=2)
        sg = cut(LATE, "sg", "p (a n) -> p a n", slab, a=2)
        mt = cut(LATE, "mt", "p (a n) -> p a n", slab, a=2)
        tbuf = cut(LATE, "t", "p (a n) -> p a n", slab, a=2)

        def row(n):
            if n < 4:
                return hbrows[0:MH, n, :]
            return rowsx[0:MH, (n - 4) * N:(n - 3) * N]

        I_, Z_, L_, F_, M_, A_, G_, W_ = range(8)
        EN_, IN_ = L_, None
        introw = rowsx[0:MH, 4 * N:4 * N + NS]
        tmprow = rowsx[0:MH, 4 * N + NS:4 * N + 2 * NS]

        def per_seq(r):
            return r.rearrange("p (b t) -> p b t", t=DECT)

        def halves(v):
            return v.rearrange("p (a n) -> p a n", a=2)

        def pair(q, cols=NHALF, rows=P):
            s = q % 4
            return ps[0:rows, 2 * s:2 * s + 2, 0:cols]

        def bc(ap, shape):
            return ap.to_broadcast(shape)

        cos, sin, ident = con("cos"), con("sin"), con("ident")
        rot = con("rot")
        sel4 = con("sel4", "p (h n) -> p h n", h=MH)
        cneg = con("cneg", "p (i n) -> p i n", i=TT)
        c01 = con("c01", "p (i n) -> p i n", i=TT)
        nneg = con("nneg", "p (a n) -> p a n", a=2)
        kneg = con("kneg", "p (a n) -> p a n", a=2)
        tsel = con("tsel", "p (a n) -> p a n", a=2)

        unit_landed = [sem(f"unit_landed{s}") for s in range(RING)]
        pair_done = sem("pair_done")
        pair_free = [sem(f"pair_free{s}") for s in range(4)]
        small_landed = sem("small_landed")
        page_landed = [sem(f"page_landed{i}") for i in range(4)]
        raw_ready = sem("raw_ready")
        sel_landed = sem("sel_landed")
        win_landed = sem("win_landed")
        c0_landed = [sem(f"c0_landed{s}") for s in range(2)]
        stored = sem("stored")
        cstored = sem("cstored")
        history_ready = sem("history_ready")
        tm_used = sem("tm_used")
        w1_used = sem("w1_used")
        dn_used = sem("dn_used")
        wh_ready = sem("wh_ready")
        wl_ready = sem("wl_ready")
        xh_ready = sem("xh_ready")
        xl_ready = sem("xl_ready")
        t_ready = sem("t_ready")
        th_ready = sem("th_ready")
        act_ready = sem("act_ready")
        u_stored = sem("u_stored")
        mix_stored = sem("mix_stored")
        raw_stored = sem("raw_stored")
        nsa_stored = sem("nsa_stored")
        num_read = sem("num_read")
        pn_ready = sem("pn_ready")
        sq_ready = sem("sq_ready")
        sq_used = sem("sq_used")
        h_ready = sem("h_ready")
        conv_ready = sem("conv_ready")
        c_ready = sem("c_ready")
        ln_ready = sem("ln_ready")
        rows_ready = sem("rows_ready")
        wexp_ready = sem("wexp_ready")
        bc_done = sem("bc_done")
        bc_ready = sem("bc_ready")
        ms_done = sem("ms_done")
        gm_ready = sem("gm_ready")
        e_ready = sem("e_ready")
        st_ready = sem("st_ready")
        nd_done = sem("nd_done")
        head_fin = sem("head_fin")
        qi_ready = sem("qi_ready")
        msq_ready = sem("msq_ready")
        ha_ready = sem("ha_ready")
        vb_ready = sem("vb_ready")
        cs_done = sem("cs_done")
        pc_done = sem("pc_done")
        pc_ready = sem("pc_ready")
        rope_ready = sem("rope_ready")
        hid_ready = sem("hid_ready")
        cmp_done = sem("cmp_done")
        cmp_ready = sem("cmp_ready")
        qb_ready = sem("qb_ready")
        s_done = sem("s_done")
        max_ready = sem("max_ready")
        exp_done = sem("exp_done")
        d_ready = sem("d_ready")
        t_done = sem("t_done")
        t_free = [sem(f"t_free{s}") for s in range(2)]
        o_done = sem("o_done")
        hb_ready = sem("hb_ready")
        gs_done = sem("gs_done")
        merged_ready = sem("merged_ready")
        dve_step = sem("dve_step")
        act_step = sem("act_step")
        pool_step = sem("pool_step")

        first_sems = len(layer_sems)
        start_landed = ctx.enter_context(nc.semaphore("start_landed"))
        start_step = ctx.enter_context(nc.semaphore("start_step"))

        with nc.Block() as block:
            @block.sync
            def _(sp):
                sp.dma_start(const[:, :], const_in).then_inc(start_landed, 16)
                sp.dma_start(xT[:, :, :], xT_in).then_inc(start_landed, 16)
                sp.dma_start(table[:, :], table_in).then_inc(start_landed, 16)
                sp.wait_ge(start_landed, 48)

            @block.vector
            def _(dve):
                dve.memset(ones[:, :], 1.0).then_inc(start_step, 1)
                dve.memset(eps[:, :], EPS).then_inc(start_step, 1)
                dve.wait_ge(start_step, 2)

        STEPS = [(i, g, rp, br) for i in range(TT) for g in range(NKV) for rp in range(2) for br in range(3)]
        CHUNKS = []
        for k, (i, g, rp, br) in enumerate(STEPS):
            for j in range(0, 1 if br == 0 else i + 1, 2):
                CHUNKS.append((k, j, 1 if br == 0 else min(2, i + 1 - j)))
        NPC = len(CHUNKS)
        SSTEPS = [(hb, br) for hb in range(2) for br in range(3)]
        NSTEP = len(STEPS)

        def chunks_of(k):
            return [(x, j, nj) for x, (kk, j, nj) in enumerate(CHUNKS) if kk == k]

        def evac_on_act(x):
            return x >= NPC or CHUNKS[x][1] > 0

        def read_out(eng, key):
            q = GROUP[key]
            eng.wait_ge(pair_free[q % 4], q // 4 + 1)

        def unit_used(eng, n):
            kind, m = UNITS[n]
            if kind == "tm" and m < KC - 1:
                eng.wait_ge(tm_used, m + 1)
            elif kind == "w1":
                eng.wait_ge(w1_used, m + 1)
            elif UNITS[n] in SPLIT:
                eng.wait_ge(wl_ready, SPLIT[UNITS[n]] + 1)
            else:
                group = {"tm": ("tm", TT), "ab": ("b", m)}.get(kind, (kind, m))
                eng.wait_ge(pair_done, GROUP[group] + 1)

        def split_used(eng, n):
            kind, m = SPLITS[n]
            if kind != "dn":
                eng.wait_ge(pair_done, GROUP[SPLITS[n]] + 1)
            else:
                f, u = divmod(m, NFH)
                if u < NFH - 1:
                    eng.wait_ge(dn_used, f * (NFH - 1) + u + 1)
                else:
                    eng.wait_ge(pair_done, GROUP[("dn", f * KC + KC - 1)] + 1)

        def late_events():
            for m in range(KC):
                yield from (("unit", ("ga", m)), ("group", ("ga", m)), ("unit", ("gb", m)), ("group", ("gb", m)),
                            ("group", ("a", m)), ("group", ("b", m)))
            for m in range(KC):
                yield from (("unit", ("out", m)), ("group", ("out", m)))
            for f in range(2):
                for m in range(f * NFH, (f + 1) * NFH):
                    for w in ("fg", "fu"):
                        yield from (("unit", (w, m)), ("group", (w, m)))
                for c in range(KC * NFH):
                    if c % 8 == 0:
                        yield "unit", ("dn", f * NFH + c // 8)
                    if c % NFH == NFH - 1:
                        yield "group", ("dn", f * KC + c // NFH)

        with nc.Fori(0, DEPTH) as layer:
            with nc.Block() as block:
                @block.sync
                def _(sp):
                    sp.dma_start(small[:, :], small_in[bass.ds(layer, 1)].rearrange("l p n -> (l p) n")).then_inc(small_landed, 16)

                    def unit(n):
                        if n >= RING:
                            unit_used(sp, n - RING)
                        sp.dma_start(ring[:, n % RING, :],
                                     W_in[bass.ds(layer, 1), n].rearrange("l p n -> (l p) n")).then_inc(unit_landed[n % RING], 16)

                    for n in range(len(UNITS)):
                        unit(n)
                    sp.wait_ge(stored, 32)
                    sp.wait_ge(u_stored, 16)
                    sp.wait_ge(mix_stored, 32)
                    sp.wait_ge(cstored, 16 * MH)
                    sp.wait_ge(raw_stored, 32)
                    sp.wait_ge(nsa_stored, 48)

                @block.gpsimd
                def _(pool):
                    pool.dma_start(oldwin_out[bass.ds(layer, 1)].rearrange("l b n -> (l b) n"),
                                   cwin_in[bass.ds(layer, 1)].rearrange("l b n -> (l b) n")[:, DECT * 2 * P:PAST * 2 * P]).then_inc(stored, 16)

                    def load_c0(h):
                        pool.dma_start(Cst[:, h % 2, :, :].rearrange("p b e -> p (b e)"),
                                       c0_in[bass.ds(layer, 1), h].rearrange("l p n -> (l p) n")).then_inc(c0_landed[h % 2], 16)

                    load_c0(0)
                    load_c0(1)
                    pool.wait_ge(small_landed, 16)
                    pool.memset(upad[:, :, 0:CONV - 1], 0.0)
                    us = upad[:, :, CONV - 1 + SEQ:UW].rearrange("p c (b t) -> p c b t", b=DECB)
                    cs = sml("cs", "p (c b t) -> p c b t", c=4, b=DECB)
                    for c in range(4):
                        last = pool.tensor_copy(us[:, c, :, 0:CONV - 1], cs[:, c])
                    last.then_inc(history_ready, 1)
                    pool.wait_ge(history_ready, 1)
                    for m in range(4):
                        read_out(pool, ("u", m))
                    pool.dma_start(u_out[bass.ds(layer, 1)].rearrange("l p c n -> (l p) c n"), upad[:, :, SEQ:UW]).then_inc(u_stored, 16)
                    pool.wait_ge(rows_ready, 1)
                    pool.dma_start(m_out[bass.ds(layer, 1)].rearrange("l p n -> (l p) n"), row(M_)).then_inc(mix_stored, 16)
                    for h in range(MH):
                        pool.wait_ge(head_fin, h + 1)
                        pool.dma_start(sC_out[bass.ds(layer, 1), h].rearrange("l p n -> (l p) n"),
                                       Cst[:, h % 2, :, :].rearrange("p b e -> p (b e)")).then_inc(cstored, 16)
                        if h + 2 < MH:
                            pool.wait_ge(cstored, 16 * (h + 1))
                            load_c0(h + 2)
                    pool.wait_ge(cstored, 16 * MH)
                    pool.wait_ge(pc_ready, 1)
                    pool.wait_ge(pn_ready, 1)
                    pool.dma_start(pC_out[bass.ds(layer, 1)].rearrange("l p n -> (l p) n"),
                                   pCs.rearrange("p h e -> p (h e)")).then_inc(mix_stored, 16)
                    pool.dma_start(pn_out[bass.ds(layer, 1)].rearrange("l p n -> (l p) n"),
                                   nstat[:, :, :].rearrange("p h b -> p (h b)")).then_inc(stored, 16)
                    pool.wait_ge(mix_stored, 32)
                    pool.wait_ge(ha_ready, MH)
                    pes = sml("pe", "p (v h l) -> p v l h", v=2, h=2)
                    for v in range(2):
                        last = pool.tensor_copy(raw[:, v, :, NBLK:NBLK + 2], pes[:, v])
                    last.then_inc(raw_ready, 1)

                    def arrange(n):
                        pool.wait_ge(page_landed[n % 4], 16 * (n // 4 + 1))
                        at = (SEQ + n * PAGE) // STRIDE
                        for v in range(2):
                            last = pool.tensor_copy(raw[:, v, :, at:at + PAGE // STRIDE].rearrange("p l n -> p n l"),
                                                    stage[:, n % 4, v, :].rearrange("p (n l) -> p n l", l=STRIDE))
                        last.then_inc(raw_ready, 1)

                    for n in range(DECB * NPG):
                        if n >= 4:
                            arrange(n - 4)
                            pool.wait_ge(raw_ready, n - 2)
                        b, j = divmod(n, NPG)
                        page = pool.value_load(table[0:1, n:n + 1], min_val=0, max_val=pages_in.shape[1] - 1)
                        src = pages_in[bass.ds(layer, 1), bass.ds(page, 1)].rearrange("l a p n -> (l a p) n")
                        pool.dma_start(stage[:, n % 4, :, :], src[:, 0:2 * PAGE].rearrange("p (v s) -> p v s", v=2)).then_inc(page_landed[n % 4], 16)
                        pool.dma_start(selp[:, b, j, :, :],
                                       src[:, 2 * PAGE:4 * PAGE].rearrange("p (v s) -> p v s", v=2)).then_inc(sel_landed, 16)
                    for n in range(DECB * NPG - 4, DECB * NPG):
                        arrange(n)
                    pool.memset(qb[:, :, :, :], 0.0).then_inc(pool_step, 1)
                    pool.wait_ge(w1_used, 8)
                    pool.wait_ge(rope_ready, 6)
                    pool.dma_start(raw_out[bass.ds(layer, 1)].rearrange("l p v i n -> (l p) (v i) n"),
                                   raw[:, :, :, 0:PBLK].rearrange("p v l n -> p (v l) n")).then_inc(raw_stored, 16)
                    pool.dma_start(knew_out[bass.ds(layer, 1)].rearrange("l p v n -> (l p) v n"), knew).then_inc(raw_stored, 16)
                    pool.wait_ge(raw_stored, 32)
                    pool.dma_start(winp, win_in[bass.ds(layer, 1)].rearrange("l p (b v j s) -> (l p) b v j s", b=DECB, v=2, j=NPG)).then_inc(win_landed, 16)
                    pool.dma_start(fm_out[bass.ds(layer, 1)].rearrange("l p v n -> (l p) v n"), kT).then_inc(nsa_stored, 16)
                    tmo = tm_out[bass.ds(layer, 1)].rearrange("l p i n -> (l p) i n")
                    pool.dma_start(tmo[:, 0:TT, :], vkv[:, 0:TT, :]).then_inc(nsa_stored, 16)
                    pool.dma_start(tmo[0:NS, TT, :], vkv[0:NS, TT, :]).then_inc(nsa_stored, 16)
                    pool.wait_ge(stored, 32)
                    pool.wait_ge(nsa_stored, 48)
                    pool.wait_ge(win_landed, 16)
                    pool.wait_ge(sel_landed, 16 * DECB * NPG)
                    pool.dma_reset()

                @block.tensor
                def _(pe):
                    def landed(key):
                        n = UNIT[key]
                        pe.wait_ge(unit_landed[n % RING], 16 * (n // RING + 1))
                        return ring[:, n % RING, :]

                    def begin(key):
                        q = GROUP[key]
                        if q >= 4:
                            pe.wait_ge(pair_free[q % 4], q // 4)
                        return pair(q)

                    def drained(q):
                        for s in range(4):
                            pe.wait_ge(pair_free[s], (q - s + 3) // 4)

                    def product(key, unit_key, src, kcs, first=0, ready=None):
                        w = landed(unit_key).rearrange("p (k m) -> p k m", m=P)
                        out = begin(key)
                        for k in range(kcs):
                            if ready is not None:
                                pe.wait_ge(ready[0], ready[1] + k + 1)
                            for a in range(2):
                                mm = pe.matmul(out[:, a, :], w[:, first + k, :], src[:, k, a * NHALF:(a + 1) * NHALF],
                                               start=(k == 0), stop=(k == kcs - 1))
                        return mm

                    def norm_sum(key, base):
                        out = begin(key)
                        pe.wait_ge(sq_used, base + KC - 1)
                        for a in range(2):
                            mm = pe.matmul(out[:, a, :], ones[:, :], acc[:, a * NHALF:(a + 1) * NHALF], start=True, stop=True)
                        mm.then_inc(pair_done, 1)

                    def product3(key, unit_key, hi, lo, ready=None):
                        n = SPLIT[unit_key]
                        pe.wait_ge(wl_ready, n + 1)
                        out = begin(key)
                        for k in range(KC):
                            if ready is not None:
                                pe.wait_ge(ready[0], ready[1] + k + 1)
                            mm = passes(out, n % SRING, k, hi[:, k, :], lo[:, k, :], k == 0, k == KC - 1)
                        return mm

                    def passes(out, slot, k, hi, lo, first, last):
                        for w, x, start, stop in ((wh, hi, first, False), (wh, lo, False, False), (wl, hi, False, last)):
                            for a in range(2):
                                mm = pe.matmul(out[:, a, :], w[:, slot, k * P:(k + 1) * P], x[:, a * NHALF:(a + 1) * NHALF],
                                               start=start, stop=stop)
                        return mm

                    norm_sum(("n1", 0), 0)
                    for i in range(TT + 1):
                        rows = P if i < TT else NS
                        q = GROUP[("tm", i)]
                        begin(("tm", i))
                        s = 2 * (q % 4)
                        for k in range(KC):
                            if i == 0:
                                pe.wait_ge(h_ready, k + 1)
                            w = landed(("tm", k))
                            x = hT[:, k, i * P:i * P + rows]
                            pe.matmul(ps[0:rows, s, :], x, w[:, 0:512], start=(k == 0), stop=(k == KC - 1))
                            mm = pe.matmul(ps[0:rows, s + 1, 0:280], x, w[:, 512:TMC], start=(k == 0), stop=(k == KC - 1))
                            if i == TT and k < KC - 1:
                                mm.then_inc(tm_used, 1)
                        mm.then_inc(pair_done, 1)

                    def fm(kind, m, src=hT, kcs=KC):
                        product((kind, m), (kind, m), src, kcs).then_inc(pair_done, 1)

                    for m in range(4):
                        fm("u", m)
                    w = landed(("if", 0)).rearrange("p (k m) -> p k m", k=KC)
                    out = begin(("if", 0))
                    for k in range(KC):
                        for a in range(2):
                            mm = pe.matmul(out[0:64, a, :], w[:, k, 0:64], hT[:, k, a * NHALF:(a + 1) * NHALF],
                                           start=(k == 0), stop=(k == KC - 1))
                    mm.then_inc(pair_done, 1)
                    for m in range(4):
                        fm("o", m)
                    pe.wait_ge(small_landed, 16)
                    for h in range(MH):
                        for name in ("mq", "mk"):
                            w = sml("w" + name, "p (h m) -> p h m", h=MH)[:, h, :]
                            out = begin((name, h))
                            pe.wait_ge(c_ready, h + 1)
                            for a in range(2):
                                mm = pe.matmul(out[:, a, :], w, cT[:, h, a * NHALF:(a + 1) * NHALF], start=True, stop=True)
                            mm.then_inc(pair_done, 1)
                    begin(("aw", 0))
                    s = 2 * (GROUP[("aw", 0)] % 4)
                    aw = ps[:, s, 0:(TT + 1) * 2 * MH].rearrange("p (i a h) -> p i a h", i=TT + 1, a=2)
                    pe.wait_ge(wexp_ready, 1)
                    for i in range(TT + 1):
                        rows = P if i < TT else NS
                        for a, r in enumerate((A_, W_)):
                            mm = pe.transpose(aw[0:rows, i, a, :], row(r)[:, i * P:i * P + rows], ident[0:MH, 0:MH])
                    mm.then_inc(pair_done, 1)
                    for i in range(TT + 1):
                        rows = P if i < TT else NS
                        begin(("kw", i))
                        s = 2 * (GROUP[("kw", i)] % 4)
                        wk = sml("wmk", "p (h m) -> p h m", h=MH)
                        for h in range(MH):
                            mm = pe.matmul(ps[0:rows, s, h * MD:(h + 1) * MD], cT[:, h, i * P:i * P + rows], wk[:, h, :],
                                           start=True, stop=True)
                        mm.then_inc(pair_done, 1)
                    drained(CORE_AT)

                    def spread(h, which):
                        x = 2 * h + which
                        if x >= 1:
                            pe.wait_ge(bc_ready, x)
                        r = row(G_) if which == 0 else row(EN_)
                        for a in range(2):
                            mm = pe.matmul(ps[:, 6 + a, 0:NHALF], sel4[0:MH, h, :], r[:, a * NHALF:(a + 1) * NHALF],
                                           start=True, stop=True)
                        if which == 1:
                            mm = pe.matmul(ps[:, 6, NHALF:NHALF + NS], sel4[0:MH, h, :], introw, start=True, stop=True)
                        mm.then_inc(bc_done, 1)

                    def scores(k):
                        h, j = divmod(k, TT + 1)
                        if k >= 2:
                            pe.wait_ge(st_ready, k - 1)
                        if j < TT:
                            mm = pe.matmul(ps[:, k % 2, 0:SEQ - j * P], km[:, h, j * P:(j + 1) * P], qm[:, h, j * P:SEQ],
                                           start=True, stop=True)
                        else:
                            mm = pe.matmul(ps[0:NS, k % 2, 0:NS], km[:, h, SEQ:N], qm[:, h, SEQ:N], start=True, stop=True)
                        mm.then_inc(ms_done, 1)

                    def numden(k):
                        h, j = divmod(k, TT + 1)
                        if j == 0 and h >= 1:
                            pe.wait_ge(num_read, h)
                        pe.wait_ge(st_ready, k + 1)
                        if j < TT:
                            s = St[:, k % 2, 0:SEQ - j * P]
                            pe.matmul(ps[:, 2, j * P:SEQ], vtm[:, j, h * MD:(h + 1) * MD], s, start=(j == 0), stop=(j == TT - 1))
                            mm = pe.matmul(ps[:, 3, j * P:SEQ], ones[:, :], s, start=(j == 0), stop=(j == TT - 1))
                        else:
                            s = St[0:NS, k % 2, 0:NS]
                            pe.matmul(ps[:, 4, 0:NS], vtm[0:NS, TT, h * MD:(h + 1) * MD], s, start=True, stop=False)
                            pe.wait_ge(qi_ready, h + 1)
                            pe.wait_ge(c0_landed[h % 2], 16 * (h // 2 + 1))
                            for b in range(DECB):
                                pe.matmul(ps[:, 4, b * DECT:(b + 1) * DECT], Cst[:, h % 2, b, :], qi[:, 0, b * DECT:(b + 1) * DECT],
                                          start=False, stop=(b == DECB - 1))
                            pe.matmul(ps[:, 4, NS:2 * NS], ones[0:NS, :], s, start=True, stop=False)
                            mm = pe.matmul(ps[:, 4, NS:2 * NS], ones[:, :], qi[:, 1, :], start=False, stop=True)
                        mm.then_inc(nd_done, 1)

                    def new_state(h):
                        pe.wait_ge(vb_ready, h + 1)
                        pe.wait_ge(bc_ready, min(2 * h + 4, 2 * MH))
                        k = kw[0:NS, TT, h * MD:(h + 1) * MD]
                        for a in range(2):
                            pe.matmul(ps[:, 6 + a, :], k, vb[0:NS, 4 * a:4 * a + 4, :], start=True, stop=True)
                        mm = pe.matmul(ps[:, 5, 0:DECB], k, con("blk")[0:NS, :], start=True, stop=True)
                        mm.then_inc(cs_done, 1)

                    nk = MH * (TT + 1)
                    spread(0, 0)
                    spread(0, 1)
                    scores(0)
                    for k in range(nk):
                        h, j = divmod(k, TT + 1)
                        if k + 1 < nk:
                            scores(k + 1)
                        if j == 0 and h + 1 < MH:
                            if h >= 1:
                                pe.wait_ge(head_fin, h)
                            spread(h + 1, 0)
                            spread(h + 1, 1)
                        numden(k)
                        if j == TT:
                            new_state(h)
                    pe.wait_ge(st_ready, nk)
                    for h in range(MH):
                        for what in range(2):
                            for i in range(TT):
                                k = kw[:, i, h * MD:(h + 1) * MD]
                                if what == 0:
                                    mm = pe.matmul(ps[:, 0, h * MD:(h + 1) * MD], k, vtm[:, i, h * MD:(h + 1) * MD],
                                                   start=(i == 0), stop=(i == TT - 1))
                                else:
                                    mm = pe.matmul(ps[:, 1, h:h + 1], k, ones[:, 0:1], start=(i == 0), stop=(i == TT - 1))
                    mm.then_inc(pc_done, 1)
                    pe.wait_ge(head_fin, MH)
                    pe.wait_ge(pc_ready, 1)
                    pe.wait_ge(pn_ready, 1)
                    for h in range(MH):
                        q = GROUP[("mn", h)]
                        begin(("mn", h))
                        pe.wait_ge(msq_ready, h + 1)
                        for a in range(2):
                            mm = pe.matmul(pair(q)[:, a, :], ones[:, :], sq[:, h % 2, a * NHALF:(a + 1) * NHALF], start=True, stop=True)
                        mm.then_inc(pair_done, 1)
                    for m in range(4):
                        fm("q", m)
                    for m in range(4):
                        fm("k", m)
                    for n in range(6):
                        out = begin(("rope", n))
                        src = qT[:, n, :] if n < 4 else kT[:, n - 4, :]
                        read_out(pe, ("q", n) if n < 4 else ("k", n - 2))
                        for a in range(2):
                            mm = pe.matmul(out[:, a, :], rot, src[:, a * NHALF:(a + 1) * NHALF], start=True, stop=True)
                        mm.then_inc(pair_done, 1)
                    drained(ATTN_AT)
                    pe.wait_ge(raw_ready, DECB * NPG + 1)
                    for v in range(2):
                        for u in range(4):
                            w = landed(("w1", 4 * v + u)).rearrange("p (l e) -> p l e", e=HID)
                            for l8 in range(8):
                                l = 8 * u + l8
                                second, l16 = divmod(l, STRIDE)
                                for g in range(NKV):
                                    x = raw[g * HD:(g + 1) * HD, v, l16, second:second + NBLK + 1]
                                    mm = pe.matmul(ps[:, 3 * v + g, 0:NBLK + 1], w[g * HD:(g + 1) * HD, l8, :], x, start=(l == 0), stop=(l == CLEN - 1))
                            mm.then_inc(w1_used, 1)
                    w2 = sml("w2", "p (v f) -> p v f", v=2)
                    pe.wait_ge(hid_ready, 1)
                    for g in range(NKV):
                        pe.matmul(ps[g * HD:(g + 1) * HD, 6, 0:NBLK], w2[:, 0, :], hid[:, 0, g, :], start=True, stop=True)
                    pe.wait_ge(hid_ready, 2)
                    for g in range(NKV):
                        pe.matmul(ps[0:NCP, 7, g * HD:(g + 1) * HD], hid[:, 1, g, 0:NCP], w2[:, 1, :], start=True, stop=True)
                        mm = pe.matmul(ps[:, 7, P + g * HD:P + (g + 1) * HD], hid[:, 1, g, PBLK:NBLK], w2[:, 1, :], start=True, stop=True)
                    mm.then_inc(cmp_done, 1)
                    pe.wait_ge(cmp_ready, 1)

                    def att_scores(k):
                        i, g, rp, br = STEPS[k]
                        if k >= 2:
                            pe.wait_ge(exp_done, k - 1)
                        src = qT if br == 0 else qrT
                        keys = kcT[g * HD:(g + 1) * HD, 0:NCP] if br == 0 else kT[g * HD:(g + 1) * HD, br - 1, 0:(i + 1) * P]
                        width = NCP if br == 0 else (i + 1) * P
                        for r in range(2):
                            mm = pe.matmul(ps[:, 2 * (k % 2) + r, 0:width], src[g * HD:(g + 1) * HD, 2 * rp + r, i * P:(i + 1) * P], keys,
                                           start=True, stop=True)
                        mm.then_inc(s_done, 1)

                    def att_turn(k):
                        i, g, rp, br = STEPS[k]
                        pe.wait_ge(d_ready, k + 1)
                        for x, j0, nj in chunks_of(k):
                            if x >= 2:
                                pe.wait_ge(t_free[x % 2], x // 2)
                            rows = NCP if br == 0 else P
                            for j in range(j0, j0 + nj):
                                for r in range(2):
                                    at = ((j - j0) * 2 + r) * P
                                    mm = pe.matmul(ps[0:rows, 4 + x % 2, at:at + P], Pt[:, k % 2, r, j * P:j * P + rows], Dg[:, k % 2, r, :],
                                                   start=True, stop=True)
                            mm.then_inc(t_done, 1)

                    def att_out(k):
                        i, g, rp, br = STEPS[k]
                        w = k // 3
                        if br == 0 and w >= 2:
                            pe.wait_ge(hb_ready, w - 1)
                        out = ps[g * HD:(g + 1) * HD, 6 + w % 2, 0:2 * P]
                        for x, j0, nj in chunks_of(k):
                            pe.wait_ge(t_free[x % 2], x // 2 + 1)
                            for j in range(j0, j0 + nj):
                                c = (j - j0) * 2 * P
                                if br == 0:
                                    mm = pe.matmul(out, vcp[0:NCP, g * HD:(g + 1) * HD], PT[0:NCP, x % 2, 0:2 * P], start=True, stop=False)
                                else:
                                    mm = pe.matmul(out, vkv[:, j, (br - 1) * P + g * HD:(br - 1) * P + (g + 1) * HD], PT[:, x % 2, c:c + 2 * P],
                                                   start=False, stop=(br == 2 and j == i))
                            mm.then_inc(o_done, 1)

                    att_scores(0)
                    pe.wait_ge(rope_ready, 6)
                    for k in range(NSTEP):
                        if k + 1 < NSTEP:
                            att_scores(k + 1)
                        att_turn(k)
                        att_out(k)
                    pe.wait_ge(hb_ready, NSTEP // 3)
                    pe.wait_ge(exp_done, NSTEP)
                    for hb in range(2):
                        mm = pe.matmul(ps[:, 3, hb * 24:(hb + 1) * 24], tsel[0:NS, hb, :], gate[0:NS, TT, :], start=True, stop=True)
                    mm.then_inc(gs_done, 1)
                    pe.wait_ge(qb_ready, 1)
                    pe.wait_ge(sel_landed, 16 * DECB * NPG)

                    def samp_scores(m):
                        hb, br = SSTEPS[m]
                        if m >= 2:
                            pe.wait_ge(exp_done, NSTEP + m - 1)
                        if br == 2:
                            pe.wait_ge(win_landed, 16)
                        for b4 in range(4):
                            b = 4 * hb + b4
                            o = ps[32 * b4:32 * b4 + 32, m % 2, :]
                            if br == 0:
                                mm = pe.matmul(o[:, 0:P], qb[:, 0, b, :], kcT[:, PBLK:NBLK], start=True, stop=True)
                            else:
                                past = selp[:, b, :, 0, :] if br == 1 else winp[:, b, 0, :, :]
                                pe.matmul(o[:, 0:PAST], qb[:, 1, b, :], past, start=True, stop=True)
                                mm = pe.matmul(o[:, PAST:PAST + NS], qb[:, 1, b, :], kT[:, br - 1, SEQ:N], start=True, stop=True)
                        mm.then_inc(s_done, 1)

                    def samp_turn(m):
                        hb, br = SSTEPS[m]
                        x = NPC + m
                        pe.wait_ge(d_ready, NSTEP + m + 1)
                        pe.wait_ge(t_free[x % 2], x // 2)
                        for j in range(1 if br == 0 else 3):
                            rows = NS if j == 2 else P
                            mm = pe.matmul(ps[0:rows, 4 + x % 2, j * P:(j + 1) * P], Pt[:, m % 2, 0, j * P:j * P + rows], Dg[:, m % 2, 0, :],
                                           start=True, stop=True)
                        mm.then_inc(t_done, 1)

                    def samp_out(m):
                        hb, br = SSTEPS[m]
                        x = NPC + m
                        pe.wait_ge(t_free[x % 2], x // 2 + 1)
                        bank = 6 + hb
                        if br == 0:
                            mm = pe.matmul(ps[:, bank, 0:P], vcs, PT[:, x % 2, 0:P], start=True, stop=False)
                        else:
                            pe.matmul(ps[:, bank, 0:P], vkv[0:NS, TT, (br - 1) * P:br * P], PT[0:NS, x % 2, 2 * P:3 * P], start=False, stop=False)
                            for b4 in range(4):
                                b = 4 * hb + b4
                                for j in range(NPG):
                                    v = selp[:, b, j, 1, :] if br == 1 else winp[:, b, 1, j, :]
                                    mm = pe.matmul(ps[:, bank, 32 * b4:32 * b4 + 32], v, PT[:, x % 2, j * P + 32 * b4:j * P + 32 * b4 + 32],
                                                   start=False, stop=(br == 2 and j == NPG - 1 and b4 == 3))
                        mm.then_inc(o_done, 1)

                    samp_scores(0)
                    for m in range(6):
                        if m + 1 < 6:
                            samp_scores(m + 1)
                        samp_turn(m)
                        samp_out(m)
                    pe.wait_ge(exp_done, NSTEP + 6)
                    pe.wait_ge(hb_ready, NSTEP // 3 + 2)
                    for m in range(KC):
                        product3(("ga", m), ("ga", m), xh, xl, (xl_ready, 0)).then_inc(pair_done, 1)
                        product3(("gb", m), ("gb", m), xh, xl).then_inc(pair_done, 1)
                        product(("a", m), ("ab", m), haT, 4).then_inc(pair_done, 1)
                        product(("b", m), ("ab", m), hbT, 4, first=4).then_inc(pair_done, 1)
                    for m in range(KC):
                        product3(("out", m), ("out", m), mh, ml, (merged_ready, 0)).then_inc(pair_done, 1)
                    norm_sum(("n2", 0), KC - 1)
                    for f in range(2):
                        for m in range(f * NFH, (f + 1) * NFH):
                            for w in ("fg", "fu"):
                                product3((w, m), (w, m), xh, xl, (xl_ready, KC)).then_inc(pair_done, 1)
                        for m in range(KC):
                            out = begin(("dn", f * KC + m))
                            for k in range(NFH):
                                u, c = divmod(m * NFH + k, 8)
                                n = SPLIT[("dn", f * NFH + u)]
                                pe.wait_ge(wl_ready, n + 1)
                                pe.wait_ge(act_ready, f * NFH + k + 1)
                                mm = passes(out, n % SRING, c, ah[:, k, :], al[:, k, :], k == 0, k == NFH - 1)
                                if c == 7 and u < NFH - 1:
                                    mm.then_inc(dn_used, 1)
                            mm.then_inc(pair_done, 1)

                @block.scalar
                def _(act):
                    steps = [0]

                    def link(ins):
                        steps[0] += 1
                        ins.then_inc(act_step, 1)
                        act.wait_ge(act_step, steps[0])

                    def done(key):
                        q = GROUP[key]
                        act.wait_ge(pair_done, q + 1)
                        return pair(q), pair_free[q % 4]

                    def square(k, base):
                        if k == 0:
                            act.activation(acc[:, :], xT[:, 0, :], ACT.Square).then_inc(sq_ready, 1)
                            return
                        if k >= 3:
                            act.wait_ge(sq_used, base + k - 2)
                        act.activation(sq[:, k % 2, :], xT[:, k, :], ACT.Square).then_inc(sq_ready, 1)

                    def split_high(n):
                        if n >= len(SPLITS):
                            return
                        if n >= SRING:
                            split_used(act, n - SRING)
                        u = UNIT[SPLITS[n]]
                        act.wait_ge(unit_landed[u % RING], 16 * (u // RING + 1))
                        act.copy(wh[:, n % SRING, :], ring[:, u % RING, :]).then_inc(wh_ready, 1)

                    def root(key):
                        out, free = done(key)
                        act.activation(halves(rstd[:, :]), out, ACT.Sqrt, bias=eps[:, :], scale=1.0 / D).then_inc(free, 1)

                    for k in range(KC):
                        square(k, 0)
                    root(("n1", 0))
                    for i in range(TT + 1):
                        rows = P if i < TT else NS
                        done(("tm", i))
                        q = GROUP[("tm", i)]
                        s = 2 * (q % 4)
                        act.activation(gate[0:rows, i, :], ps[0:rows, s + 1, 2 * P:2 * P + 24], ACT.Sigmoid)
                        act.copy(vkv[0:rows, i, :], ps[0:rows, s + 1, 0:2 * P])
                        act.copy(vtm[0:rows, i, :], ps[0:rows, s, :]).then_inc(pair_free[q % 4], 1)
                    for m in range(4):
                        out, free = done(("u", m))
                        act.copy(upad[:, m, 3:3 + NHALF], out[:, 0, :])
                        act.copy(upad[:, m, 3 + NHALF:3 + SEQ], out[:, 1, 0:SEQ - NHALF])
                        us = upad[:, m, 3 + SEQ:UW].rearrange("p (b t) -> p b t", b=DECB)
                        act.copy(us[:, :, 3:7], out[:, 1, SEQ - NHALF:NHALF].rearrange("p (b t) -> p b t", b=DECB)).then_inc(free, 1)
                    out, free = done(("if", 0))
                    act.wait_ge(small_landed, 16)
                    act.activation(halves(row(I_)), out[0:MH], ACT.Identity, bias=sml("bi")[0:MH, :])
                    act.copy(halves(row(A_)), out[32:32 + MH]).then_inc(free, 1)
                    read_out(act, ("if", 0))
                    link(act.activation(row(Z_), row(A_), ACT.Identity, bias=sml("bf")[0:MH, :]))
                    link(act.activation(row(L_), row(Z_), ACT.Abs))
                    link(act.activation(row(A_), row(L_), ACT.Exp, scale=-1.0))
                    act.activation(row(L_), row(A_), ACT.Ln, bias=ones[0:MH, 0:1]).then_inc(ln_ready, 1)
                    for m in range(4):
                        act.wait_ge(conv_ready, m + 1)
                        act.activation(cT[:, m, :], ctmp[:, m % 2, :], ACT.Silu).then_inc(c_ready, 1)
                    for m in range(4):
                        out, free = done(("o", m))
                        act.activation(halves(haT[:, m, :]), out, ACT.Sigmoid).then_inc(free, 1)
                    act.wait_ge(rows_ready, 1)
                    act.activation(row(W_)[:, 0:SEQ], row(A_)[:, 0:SEQ], ACT.Exp, bias=row(G_)[:, SEQ - 1:SEQ])
                    act.activation(row(W_)[:, SEQ:N], tmprow, ACT.Exp)
                    act.activation(row(EN_), row(M_), ACT.Exp, scale=-1.0)
                    act.activation(introw, introw, ACT.Exp).then_inc(wexp_ready, 1)
                    for h in range(MH):
                        for name, dst, scale in (("mq", qm, 1.0), ("mk", km, MD ** -0.5)):
                            out, free = done((name, h))
                            act.activation(halves(dst[:, h, :]), out, ACT.Copy, scale=scale).then_inc(free, 1)
                    act.wait_ge(pair_done, CORE_AT)
                    act.wait_ge(u_stored, 16)
                    read_out(act, ("aw", 0))

                    def spread(h):
                        if h >= 2:
                            act.wait_ge(head_fin, h - 1)
                        act.wait_ge(bc_done, 2 * h + 1)
                        act.copy(halves(gbc[:, h % 2, :]), ps[:, 6:8, 0:NHALF]).then_inc(bc_ready, 1)
                        act.wait_ge(bc_done, 2 * h + 2)
                        act.copy(inter[:, h % 2, :], ps[:, 6, NHALF:NHALF + NS])
                        act.copy(halves(enm[:, h % 2, :]), ps[:, 6:8, 0:NHALF]).then_inc(bc_ready, 1)

                    spread(0)
                    for k in range(MH * (TT + 1)):
                        h, j = divmod(k, TT + 1)
                        if j == 1 and h + 1 < MH:
                            spread(h + 1)
                        if k >= 2:
                            act.wait_ge(st_ready, k - 1)
                        act.wait_ge(gm_ready, k + 1)
                        if j < TT:
                            if j < TT - 1:
                                act.wait_ge(bc_ready, 2 * h + 1)
                                act.activation(Et[:, k % 2, P:SEQ - j * P], gbc[:, h % 2, (j + 1) * P:SEQ], ACT.Exp, bias=awt[:, j, 0, h:h + 1])
                            act.activation(Et[:, k % 2, 0:P], gmask, ACT.Exp, bias=awt[:, j, 0, h:h + 1]).then_inc(e_ready, 1)
                        else:
                            act.activation(Et[0:NS, k % 2, 0:NS], gmask[0:NS, 0:NS], ACT.Exp, bias=awt[0:NS, j, 0, h:h + 1]).then_inc(e_ready, 1)
                    act.wait_ge(pc_done, 1)
                    act.copy(pCs, ps[:, 0, :].rearrange("p (h e) -> p h e", h=MH)).then_inc(pc_ready, 1)
                    for h in range(MH):
                        if h >= 2:
                            act.wait_ge(pair_done, GROUP[("mn", h - 2)] + 1)
                        act.wait_ge(num_read, h + 1)
                        act.activation(sq[:, h % 2, :], qm[:, h, :], ACT.Square).then_inc(msq_ready, 1)
                    for h in range(MH):
                        out, free = done(("mn", h))
                        if h >= 1:
                            act.wait_ge(ha_ready, h)
                        act.activation(halves(rstd[:, :]), out, ACT.Sqrt, bias=eps[:, :], scale=1.0 / MD).then_inc(free, 1)
                    act.wait_ge(ha_ready, MH)
                    act.wait_ge(mix_stored, 32)
                    act.wait_ge(cstored, 16 * MH)
                    for m in range(4):
                        out, free = done(("q", m))
                        act.activation(halves(qT[:, m, :]), out, ACT.Copy, scale=HD ** -0.5).then_inc(free, 1)
                    for m in range(4):
                        out, free = done(("k", m))
                        if m < 2:
                            chunks = raw[:, m, :, :].rearrange("p l n -> p n l")
                            act.copy(chunks[:, 0:NHALF // STRIDE, :], out[:, 0, :].rearrange("p (n l) -> p n l", l=STRIDE))
                            act.copy(chunks[:, NHALF // STRIDE:PBLK, :], out[:, 1, 0:SEQ - NHALF].rearrange("p (n l) -> p n l", l=STRIDE))
                            act.copy(knew[:, m, :], out[:, 1, SEQ - NHALF:NHALF]).then_inc(free, 1)
                        else:
                            act.copy(halves(kT[:, m - 2, :]), out).then_inc(free, 1)
                    for v in range(2):
                        act.wait_ge(w1_used, 4 * (v + 1))
                        link(act.copy(hbias[:, v:v + 1], ps[:, 3 * v, NBLK:NBLK + 1]))
                        for g in range(NKV):
                            ins = act.activation(hid[:, v, g, :], ps[:, 3 * v + g, 0:NBLK], ACT.Gelu_apprx_tanh, bias=hbias[:, v:v + 1])
                        ins.then_inc(hid_ready, 1)
                    act.wait_ge(cmp_done, 1)
                    act.copy(kcT, ps[:, 6, 0:NBLK])
                    act.copy(vcp[0:NCP, :], ps[0:NCP, 7, 0:P])
                    act.copy(vcs, ps[:, 7, P:2 * P]).then_inc(cmp_ready, 1)

                    def att_exp(k):
                        i, g, rp, br = STEPS[k]
                        act.wait_ge(max_ready, k + 1)
                        if k >= 2:
                            act.wait_ge(t_done, chunks_of(k - 2)[-1][0] + 1)
                        width = NCP if br == 0 else (i + 1) * P
                        for r in range(2):
                            ins = act.activation(Pt[:, k % 2, r, 0:width], ps[:, 2 * (k % 2) + r, 0:width], ACT.Exp,
                                                 bias=stat[:, k % 2, r:r + 1],
                                                 accum_out=None if br == 0 else stat[:, 2 + k % 2, r:r + 1])
                        ins.then_inc(exp_done, 1)

                    def evac(x, rows, cols):
                        act.wait_ge(t_done, x + 1)
                        if x >= 2:
                            act.wait_ge(o_done, x - 1)
                        act.copy(PT[0:rows, x % 2, 0:cols], ps[0:rows, 4 + x % 2, 0:cols]).then_inc(t_free[x % 2], 1)

                    att_exp(0)
                    for k in range(NSTEP):
                        i, g, rp, br = STEPS[k]
                        if k + 1 < NSTEP:
                            att_exp(k + 1)
                        for x, j0, nj in chunks_of(k):
                            if evac_on_act(x):
                                evac(x, P, nj * 2 * P)
                        if br == 2:
                            act.wait_ge(o_done, chunks_of(k)[-1][0] + 1)
                            act.copy(hbT[g * HD:(g + 1) * HD, 2 * rp:2 * rp + 2, i * P:(i + 1) * P],
                                     ps[g * HD:(g + 1) * HD, 6 + (k // 3) % 2, 0:2 * P].rearrange("p (r t) -> p r t", r=2)).then_inc(hb_ready, 1)

                    def samp_exp(m):
                        hb, br = SSTEPS[m]
                        act.wait_ge(max_ready, NSTEP + m + 1)
                        if m >= 2:
                            act.wait_ge(t_done, NPC + m - 1)
                        else:
                            act.wait_ge(t_done, NPC)
                        width = P if br == 0 else PAST + NS
                        act.activation(Pt[:, m % 2, 0, 0:width], ps[:, m % 2, 0:width], ACT.Exp, bias=stat[:, m % 2, 0:1],
                                       accum_out=stat[:, 2 + m % 2, 0:1]).then_inc(exp_done, 1)

                    samp_exp(0)
                    for m in range(6):
                        hb, br = SSTEPS[m]
                        if m + 1 < 6:
                            samp_exp(m + 1)
                        x = NPC + m
                        if br == 0:
                            evac(x, P, P)
                        else:
                            act.wait_ge(t_done, x + 1)
                            act.wait_ge(o_done, x - 1)
                            act.copy(PT[:, x % 2, 0:2 * P], ps[:, 4 + x % 2, 0:2 * P])
                            act.copy(PT[0:NS, x % 2, 2 * P:3 * P], ps[0:NS, 4 + x % 2, 2 * P:3 * P]).then_inc(t_free[x % 2], 1)
                        if br == 2:
                            act.wait_ge(o_done, x + 1)
                            for g in range(NKV):
                                o = ps[g * HD:(g + 1) * HD, 6 + hb, 0:P].rearrange("p (b g r t) -> p b g r t", b=4, g=NKV, r=R)
                                d = hbT[g * HD:(g + 1) * HD, :, SEQ + 16 * hb:SEQ + 16 * hb + 16].rearrange("p r (b t) -> p b r t", b=4)
                                for b4 in range(4):
                                    ins = act.copy(d[:, b4], o[:, b4, g])
                            ins.then_inc(hb_ready, 1)
                    for k in range(KC):
                        if k in (0, 2, 4):
                            split_high(k // 2)
                        act.copy(xh[:, k, :], hT[:, k, :]).then_inc(xh_ready, 1)
                    for what, key in late_events():
                        name, m = key
                        if what == "unit":
                            split_high(SPLIT[key] + SRING)
                        elif name in ("ga", "gb"):
                            out, free = done(key)
                            n = 0 if name == "ga" else 1
                            if m >= 1:
                                read_out(act, (("a", "b")[n], m - 1))
                            act.activation(halves(sg[:, n, :]), out, ACT.Sigmoid).then_inc(free, 1)
                        elif name == "out":
                            read_out(act, key)
                            square(m, KC - 1)
                            if m == KC - 1:
                                root(("n2", 0))
                                for k in range(KC):
                                    act.wait_ge(t_ready, k + 1)
                                    act.copy(xh[:, k, :], tbuf[:, k % 2, :]).then_inc(th_ready, 1)
                        elif name == "fg":
                            out, free = done(key)
                            if m >= 2:
                                read_out(act, ("fu", m - 2))
                            act.activation(halves(sg[:, m % 2, :]), out, ACT.Silu).then_inc(free, 1)

                @block.vector
                def _(dve):
                    steps = [0]

                    def link(ins):
                        steps[0] += 1
                        ins.then_inc(dve_step, 1)
                        dve.wait_ge(dve_step, steps[0])

                    def done(key):
                        q = GROUP[key]
                        dve.wait_ge(pair_done, q + 1)
                        return pair(q), pair_free[q % 4]

                    def add_squares(base):
                        for k in range(1, KC):
                            dve.wait_ge(sq_ready, base + k + 1)
                            if k >= 2:
                                dve.wait_ge(sq_used, base + k - 1)
                            dve.tensor_tensor(acc[:, :], acc[:, :], sq[:, k % 2, :], ALU.add).then_inc(sq_used, 1)

                    def add_square(k):
                        dve.wait_ge(sq_ready, KC + k + 1)
                        dve.wait_ge(sq_used, KC - 1 + k - 1)
                        dve.tensor_tensor(acc[:, :], acc[:, :], sq[:, k % 2, :], ALU.add).then_inc(sq_used, 1)

                    def split_low(n):
                        if n >= len(SPLITS):
                            return
                        u = UNIT[SPLITS[n]]
                        dve.wait_ge(wh_ready, n + 1)
                        dve.tensor_tensor(wl[:, n % SRING, :], ring[:, u % RING, :], wh[:, n % SRING, :].bitcast(F32),
                                          ALU.subtract).then_inc(wl_ready, 1)

                    def split(t, hi, lo, ready):
                        link(dve.tensor_copy(hi, t))
                        dve.tensor_tensor(lo, t, hi.bitcast(F32), ALU.subtract).then_inc(ready, 1)

                    dve.wait_ge(small_landed, 16)
                    add_squares(0)
                    read_out(dve, ("n1", 0))
                    link(dve.reciprocal(rstd[:, :], rstd[:, :]))
                    for k in range(KC):
                        dve.scalar_tensor_tensor(out=hT[:, k, :], in0=xT[:, k, :], scalar=sml("n1g")[:, k:k + 1], in1=rstd[:, :],
                                                 op0=ALU.mult, op1=ALU.mult).then_inc(h_ready, 1)
                    dve.wait_ge(history_ready, 1)
                    cw = sml("cw", "p (c j) -> p c j", c=4)
                    for m in range(4):
                        read_out(dve, ("u", m))
                        if m >= 2:
                            dve.wait_ge(c_ready, m - 1)
                        us = upad[:, m, 3 + SEQ:UW].rearrange("p (b t) -> p b t", b=DECB)
                        up, dp = upad[:, m, 0:3 + SEQ], ctmp[:, m % 2, 0:SEQ]
                        dsm = ctmp[:, m % 2, SEQ:N].rearrange("p (b t) -> p b t", b=DECB)
                        dve.tensor_scalar(dp, up[:, 0:SEQ], cw[:, m, 0:1], sml("cb")[:, m:m + 1], ALU.mult, ALU.add)
                        link(dve.tensor_scalar(dsm, us[:, :, 0:DECT], cw[:, m, 0:1], sml("cb")[:, m:m + 1], ALU.mult, ALU.add))
                        for j in range(1, CONV):
                            dve.scalar_tensor_tensor(out=dp, in0=up[:, j:j + SEQ], scalar=cw[:, m, j:j + 1], in1=dp, op0=ALU.mult, op1=ALU.add)
                            ins = dve.scalar_tensor_tensor(out=dsm, in0=us[:, :, j:j + DECT], scalar=cw[:, m, j:j + 1], in1=dsm,
                                                           op0=ALU.mult, op1=ALU.add)
                            if j < CONV - 1:
                                link(ins)
                            else:
                                ins.then_inc(conv_ready, 1)
                    dve.wait_ge(ln_ready, 1)
                    lf = row(Z_)
                    link(dve.scalar_tensor_tensor(out=lf, in0=row(Z_), scalar=0.0, in1=row(L_), op0=ALU.min, op1=ALU.subtract))
                    dve.memset(row(A_), 1.0)
                    m0 = sml("m0")[0:MH, :]
                    fs, ms, ls, is_ = (per_seq(r[:, SEQ:N]) for r in (row(F_), row(M_), lf, row(I_)))
                    link(dve.tensor_tensor_scan(out=row(M_)[:, 0:SEQ], data0=lf[:, 0:SEQ], data1=row(I_)[:, 0:SEQ], initial=0.0,
                                                op0=ALU.add, op1=ALU.max))
                    dve.tensor_tensor_scan(out=row(F_)[:, 0:SEQ], data0=row(A_)[:, 0:SEQ], data1=lf[:, 0:SEQ], initial=0.0,
                                           op0=ALU.mult, op1=ALU.add)
                    for t in range(DECT):
                        link(dve.tensor_tensor(ms[:, :, t], m0 if t == 0 else ms[:, :, t - 1], ls[:, :, t], ALU.add))
                        dve.tensor_tensor(ms[:, :, t], ms[:, :, t], is_[:, :, t], ALU.max)
                        link(dve.tensor_copy(fs[:, :, t], ls[:, :, t]) if t == 0 else
                             dve.tensor_tensor(fs[:, :, t], fs[:, :, t - 1], ls[:, :, t], ALU.add))
                    dve.tensor_tensor(row(A_), row(I_), row(F_), ALU.subtract)
                    link(dve.tensor_tensor(row(G_), row(F_), row(M_), ALU.subtract))
                    gs = per_seq(row(G_)[:, SEQ:N])
                    dve.tensor_tensor(per_seq(introw), gs, bc(m0.unsqueeze(2), [MH, DECB, DECT]), ALU.add)
                    dve.tensor_tensor(per_seq(tmprow), per_seq(row(A_)[:, SEQ:N]), bc(gs[:, :, DECT - 1:DECT], [MH, DECB, DECT]),
                                      ALU.add).then_inc(rows_ready, 1)
                    q = GROUP[("aw", 0)]
                    done(("aw", 0))
                    dve.tensor_copy(awt[:, 0:TT].rearrange("p i a h -> p (i a h)"), ps[:, 2 * (q % 4), 0:TT * 2 * MH])
                    dve.tensor_copy(awt[0:NS, TT].rearrange("p a h -> p (a h)"),
                                    ps[0:NS, 2 * (q % 4), TT * 2 * MH:(TT + 1) * 2 * MH]).then_inc(pair_free[q % 4], 1)
                    read_out(dve, ("aw", 0))
                    for i in range(TT + 1):
                        rows = P if i < TT else NS
                        done(("kw", i))
                        q = GROUP[("kw", i)]
                        for h in range(MH):
                            ins = dve.tensor_scalar(kw[0:rows, i, h * MD:(h + 1) * MD], ps[0:rows, 2 * (q % 4), h * MD:(h + 1) * MD],
                                                    awt[0:rows, i, 1, h:h + 1], MD ** -0.5, ALU.mult, ALU.mult)
                        ins.then_inc(pair_free[q % 4], 1)
                    for name in ("mq", "mk"):
                        for h in range(MH):
                            read_out(dve, (name, h))

                    def masked(k):
                        h, j = divmod(k, TT + 1)
                        dve.wait_ge(bc_ready, 2 * h + 1)
                        if k >= 1:
                            dve.wait_ge(e_ready, k)
                        if j < TT:
                            dve.tensor_tensor(gmask, gbc[:, h % 2, j * P:(j + 1) * P], con("sneg"), ALU.add).then_inc(gm_ready, 1)
                        else:
                            dve.tensor_tensor(gmask[0:NS, 0:NS], gbc[0:NS, h % 2, SEQ:N], con("m32")[0:NS, :], ALU.add).then_inc(gm_ready, 1)

                    masked(0)
                    for k in range(MH * (TT + 1)):
                        h, j = divmod(k, TT + 1)
                        if j == 0:
                            if h >= 1:
                                dve.wait_ge(nd_done, h * (TT + 1))
                            dve.wait_ge(bc_ready, 2 * h + 2)
                            link(dve.tensor_tensor(qi[:, 0, :], qm[:, h, SEQ:N], inter[:, h % 2, :], ALU.mult))
                            n0 = sml("n0", "p (h b) -> p h b", h=MH)[:, h, :]
                            dve.tensor_tensor(per_seq(qi[:, 1, :]), per_seq(qi[:, 0, :]), bc(n0.unsqueeze(2), [P, DECB, DECT]),
                                              ALU.mult).then_inc(qi_ready, 1)
                        dve.wait_ge(e_ready, k + 1)
                        dve.wait_ge(ms_done, k + 1)
                        if k >= 2:
                            dve.wait_ge(nd_done, k - 1)
                        if j < TT:
                            w = SEQ - j * P
                            dve.tensor_tensor(St[:, k % 2, 0:w], ps[:, k % 2, 0:w], Et[:, k % 2, 0:w], ALU.mult).then_inc(st_ready, 1)
                        else:
                            dve.tensor_tensor(St[0:NS, k % 2, 0:NS], ps[0:NS, k % 2, 0:NS], Et[0:NS, k % 2, 0:NS], ALU.mult).then_inc(st_ready, 1)
                        if k + 1 < MH * (TT + 1):
                            masked(k + 1)
                        if j == TT:
                            if h >= 1:
                                dve.wait_ge(cs_done, h)
                            v = vtm[0:NS, TT, h * MD:(h + 1) * MD]
                            dve.tensor_tensor(vb[0:NS], bc(v.unsqueeze(1), [NS, DECB, MD]), bc(con("blk")[0:NS, :].unsqueeze(2), [NS, DECB, MD]),
                                              ALU.mult).then_inc(vb_ready, 1)
                            dve.wait_ge(nd_done, (h + 1) * (TT + 1))
                            for num, den, en, dst in ((ps[:, 2, :], ps[:, 3, :], enm[:, h % 2, 0:SEQ], qm[:, h, 0:SEQ]),
                                                      (ps[:, 4, 0:NS], ps[:, 4, NS:2 * NS], enm[:, h % 2, SEQ:N], qm[:, h, SEQ:N])):
                                link(dve.scalar_tensor_tensor(out=en, in0=den, scalar=-1.0, in1=en, op0=ALU.mult, op1=ALU.max))
                                link(dve.tensor_tensor(en, den, en, ALU.max))
                                link(dve.reciprocal(en, en))
                                ins = dve.tensor_tensor(dst, num, en, ALU.mult)
                            ins.then_inc(num_read, 1)
                            dve.wait_ge(cs_done, h + 1)
                            dec = per_seq(inter[:, h % 2, :])[:, :, DECT - 1:DECT]
                            C = Cst[:, h % 2]
                            n0 = sml("n0", "p (h b) -> p h b", h=MH)[:, h, :]
                            dve.tensor_tensor(C, C, bc(dec, [P, DECB, MD]), ALU.mult)
                            link(dve.tensor_tensor(nstat[:, h, 1:1 + DECB], n0, dec.rearrange("p b o -> p (b o)"), ALU.mult))
                            dve.tensor_tensor(nstat[:, h, 1:1 + DECB], nstat[:, h, 1:1 + DECB], ps[:, 5, 0:DECB], ALU.add)
                            dve.tensor_tensor(C.rearrange("p (a b) e -> p a (b e)", a=2), C.rearrange("p (a b) e -> p a (b e)", a=2),
                                              ps[:, 6:8, :], ALU.add).then_inc(head_fin, 1)
                    dve.wait_ge(pc_done, 1)
                    dve.tensor_copy(nstat[:, :, 0], ps[:, 1, 0:MH]).then_inc(pn_ready, 1)
                    for h in range(MH):
                        read_out(dve, ("mn", h))
                        link(dve.reciprocal(rstd[:, :], rstd[:, :]))
                        link(dve.scalar_tensor_tensor(out=qm[:, h, :], in0=qm[:, h, :], scalar=sml("mng")[:, h:h + 1], in1=rstd[:, :],
                                                      op0=ALU.mult, op1=ALU.mult))
                        dve.tensor_tensor(haT[:, h, :], haT[:, h, :], qm[:, h, :], ALU.mult).then_inc(ha_ready, 1)
                    for n in range(6):
                        out, free = done(("rope", n))
                        src = qT[:, n, :] if n < 4 else kT[:, n - 4, :]
                        dst = qrT[:, n, :] if n < 4 else kT[:, n - 4, :]
                        if n:
                            dve.wait_ge(rope_ready, n)
                        dve.tensor_tensor(halves(rtmp[:, 0, :]), out, halves(sin), ALU.mult).then_inc(free, 1)
                        link(dve.tensor_tensor(rtmp[:, 1, :], src, cos, ALU.mult))
                        dve.tensor_tensor(dst, rtmp[:, 0, :], rtmp[:, 1, :], ALU.add).then_inc(rope_ready, 1)
                    dve.wait_ge(rope_ready, 4)
                    dve.wait_ge(pool_step, 1)
                    for a, src in enumerate((qT, qrT)):
                        for g in range(NKV):
                            for r in range(R):
                                ins = dve.tensor_copy(qb[g * HD:(g + 1) * HD, a, :, g * 16 + r * 4:g * 16 + r * 4 + 4],
                                                      per_seq(src[g * HD:(g + 1) * HD, r, SEQ:N]))
                    ins.then_inc(qb_ready, 1)

                    def att_max(k):
                        i, g, rp, br = STEPS[k]
                        dve.wait_ge(s_done, k + 1)
                        b = 2 * (k % 2)
                        width = NCP if br == 0 else (i + 1) * P
                        lo = 0 if br == 0 else i * P
                        mask = cneg[:, i, :] if br == 0 else con("qneg")
                        link(dve.tensor_tensor(ps[:, b:b + 2, lo:width], ps[:, b:b + 2, lo:width], bc(mask.unsqueeze(1), [P, 2, width - lo]), ALU.add))
                        dve.tensor_reduce(stat[:, k % 2, :], ps[:, b:b + 2, 0:width], AX.X, ALU.max, negate=True).then_inc(max_ready, 1)

                    def diagonal(k, heads, total, gates):
                        link(dve.tensor_scalar(stat[:, 4, 0:heads], total, TINY, None, ALU.max))
                        link(dve.reciprocal(stat[:, 5, 0:heads], stat[:, 4, 0:heads]))
                        for r in range(heads):
                            ins = dve.tensor_scalar(Dg[:, k % 2, r, :], ident, stat[:, 5, r:r + 1], gates[:, r:r + 1], ALU.mult, ALU.mult)
                        ins.then_inc(d_ready, 1)

                    def att_diag(k):
                        i, g, rp, br = STEPS[k]
                        dve.wait_ge(exp_done, k + 1)
                        total = stat[:, 2 + k % 2, :]
                        if br == 0:
                            link(dve.tensor_tensor(Pt[:, k % 2, :, 0:NCP], Pt[:, k % 2, :, 0:NCP], bc(c01[:, i, :].unsqueeze(1), [P, 2, NCP]), ALU.mult))
                            link(dve.tensor_reduce(total, Pt[:, k % 2, :, 0:NCP], AX.X, ALU.add))
                        if k >= 2:
                            dve.wait_ge(t_done, chunks_of(k - 2)[-1][0] + 1)
                        gv = gate[:, i, :].rearrange("p (h b) -> p h b", b=3)
                        diagonal(k, 2, total, gv[:, g * R + 2 * rp:g * R + 2 * rp + 2, br])

                    att_max(0)
                    att_diag(0)
                    for k in range(NSTEP):
                        if k + 1 < NSTEP:
                            att_max(k + 1)
                        for x, j0, nj in chunks_of(k):
                            if not evac_on_act(x):
                                rows = NCP if STEPS[k][3] == 0 else P
                                dve.wait_ge(t_done, x + 1)
                                if x >= 2:
                                    dve.wait_ge(o_done, x - 1)
                                dve.tensor_copy(PT[0:rows, x % 2, 0:nj * 2 * P], ps[0:rows, 4 + x % 2, 0:nj * 2 * P]).then_inc(t_free[x % 2], 1)
                        if k + 1 < NSTEP:
                            att_diag(k + 1)
                    dve.wait_ge(gs_done, 1)
                    for hb in range(2):
                        gall = ps[:, 3, hb * 24:(hb + 1) * 24].rearrange("p (h b) -> p b h", b=3)
                        link(dve.tensor_tensor(gtmp[:, :, :], gall, bc(con("rowm").unsqueeze(1), [P, 3, NH]), ALU.mult))
                        link(dve.tensor_reduce(gsel[:, hb, :], gtmp[:, :, :], AX.X, ALU.add))

                    def samp_max(m):
                        hb, br = SSTEPS[m]
                        dve.wait_ge(s_done, NSTEP + m + 1)
                        width = P if br == 0 else PAST + NS
                        lo = 0 if br == 0 else PAST
                        mask = kneg[:, hb, :] if br == 0 else nneg[:, hb, :]
                        link(dve.tensor_tensor(ps[:, m % 2, lo:width], ps[:, m % 2, lo:width], mask, ALU.add))
                        dve.tensor_reduce(stat[:, m % 2, 0:1], ps[:, m % 2, 0:width], AX.X, ALU.max, negate=True).then_inc(max_ready, 1)

                    def samp_diag(m):
                        hb, br = SSTEPS[m]
                        dve.wait_ge(exp_done, NSTEP + m + 1)
                        dve.wait_ge(t_done, NPC + max(m - 1, 0))
                        diagonal(m, 1, stat[:, 2 + m % 2, 0:1], gsel[:, hb, br:br + 1])

                    for m in range(6):
                        samp_max(m)
                        samp_diag(m)
                    dve.wait_ge(hb_ready, NSTEP // 3 + 2)
                    dve.wait_ge(nsa_stored, 48)
                    for k in range(KC):
                        if k in (0, 2, 4):
                            split_low(k // 2)
                        dve.wait_ge(xh_ready, k + 1)
                        dve.tensor_tensor(xl[:, k, :], hT[:, k, :], xh[:, k, :].bitcast(F32), ALU.subtract).then_inc(xl_ready, 1)
                    for what, key in late_events():
                        name, m = key
                        if what == "unit":
                            split_low(SPLIT[key] + SRING)
                        elif name in ("a", "b"):
                            n = 0 if name == "a" else 1
                            if m and n == 0:
                                dve.wait_ge(merged_ready, m)
                            read_out(dve, (("ga", "gb")[n], m))
                            out, free = done(key)
                            dve.tensor_tensor(halves(mt[:, n, :]), out, halves(sg[:, n, :]), ALU.mult).then_inc(free, 1)
                            if n == 1:
                                read_out(dve, ("a", m))
                                read_out(dve, ("b", m))
                                link(dve.tensor_tensor(tbuf[:, 0, :], mt[:, 0, :], mt[:, 1, :], ALU.add))
                                split(tbuf[:, 0, :], mh[:, m, :], ml[:, m, :], merged_ready)
                        elif name in ("out", "dn"):
                            out, free = done(key)
                            c = m % KC
                            dve.tensor_tensor(halves(xT[:, c, :]), halves(xT[:, c, :]), out, ALU.add).then_inc(free, 1)
                            if name == "out" and m >= 1:
                                add_square(m)
                            if name == "out" and m == KC - 1:
                                read_out(dve, ("n2", 0))
                                link(dve.reciprocal(rstd[:, :], rstd[:, :]))

                                def scaled(k):
                                    if k >= 2:
                                        dve.wait_ge(xl_ready, KC + k - 1)
                                    dve.scalar_tensor_tensor(out=tbuf[:, k % 2, :], in0=xT[:, k, :], scalar=sml("n2g")[:, k:k + 1],
                                                             in1=rstd[:, :], op0=ALU.mult, op1=ALU.mult).then_inc(t_ready, 1)

                                dve.wait_ge(merged_ready, KC)
                                scaled(0)
                                for k in range(KC):
                                    if k + 1 < KC:
                                        scaled(k + 1)
                                    dve.wait_ge(th_ready, k + 1)
                                    dve.tensor_tensor(xl[:, k, :], tbuf[:, k % 2, :], xh[:, k, :].bitcast(F32),
                                                      ALU.subtract).then_inc(xl_ready, 1)
                        elif name == "fu":
                            read_out(dve, ("fg", m))
                            out, free = done(key)
                            if m >= 1:
                                dve.wait_ge(act_ready, m)
                            dve.tensor_tensor(halves(tbuf[:, 0, :]), out, halves(sg[:, m % 2, :]), ALU.mult).then_inc(free, 1)
                            read_out(dve, key)
                            if m % NFH == 0:
                                dve.wait_ge(pair_done, GROUP[key] + 1)
                            split(tbuf[:, 0, :], ah[:, m % NFH, :], al[:, m % NFH, :], act_ready)

            for s in layer_sems:
                nc.sync.sem_clear(s)
            nc.all_engine_barrier()

        yT = slab[:, MIX_AT:MIX_AT + KC * N].rearrange("p (k n) -> p k n", k=KC)
        fin_sq = ctx.enter_context(nc.semaphore("fin_sq"))
        fin_sum = ctx.enter_context(nc.semaphore("fin_sum"))
        fin_done = ctx.enter_context(nc.semaphore("fin_done"))
        fin_root = ctx.enter_context(nc.semaphore("fin_root"))
        fin_step = ctx.enter_context(nc.semaphore("fin_step"))
        fin_y = ctx.enter_context(nc.semaphore("fin_y"))
        fin_stored = ctx.enter_context(nc.semaphore("fin_stored"))
        with nc.Block() as block:
            @block.scalar
            def _(act):
                for k in range(KC):
                    if k >= 3:
                        act.wait_ge(fin_sum, k - 2)
                    act.activation(acc[:, :] if k == 0 else sq[:, k % 2, :], xT[:, k, :], ACT.Square).then_inc(fin_sq, 1)
                act.wait_ge(fin_done, 1)
                act.activation(halves(rstd[:, :]), ps[:, 0:2, 0:NHALF], ACT.Sqrt, bias=eps[:, :], scale=1.0 / D).then_inc(fin_root, 1)

            @block.tensor
            def _(pe):
                pe.wait_ge(fin_sum, KC - 1)
                for a in range(2):
                    mm = pe.matmul(ps[:, a, 0:NHALF], ones[:, :], acc[:, a * NHALF:(a + 1) * NHALF], start=True, stop=True)
                mm.then_inc(fin_done, 1)

            @block.vector
            def _(dve):
                for k in range(1, KC):
                    dve.wait_ge(fin_sq, k + 1)
                    if k >= 2:
                        dve.wait_ge(fin_sum, k - 1)
                    dve.tensor_tensor(acc[:, :], acc[:, :], sq[:, k % 2, :], ALU.add).then_inc(fin_sum, 1)
                dve.wait_ge(fin_root, 1)
                dve.reciprocal(rstd[:, :], rstd[:, :]).then_inc(fin_step, 1)
                dve.wait_ge(fin_step, 1)
                fng = con("fng")
                for k in range(KC):
                    dve.scalar_tensor_tensor(out=yT[:, k, :], in0=xT[:, k, :], scalar=fng[:, k:k + 1], in1=rstd[:, :],
                                             op0=ALU.mult, op1=ALU.mult).then_inc(fin_y, 1)

            @block.sync
            def _(sp):
                for k in range(KC):
                    sp.wait_ge(fin_y, k + 1)
                    sp.dma_start(y_out[:, k, :], yT[:, k, :]).then_inc(fin_stored, 16)
                sp.wait_ge(fin_stored, 16 * KC)


def shape_constants():
    c = np.zeros((P, CONST_W), np.float32)

    def put(name, value):
        a, b = CONST[name]
        v = np.asarray(value, np.float32)
        v = v.reshape(v.shape[0], -1)
        c[:v.shape[0], a:b] = v

    pos = np.concatenate([np.arange(SEQ), np.tile(PAST + np.arange(DECT), DECB)]).astype(np.float32)
    half = HD // 8
    inv = (np.float32(500000.0) ** (-np.arange(half, dtype=np.float32) / np.float32(half))).astype(np.float32)
    ang = (pos[None, :] * inv[:, None]).astype(np.float32)
    cos, sin, rot = np.ones((P, N)), np.zeros((P, N)), np.zeros((P, P))
    for g in range(NKV):
        for a in range(2):
            cos[g * HD + a * half:g * HD + (a + 1) * half] = np.cos(ang.astype(np.float64))
            sin[g * HD + a * half:g * HD + (a + 1) * half] = np.sin(ang.astype(np.float64))
        for d in range(half):
            rot[g * HD + half + d, g * HD + d] = -1.0
            rot[g * HD + d, g * HD + half + d] = 1.0
    put("cos", cos)
    put("sin", sin)
    put("rot", rot)
    put("ident", np.eye(P))
    t = np.arange(P)
    put("qneg", np.where(t[None, :] <= t[:, None], 0.0, NEG))
    put("sneg", np.where(t[:, None] <= t[None, :], 0.0, NEG))
    q = t[:, None, None] + P * np.arange(TT)[None, :, None]
    seen = np.arange(NCP)[None, None, :] * STRIDE + CLEN - 1 <= q
    put("cneg", np.where(seen, 0.0, NEG))
    put("c01", seen)
    put("sel4", np.repeat(np.eye(MH)[:, :, None], P, 2))
    s = np.arange(NS)
    same = s[:, None] // DECT == s[None, :] // DECT
    put("m32", np.where(same & (s[:, None] <= s[None, :]), 0.0, NEG))
    put("blk", s[:, None] // DECT == np.arange(DECB)[None, :])
    b4, g, r, tok = t // 32, t // 16 % 2, t // 4 % 4, t % 4
    b = b4[:, None] + 4 * np.arange(2)[None, :]
    put("nneg", np.where((b[:, :, None] == s // DECT) & (s % DECT <= tok[:, None, None]), 0.0, NEG))
    put("kneg", np.where((b[:, :, None] == t // SBLK) & (t % SBLK < SBLK - 1), 0.0, NEG))
    put("tsel", s[:, None, None] == (b * DECT + tok[:, None]).T[None])
    put("rowm", (g * R + r)[:, None] == np.arange(NH)[None, :])
    return c


def chunked(a):
    return a.reshape(-1, P, a.shape[-1]).transpose(1, 0, 2)


def weight_units(l, w):
    w_in = w["w_in"][l]
    at = np.cumsum([0, 512, 512, 512, 4, 4, 512, 768, 24, D, D])
    u, v, o, ig, fg, q, kv, ng, ga, gb = (w_in[:, a:b] for a, b in zip(at[:-1], at[1:]))
    kv = kv.reshape(D, 6, P)
    q = q.reshape(D, NKV, R, HD).transpose(0, 2, 1, 3).reshape(D, 512)
    out = np.zeros((len(UNITS), P, UCOLS), np.float32)

    def put(key, a):
        a = np.ascontiguousarray(a).reshape(P, -1)
        out[UNIT[key], :, :a.shape[1]] = a

    tm = np.concatenate([v, kv[:, 3], kv[:, 5], ng], 1)
    for k in range(KC):
        put(("tm", k), tm[k * P:(k + 1) * P])
    gates = np.zeros((D, P), np.float32)
    gates[:, 0:MH] = ig
    gates[:, 32:32 + MH] = fg
    put(("if", 0), chunked(gates))
    kk = kv[:, [0, 1, 2, 4]].reshape(D, 512)
    for m in range(4):
        for name, a in (("u", u), ("o", o), ("q", q), ("k", kk)):
            put((name, m), chunked(a[:, m * P:(m + 1) * P]))
    for v2, name in enumerate(("cmp_w1_k", "cmp_w1_v")):
        w1 = w[name][l].transpose(1, 0, 2)
        w1 = np.concatenate([w1, w1], 0)
        for n in range(4):
            put(("w1", 4 * v2 + n), w1[:, 8 * n:8 * n + 8])
    wb = w["w_branch_b"][l].reshape(NKV, R, HD, D).transpose(1, 0, 2, 3).reshape(512, D)
    for m in range(KC):
        c = slice(m * P, (m + 1) * P)
        put(("ga", m), chunked(ga[:, c]))
        put(("gb", m), chunked(gb[:, c]))
        put(("ab", m), np.concatenate([chunked(w["w_branch_a"][l][:, c]), chunked(wb[:, c])], 1))
        put(("out", m), chunked(w["w_out"][l][:, c]))
    dn = w["w_ffn_down"][l].reshape(2, NFH, P, KC, P).transpose(0, 3, 1, 2, 4).reshape(2, NFH, 8, P, P)
    for n in range(2 * NFH):
        put(("dn", n), dn[n // NFH, n % NFH].transpose(1, 0, 2))
    for m in range(NFF):
        put(("fg", m), chunked(w["w_ffn_up"][l][:, m * P:(m + 1) * P]))
        put(("fu", m), chunked(w["w_ffn_up"][l][:, (NFF + m) * P:(NFF + m + 1) * P]))
    return out


def small_weights(l, w):
    out = np.zeros((P, SMALL_W), np.float32)

    def put(name, a):
        a = np.ascontiguousarray(a)
        a = a.reshape(a.shape[0], -1)
        lo, hi = SMALL[name]
        out[:a.shape[0], lo:lo + a.shape[1]] = a

    def vec(a):
        return a.reshape(-1, P).T

    put("n1g", vec(w["norm1_g"][l]))
    put("n2g", vec(w["norm2_g"][l]))
    put("mng", vec(w["mlstm_norm_g"][l]))
    put("cw", w["conv_w"][l].reshape(CONV, 4, P).transpose(2, 1, 0))
    put("cb", vec(w["conv_b"][l]))
    put("wmq", w["w_mq"][l].transpose(1, 0, 2))
    put("wmk", w["w_mk"][l].transpose(1, 0, 2))
    put("w2", np.stack([w["cmp_w2_k"][l], w["cmp_w2_v"][l]], 1))
    pe = np.stack([w["cmp_pe_k"][l].T, w["cmp_pe_v"][l].T], 1)
    put("pe", np.concatenate([pe, pe], 0))
    put("bi", w["b_gates"][l][:MH, None])
    put("bf", w["b_gates"][l][MH:, None])
    put("m0", w["state_mlstm_m"][l].T)
    put("n0", w["state_mlstm_n"][l].transpose(2, 1, 0))
    put("cs", w["state_mlstm_conv"][l].reshape(DECB, CONV - 1, 4, P).transpose(3, 2, 0, 1))
    return out


def kernel(**inputs):
    import concourse.bacc as bacc
    from concourse.bass_utils import run_bass_kernel_spmd

    w = {k: np.asarray(v) for k, v in inputs.items()}
    x = np.concatenate([w["x_prompt"].reshape(SEQ, D), w["x_sample"].reshape(NS, D)], 0)
    const = shape_constants()
    a, b = CONST["fng"]
    const[:, a:b] = w["final_norm_g"].reshape(KC, P).T
    pages = w["cache_kv_pages"]
    pool = pages.shape[1]
    pg = pages.reshape(DEPTH, pool, PAGE, 4, P)
    turned = pg[:, :, :, 0:3].transpose(0, 1, 4, 3, 2).reshape(DEPTH, pool, P, 3 * PAGE)
    packed = np.concatenate([turned, pg[:, :, :, 3]], 3)
    cw = w["cache_win"].reshape(DEPTH, DECB, PAST, 2, P)
    wk = cw[:, :, :, 0].transpose(0, 3, 1, 2)
    wv = cw[:, :, :, 1].reshape(DEPTH, DECB, NPG, P, P).transpose(0, 3, 1, 2, 4).reshape(DEPTH, P, DECB, PAST)
    win = np.stack([wk, wv], 3).reshape(DEPTH, P, DECB * 2 * PAST)
    arrays = {
        "xT": chunked(np.ascontiguousarray(x.T)),
        "W": np.stack([weight_units(l, w) for l in range(DEPTH)]),
        "small": np.stack([small_weights(l, w) for l in range(DEPTH)]),
        "consts": const,
        "c0": w["state_mlstm_C"].transpose(0, 2, 3, 1, 4).reshape(DEPTH, MH, P, DECB * MD),
        "pages": packed,
        "table": w["page_table"].reshape(1, -1).astype(np.int32),
        "win": win,
        "cwin": w["cache_win"].reshape(DEPTH, DECB, PAST * 2 * P),
    }
    outs = {
        "y": (P, KC, N), "fm": (DEPTH, P, 2, N), "raw": (DEPTH, P, 2, STRIDE, PBLK), "knew": (DEPTH, P, 2, NS), "tm": (DEPTH, P, TT + 1, 2 * P), "u": (DEPTH, P, 4, UW - SEQ),
        "pC": (DEPTH, P, MH * MD), "pn": (DEPTH, P, MH * (1 + DECB)), "m": (DEPTH, MH, N),
        "sC": (DEPTH, MH, P, DECB * MD), "oldwin": (DEPTH, DECB, (PAST - DECT) * 2 * P),
    }
    nc = bacc.Bacc("TRN2", target_bir_lowering=False, num_devices=1)
    ins, args = {}, []
    for name, v in arrays.items():
        v = np.ascontiguousarray(v)
        ins["in_" + name] = v
        args.append(nc.dram_tensor("in_" + name, v.shape, mybir.dt.from_np(v.dtype), kind="ExternalInput").ap())
    oap = {n: nc.dram_tensor("out_" + n, s, F32, kind="ExternalOutput").ap() for n, s in outs.items()}
    build_step(nc, *args, *(oap[n] for n in ("y", "fm", "raw", "knew", "tm", "u", "pC", "pn", "m", "sC", "oldwin")))
    got = run_bass_kernel_spmd(nc, [ins], core_ids=[0]).results[0]
    o = {n: np.asarray(got["out_" + n]) for n in outs}

    y = o["y"].transpose(2, 1, 0).reshape(N, D)
    fm, tmv = o["fm"], o["tm"]
    ks, kwin = (fm[:, :, n].transpose(0, 2, 1) for n in range(2))
    raw = o["raw"].transpose(0, 2, 4, 3, 1).reshape(DEPTH, 2, SEQ, P)
    raw = np.concatenate([raw, o["knew"].transpose(0, 2, 3, 1)], 2)
    kc, vc = raw[:, 0], raw[:, 1]
    tok = np.concatenate([tmv[:, :, :TT].transpose(0, 2, 1, 3).reshape(DEPTH, SEQ, 2 * P), tmv[:, :NS, TT]], 1)
    vs, vw = tok[..., :P], tok[..., P:]
    rows = np.stack([kc, vc, ks, vs], 2).reshape(DEPTH, N, 4, NKV, HD)
    wins = np.stack([kwin, vw], 2).reshape(DEPTH, N, 2, NKV, HD)
    old = o["oldwin"].reshape(DEPTH, DECB, PAST - DECT, 2, NKV, HD)
    u = o["u"]
    hist = CONV - 1
    p_conv = u[..., :hist].transpose(0, 3, 2, 1).reshape(DEPTH, 1, hist, 512)
    s_conv = u[..., hist:].reshape(DEPTH, P, 4, DECB, hist + DECT)[..., DECT:].transpose(0, 3, 4, 2, 1).reshape(DEPTH, DECB, hist, 512)
    n_ = o["pn"].reshape(DEPTH, P, MH, 1 + DECB).transpose(0, 3, 2, 1)
    m_ = o["m"]
    got = (
        y[:SEQ].reshape(1, SEQ, D), y[SEQ:].reshape(DECB, DECT, D),
        rows[:, None, :SEQ], wins[:, None, :SEQ],
        o["pC"].reshape(DEPTH, P, MH, MD).transpose(0, 2, 1, 3)[:, None], n_[:, 0:1], m_[:, None, :, SEQ - 1], p_conv,
        rows[:, SEQ:].reshape(DEPTH, DECB, DECT, 4, NKV, HD),
        np.concatenate([old, wins[:, SEQ:].reshape(DEPTH, DECB, DECT, 2, NKV, HD)], 2),
        o["sC"].reshape(DEPTH, MH, P, DECB, MD).transpose(0, 3, 1, 2, 4), n_[:, 1:],
        m_[:, :, SEQ:].reshape(DEPTH, MH, DECB, DECT)[..., -1].transpose(0, 2, 1), s_conv,
    )
    return tuple(np.ascontiguousarray(a) for a in got)
```

```python
from contextlib import ExitStack

import numpy as np

import concourse.bass as bass
from concourse import mybir

ALU = mybir.AluOpType
ACT = mybir.ActivationFunctionType
F32 = mybir.dt.float32
I32 = mybir.dt.int32
F32R = mybir.dt.float32r
AX = mybir.AxisListType

P = 128
DEPTH, D, SEQ, DECB, DECT, PAST, PAGE = 2, 1024, 512, 8, 4, 256, 128
KC = D // P
NS = DECB * DECT
N = SEQ + NS
NHALF = N // 2
MH, MD = 4, 128
NH, NKV, HD = 8, 2, 64
R = NH // NKV
CONV = 4
STRIDE, CLEN, HID = 16, 32, 128
NFF = 2816 // P
TT = SEQ // P
NPG = PAST // PAGE
EPS, NEG, TINY = 1e-6, -1e30, 1e-30
RAW = SEQ + DECB * PAST
NBLK = RAW // STRIDE
RC = NBLK + 2
NCP = SEQ // STRIDE - 1
PBLK = SEQ // STRIDE
SBLK = PAST // STRIDE
UW = (CONV - 1) + SEQ + DECB * (CONV - 1 + DECT)

NFH = NFF // 2

K_ORDER = (2, 3, 0, 1)
QK_TAIL = [("k", 2), ("rope", 0), ("k", 3), ("rope", 4), ("rope", 1), ("rope", 5), ("k", 0), ("rope", 2), ("rope", 3), ("k", 1)]
ROPE_ORDER = [n for kind, n in QK_TAIL if kind == "rope"]

UNITS = ([("u", m) for m in range(4)] + [("tm", k) for k in range(KC)] + [("if", 0)]
         + [("o", m) for m in range(4)] + [("q", m) for m in range(4)] + [("k", m) for m in K_ORDER]
         + [("w1", n) for n in range(8)]
         + [(w, m) for m in range(KC) for w in ("ga", "gb", "ab")]
         + [("out", m) for m in range(KC)]
         + [u for f in range(2) for u in
            [(w, m) for m in range(f * NFH, (f + 1) * NFH) for w in ("fg", "fu")] + [("dn", n) for n in range(f * NFH, (f + 1) * NFH)]])
UNIT = {key: n for n, key in enumerate(UNITS)}
RING = 8
UCOLS = 1024
TMC = 512 + 280

GROUPS = ([("n1", 0)] + [("u", m) for m in range(4)] + [("tm", i) for i in range(TT + 1)] + [("if", 0)]
          + [("o", m) for m in range(4)] + [(w, h) for h in range(MH) for w in ("mq", "mk")]
          + [("aw", 0)] + [("kw", i) for i in range(TT + 1)]
          + [("mn", h) for h in range(MH)]
          + [("q", m) for m in range(4)] + QK_TAIL
          + [(w, m) for m in range(KC) for w in ("ga", "gb", "a", "b")]
          + [("out", m) for m in range(KC)] + [("n2", 0)]
          + [g for f in range(2) for g in
             [(w, m) for m in range(f * NFH, (f + 1) * NFH) for w in ("fg", "fu")] + [("dn", f * KC + m) for m in range(KC)]])
GROUP = {key: n for n, key in enumerate(GROUPS)}
CORE_AT = GROUP[("mn", 0)]
ATTN_AT = GROUP[("ga", 0)]


SPLITS = [key for key in UNITS if key[0] in ("o", "q", "k", "ga", "gb", "ab", "out", "fg", "fu", "dn")]
SPLIT = {key: n for n, key in enumerate(SPLITS)}
SRING = 3
QSPLIT, LSPLIT = 4, 12


def columns(spec):
    at, out = 0, {}
    for name, width in spec:
        out[name] = (at, at + width)
        at += width
    return out, at


SMALL, SMALL_W = columns([("n1g", KC), ("n2g", KC), ("mng", MH), ("cw", 4 * CONV), ("cb", 4), ("wmq", MH * MD),
                          ("wmk", MH * MD), ("w2", 2 * HD), ("pe", 2 * CLEN), ("bi", 1), ("bf", 1), ("m0", DECB),
                          ("n0", MH * DECB), ("cs", 4 * DECB * (CONV - 1))])
SMALL_FIRST = SMALL["cb"][1]
CONST, CONST_W = columns([("cos", N), ("sin", N), ("rot", P), ("ident", P), ("qneg", P), ("sneg", P),
                          ("cneg", TT * NCP), ("c01", TT * NCP), ("sel4", MH * P), ("m32", NS), ("blk", DECB),
                          ("nneg", 2 * NS), ("kneg", 2 * P), ("tsel", 2 * P), ("rowm", NH), ("fng", KC)])


MIX, MIX_W = columns([("upad", 4 * UW), ("cT", 4 * N), ("ctmp", 2 * N), ("qm", MH * N), ("km", MH * N),
                    ("vtm", (TT + 1) * 512), ("kw", (TT + 1) * 512), ("C", 2 * DECB * MD), ("vb", DECB * MD),
                    ("rows", 2 * NS)])
CORE, CORE_W = columns([("gbc", 2 * N), ("enm", 2 * N), ("int", 2 * NS), ("E", 2 * 512), ("St", 2 * 512),
                      ("qi", 2 * NS), ("gmask", 2 * P), ("pC", MH * MD)])
assert CORE_W <= 4 * UW + 4 * N + 2 * N
NSA, NSA_W = columns([("qT", 4 * N), ("qrT", 4 * N), ("kT", 2 * N), ("knew", 2 * NS), ("selp", DECB * 2 * NPG * P),
                    ("P", 2 * 2 * 512), ("Pc", MH * 64), ("PT", 2 * 512), ("kcT", NBLK), ("vcp", P), ("vcs", P),
                    ("qb", 2 * DECB * 32), ("raw", 2 * STRIDE * RC)])
UNDER, UNDER_W = columns([("stage", 4 * 2 * PAGE), ("rtmp", 2 * N), ("hid", 2 * 2 * NBLK)])
assert UNDER_W <= NSA["selp"][1] - NSA["selp"][0]
NSA.update({name: (NSA["selp"][0] + a, NSA["selp"][0] + b) for name, (a, b) in UNDER.items()})
assert NSA["raw"][0] - NSA["P"][0] >= 4 * UCOLS + 8 and MIX["km"][0] <= NSA["P"][0] and NSA["raw"][0] <= MIX["C"][0]
XH_AT = KC * N
HA_AT = 2 * KC * N
MIX_AT = HA_AT + MH * N + R * N
LATE, LATE_W = columns([("before", MIX_AT), ("w", 2 * SRING * UCOLS), ("mh", KC * N), ("ml", KC * N),
                        ("sg", 2 * N), ("mt", 2 * N), ("t", 2 * N)])
AH_AT = LATE["mh"][0]
AL_FIRST = (MIX_AT - HA_AT) // N - 2
AL_REST_AT = AH_AT + NFH * N
assert NSA["kT"][0] >= 4 * UCOLS and HA_AT + AL_FIRST * N <= MIX_AT
assert AL_REST_AT + (NFH - AL_FIRST) * N <= LATE["ml"][1]
SLAB_W = max(MIX_AT + max(MIX_W, NSA_W), LATE_W + N)


def build_step(nc, xT_in, W_in, small_in, const_in, c0_in, pages_in, table_in, win_in, cwin_in,
               y_out, fm_out, raw_out, knew_out, tm_out, u_out, pC_out, pn_out, m_out, sC_out, oldwin_out):
    with ExitStack() as ctx:
        def sb(name, shape, dt=F32):
            return ctx.enter_context(nc.sbuf_tensor(name, shape, dt))

        def sem(name):
            s = ctx.enter_context(nc.semaphore(name))
            layer_sems.append(s)
            return s

        layer_sems = []

        def where():
            return -(-nc.sbuf_base // 32) * 32

        slab_at = where()
        slab = sb("slab", [P, SLAB_W])

        def at_slab(name, col, shape):
            return nc.alloc_sbuf_tensor_at(name, shape, F32R, offset=slab_at + 4 * col)

        xT = sb("xT", [P, KC, N])
        hT = slab[:, 0:KC * N].rearrange("p (k n) -> p k n", k=KC)
        haT = slab[:, HA_AT:HA_AT + MH * N].rearrange("p (k n) -> p k n", k=MH)
        hbT = slab[:, HA_AT + MH * N:MIX_AT].rearrange("p (k n) -> p k n", k=R)
        xl = at_slab("xl", 0, [P, KC, N])
        xh = at_slab("xh", XH_AT, [P, KC, N])
        mh = at_slab("mh", LATE["mh"][0], [P, KC, N])
        ml = at_slab("ml", LATE["ml"][0], [P, KC, N])
        ah = at_slab("ah", AH_AT, [P, NFH, N])
        al_first = at_slab("al_first", HA_AT, [P, AL_FIRST, N])
        al_rest = at_slab("al_rest", AL_REST_AT, [P, NFH - AL_FIRST, N])
        late_w = at_slab("late_w", LATE["w"][0], [P, SRING, 2, UCOLS])
        gate_at, query_at = (-(-(MIX_AT + col) // 8) * 8 for col in (MIX["qm"][0], NSA["P"][0]))
        gate_w = (at_slab("gwh", gate_at, [P, 2, UCOLS]), at_slab("gwl", gate_at + 2 * UCOLS, [P, 2, UCOLS]))
        query_w = (at_slab("qwh", query_at, [P, 2, UCOLS]), at_slab("qwl", query_at + 2 * UCOLS, [P, 2, UCOLS]))

        def split_weights(n):
            if n >= LSPLIT:
                return late_w[:, n % SRING, 0, :], late_w[:, n % SRING, 1, :], SRING
            hi, lo = gate_w if n < QSPLIT else query_w
            return hi[:, n % 2, :], lo[:, n % 2, :], 2

        def al(k):
            return al_first[:, k, :] if k < AL_FIRST else al_rest[:, k - AL_FIRST, :]

        ring = sb("ring", [P, RING, UCOLS])
        const = sb("const", [P, CONST_W])
        small = sb("small", [P, SMALL_W])
        hbrows = hbT
        sq_at = where()
        sq = sb("sq", [P, 2, N])
        rstd_at = where()
        rstd = sb("rstd", [P, N])
        vkv = sb("vkv", [P, TT + 1, 2 * P])
        gate = sb("gate", [P, TT + 1, NH * 3])
        ones = sb("ones", [P, P])
        eps = sb("eps", [P, 1])
        awt = sb("awt", [P, TT + 1, 2, MH])
        stat = sb("stat", [P, 11, 4])
        nstat = sb("nstat", [P, MH, 1 + DECB])
        gsel = sb("gsel", [P, 2, 3])
        gtmp = sb("gtmp", [P, 3, NH])
        hbias = sb("hbias", [P, 2])
        table = sb("table", [1, DECB * NPG], I32)
        big = slab[:, MIX_AT:SLAB_W]
        kwsum = rstd[:, 0:MH * MD]
        acc_at = where()
        acc = sb("acc", [P, N])
        ha_low = at_slab("ha_low", HA_AT, [P, MH, N])
        hb_low = at_slab("hb_low", HA_AT + MH * N, [P, R, N])
        sq_high = nc.alloc_sbuf_tensor_at("sq_high", [P, 2, N], F32R, offset=sq_at)
        rstd_high = nc.alloc_sbuf_tensor_at("rstd_high", [P, N], F32R, offset=rstd_at)
        acc_high = nc.alloc_sbuf_tensor_at("acc_high", [P, N], F32R, offset=acc_at)
        t_high = at_slab("t_high", LATE["t"][0] + N, [P, N])
        end_high = at_slab("end_high", LATE_W, [P, N])
        ha_high = (sq_high[:, 0, :], sq_high[:, 1, :], rstd_high[:, :], acc_high[:, :])
        hb_high = (mh[:, KC - 1, :], ml[:, KC - 1, :], t_high[:, :], end_high[:, :])

        ps = ctx.enter_context(nc.psum_tensor("ps", [P, 8, 512], F32))

        def cut(lay, name, pattern=None, base=None, **k):
            a, b = lay[name]
            v = (big if base is None else base)[:, a:b]
            return v.rearrange(pattern, **k) if pattern else v

        def con(name, pattern=None, **k):
            return cut(CONST, name, pattern, const, **k)

        def sml(name, pattern=None, **k):
            return cut(SMALL, name, pattern, small, **k)

        upad = cut(MIX, "upad", "p (c n) -> p c n", c=4)
        cT = cut(MIX, "cT", "p (c n) -> p c n", c=4)
        ctmp = cut(MIX, "ctmp", "p (c n) -> p c n", c=2)
        qm = cut(MIX, "qm", "p (c n) -> p c n", c=MH)
        km = cut(MIX, "km", "p (c n) -> p c n", c=MH)
        vtm = cut(MIX, "vtm", "p (i n) -> p i n", n=512)
        kw = cut(MIX, "kw", "p (i n) -> p i n", n=512)
        Cst = cut(MIX, "C", "p (a b e) -> p a b e", a=2, b=DECB)
        vb = cut(MIX, "vb", "p (b e) -> p b e", b=DECB)
        rowsx = cut(MIX, "rows")
        pCs = cut(CORE, "pC", "p (h e) -> p h e", h=MH)
        gbc = cut(CORE, "gbc", "p (a n) -> p a n", a=2)
        enm = cut(CORE, "enm", "p (a n) -> p a n", a=2)
        inter = cut(CORE, "int", "p (a n) -> p a n", a=2)
        Et = cut(CORE, "E", "p (a n) -> p a n", a=2)
        St = cut(CORE, "St", "p (a n) -> p a n", a=2)
        qi = cut(CORE, "qi", "p (a n) -> p a n", a=2)
        gmask = cut(CORE, "gmask", "p (a n) -> p a n", a=2)
        qT = cut(NSA, "qT", "p (c n) -> p c n", c=4)
        qrT = cut(NSA, "qrT", "p (c n) -> p c n", c=4)
        kT = cut(NSA, "kT", "p (c n) -> p c n", c=2)
        raw = cut(NSA, "raw", "p (v l n) -> p v l n", v=2, l=STRIDE)
        knew = cut(NSA, "knew", "p (v n) -> p v n", v=2)
        stage = cut(NSA, "stage", "p (a v n) -> p a v n", a=4, v=2)
        winp = cut(NSA, "raw")[:, 0:DECB * 2 * NPG * P].rearrange("p (b v j s) -> p b v j s", b=DECB, v=2, j=NPG)
        selp = cut(NSA, "selp", "p (b j v s) -> p b j v s", b=DECB, j=NPG, v=2)
        Pt = cut(NSA, "P", "p (a n) -> p a n", a=2)
        Pc = cut(NSA, "Pc")
        PT = cut(NSA, "PT", "p (a n) -> p a n", a=2)
        qb = cut(NSA, "qb", "p (a b m) -> p a b m", a=2, b=DECB)
        hid = cut(NSA, "hid", "p (v g n) -> p v g n", v=2, g=2)
        kcT = cut(NSA, "kcT")
        vcp = cut(NSA, "vcp")
        vcs = cut(NSA, "vcs")
        rtmp = cut(NSA, "rtmp", "p (a n) -> p a n", a=2)
        sg = cut(LATE, "sg", "p (a n) -> p a n", slab, a=2)
        mt = cut(LATE, "mt", "p (a n) -> p a n", slab, a=2)
        tbuf = cut(LATE, "t", "p (a n) -> p a n", slab, a=2)

        def row(n):
            if n < 4:
                return hbrows[0:MH, n, :]
            return (rstd[0:MH, :], sq[0:MH, 0, :], acc[0:MH, :], sq[0:MH, 1, :])[n - 4]

        I_, Z_, L_, F_, M_, A_, G_, W_ = range(8)
        EN_ = L_
        introw = rowsx[0:MH, 0:NS]
        tmprow = rowsx[0:MH, NS:2 * NS]

        def per_seq(r):
            return r.rearrange("p (b t) -> p b t", t=DECT)

        def halves(v):
            return v.rearrange("p (a n) -> p a n", a=2)

        def pair(q, cols=NHALF, rows=P):
            s = q % 4
            return ps[0:rows, 2 * s:2 * s + 2, 0:cols]

        def bc(ap, shape):
            return ap.to_broadcast(shape)

        cos, sin, ident = con("cos"), con("sin"), con("ident")
        rot = con("rot")
        sel4 = con("sel4", "p (h n) -> p h n", h=MH)
        cneg = con("cneg", "p (i n) -> p i n", i=TT)
        c01 = con("c01", "p (i n) -> p i n", i=TT)
        nneg = con("nneg", "p (a n) -> p a n", a=2)
        kneg = con("kneg", "p (a n) -> p a n", a=2)
        tsel = con("tsel", "p (a n) -> p a n", a=2)

        unit_landed = [sem(f"unit_landed{s}") for s in range(RING)]
        pair_done = sem("pair_done")
        pair_free = [sem(f"pair_free{s}") for s in range(4)]
        small_landed = sem("small_landed")
        scales_landed = sem("scales_landed")
        page_landed = [sem(f"page_landed{i}") for i in range(4)]
        raw_ready = sem("raw_ready")
        page_arranged = sem("page_arranged")
        sel_landed = sem("sel_landed")
        win_landed = sem("win_landed")
        c0_landed = [sem(f"c0_landed{s}") for s in range(2)]
        stored = sem("stored")
        cstored = sem("cstored")
        history_ready = sem("history_ready")
        tm_used = sem("tm_used")
        w1_used = sem("w1_used")
        dn_used = sem("dn_used")
        wh_ready = sem("wh_ready")
        wl_ready = sem("wl_ready")
        xh_ready = sem("xh_ready")
        xl_ready = sem("xl_ready")
        t_ready = sem("t_ready")
        th_ready = sem("th_ready")
        ha_high_ready = sem("ha_high_ready")
        ha_low_ready = sem("ha_low_ready")
        hb_high_ready = sem("hb_high_ready")
        hb_low_ready = sem("hb_low_ready")
        act_ready = sem("act_ready")
        u_stored = sem("u_stored")
        mix_stored = sem("mix_stored")
        raw_stored = sem("raw_stored")
        nsa_stored = sem("nsa_stored")
        num_copied = sem("num_copied")
        den_read = sem("den_read")
        num_ready = sem("num_ready")
        pn_ready = sem("pn_ready")
        sq_ready = sem("sq_ready")
        sq_used = sem("sq_used")
        h_ready = sem("h_ready")
        conv_ready = sem("conv_ready")
        c_ready = sem("c_ready")
        ln_ready = sem("ln_ready")
        rows_ready = sem("rows_ready")
        wexp_ready = sem("wexp_ready")
        bc_done = sem("bc_done")
        bc_ready = sem("bc_ready")
        ms_done = sem("ms_done")
        gm_ready = sem("gm_ready")
        e_ready = sem("e_ready")
        st_ready = sem("st_ready")
        nd_done = sem("nd_done")
        head_fin = sem("head_fin")
        qi_ready = sem("qi_ready")
        msq_ready = sem("msq_ready")
        ha_ready = sem("ha_ready")
        vb_ready = sem("vb_ready")
        cs_done = sem("cs_done")
        c_decayed = sem("c_decayed")
        kw_summed = sem("kw_summed")
        pc_done = sem("pc_done")
        pc_ready = sem("pc_ready")
        rope_ready = sem("rope_ready")
        hid_ready = sem("hid_ready")
        cmp_done = sem("cmp_done")
        cmp_ready = sem("cmp_ready")
        qb_ready = sem("qb_ready")
        s_done = sem("s_done")
        max_ready = sem("max_ready")
        exp_done = sem("exp_done")
        weight_ready = sem("weight_ready")
        p_ready = sem("p_ready")
        cp_ready = sem("cp_ready")
        t_done = sem("t_done")
        t_free = [sem(f"t_free{s}") for s in range(2)]
        o_done = sem("o_done")
        hb_ready = sem("hb_ready")
        gs_done = sem("gs_done")
        gs_read = sem("gs_read")
        merged_ready = sem("merged_ready")
        dve_step = sem("dve_step")
        act_step = sem("act_step")
        qb_cleared = sem("qb_cleared")

        x_landed = [ctx.enter_context(nc.semaphore(f"x_landed{k}")) for k in range(KC)]
        const_landed = ctx.enter_context(nc.semaphore("const_landed"))
        table_landed = ctx.enter_context(nc.semaphore("table_landed"))
        start_squared = ctx.enter_context(nc.semaphore("start_squared"))
        start_added = ctx.enter_context(nc.semaphore("start_added"))

        with nc.Block() as block:
            @block.sync
            def _(sp):
                for k in range(KC):
                    sp.dma_start(xT[:, k, :], xT_in[:, k, :]).then_inc(x_landed[k], 16)
                sp.dma_start(const[:, :], const_in).then_inc(const_landed, 16)
                sp.dma_start(table[:, :], table_in).then_inc(table_landed, 16)

            @block.scalar
            def _(act):
                for k in range(KC):
                    act.wait_ge(x_landed[k], 16)
                    if k >= 3:
                        act.wait_ge(start_added, k - 2)
                    act.activation(acc[:, :] if k == 0 else sq[:, k % 2, :], xT[:, k, :], ACT.Square).then_inc(start_squared, 1)

            @block.vector
            def _(dve):
                dve.memset(ones[:, :], 1.0)
                dve.memset(eps[:, :], EPS)
                for k in range(1, KC):
                    dve.wait_ge(start_squared, k + 1)
                    if k >= 2:
                        dve.wait_ge(start_added, k - 1)
                    dve.tensor_tensor(acc[:, :], acc[:, :], sq[:, k % 2, :], ALU.add).then_inc(start_added, 1)
                dve.wait_ge(start_added, KC - 1)

        STEPS = []
        for i, g in [(i, g) for i in range(TT) for g in range(NKV)] + [(None, 0), (None, 1)]:
            if i is None:
                STEPS += [(None, g, None, 1, (br,), br) for br in (1, 2, 0)]
                continue
            for rp in range(2):
                if i < 2:
                    STEPS.append((i, g, 2 * rp, 2, (1, 2), 1 + rp))
                else:
                    STEPS += [(i, g, 2 * rp, 2, (br,), br) for br in (1, 2)]
            STEPS.append((i, g, 0, R, (0,), 0))
        NSTEP = len(STEPS)
        CHUNKS = []
        for k, (i, g, r0, heads, brs, region) in enumerate(STEPS):
            if i is None or brs == (0,):
                CHUNKS.append((k, [(brs[0], 0)]))
            else:
                blocks = [(br, j) for br in brs for j in range(i + 1)]
                CHUNKS += [(k, blocks[x:x + 2]) for x in range(0, len(blocks), 2)]

        HIDDEN_BANK = ((0, 6), (5, 7))

        def chunks_of(k):
            return [(x, blocks) for x, (kk, blocks) in enumerate(CHUNKS) if kk == k]

        def pieces_through(k):
            return chunks_of(k)[-1][0] + 1

        def before(k):
            same = [n for n in range(k) if STEPS[n][5] == STEPS[k][5]]
            return same[-1] if same else None

        LAST_PROMPT = max(k for k in range(NSTEP) if STEPS[k][0] is not None)

        ENDS = [k for k in range(NSTEP) if STEPS[k][4] == (0,)]

        def outputs_before(k):
            return sum(e < k for e in ENDS)

        def parts_of(k):
            return STEPS[k][3] * len(STEPS[k][4])

        def width_of(k):
            i, _, _, _, brs, _ = STEPS[k]
            if i is None:
                return P if brs == (0,) else PAST + NS
            return NCP if brs == (0,) else (i + 1) * P

        def parted(cols, k):
            if STEPS[k][0] is None:
                return cols[:, 0:width_of(k)].unsqueeze(1)
            n = parts_of(k)
            pitch = 64 if STEPS[k][4] == (0,) else 512 if width_of(k) > 256 else width_of(k)
            return cols[:, 0:n * pitch].rearrange("p (r n) -> p r n", r=n)[:, :, 0:width_of(k)]

        def score(k):
            a, b = ((0, 1), (1, 3), (3, 5))[STEPS[k][5]]
            return parted(ps[:, a:b, :].rearrange("p a n -> p (a n)"), k)

        def prob(k):
            region = STEPS[k][5]
            return parted(Pc if region == 0 else Pt[:, region - 1, :], k)

        def exp_turn(n):
            return n - 3 if before(n) is None else max(n - 3, before(n))

        def own_total(k):
            return STEPS[k][0] is None or STEPS[k][4] != (0,)

        def scaled_through(k):
            return sum(own_total(n) for n in range(k + 1))

        def evac_shape(k, blocks):
            i, _, _, heads, _, _ = STEPS[k]
            return (P if i is None or blocks[0][0] else NCP), len(blocks) * heads * P

        def evac_on_act(x):
            k = CHUNKS[x][0]
            return STEPS[k][0] is None or chunks_of(k)[0][0] != x

        def read_out(eng, key):
            q = GROUP[key]
            eng.wait_ge(pair_free[q % 4], q // 4 + 1)

        def unit_used(eng, n):
            kind, m = UNITS[n]
            if kind == "tm" and m < KC - 1:
                eng.wait_ge(tm_used, m + 1)
            elif kind == "w1":
                eng.wait_ge(w1_used, m + 1)
            elif UNITS[n] in SPLIT:
                eng.wait_ge(wl_ready, SPLIT[UNITS[n]] + 1)
            else:
                group = ("tm", TT) if kind == "tm" else (kind, m)
                eng.wait_ge(pair_done, GROUP[group] + 1)

        def split_used(eng, n):
            kind, m = SPLITS[n]
            if kind != "dn":
                eng.wait_ge(pair_done, GROUP[("b", m) if kind == "ab" else SPLITS[n]] + 1)
            else:
                f, u = divmod(m, NFH)
                if u < NFH - 1:
                    eng.wait_ge(dn_used, f * (NFH - 1) + u + 1)
                else:
                    eng.wait_ge(pair_done, GROUP[("dn", f * KC + KC - 1)] + 1)

        def late_events():
            for m in range(KC):
                yield from (("unit", ("ga", m)), ("group", ("ga", m)), ("unit", ("gb", m)), ("group", ("gb", m)),
                            ("group", ("a", m)), ("unit", ("ab", m)), ("group", ("b", m)))
            for m in range(KC):
                yield from (("unit", ("out", m)), ("group", ("out", m)))
            for f in range(2):
                for m in range(f * NFH, (f + 1) * NFH):
                    for w in ("fg", "fu"):
                        yield from (("unit", (w, m)), ("group", (w, m)))
                for c in range(KC * NFH):
                    if c % 8 == 0:
                        yield "unit", ("dn", f * NFH + c // 8)
                    if c % NFH == NFH - 1:
                        yield "group", ("dn", f * KC + c // NFH)

        with nc.Fori(0, DEPTH) as layer:
            with nc.Block() as block:
                @block.sync
                def _(sp):
                    parameters = small_in[bass.ds(layer, 1)].rearrange("l p n -> (l p) n")
                    sp.dma_start(small[:, 0:SMALL_FIRST], parameters[:, 0:SMALL_FIRST]).then_inc(scales_landed, 16)

                    def unit(n):
                        if n >= RING:
                            unit_used(sp, n - RING)
                        sp.dma_start(ring[:, n % RING, :],
                                     W_in[bass.ds(layer, 1), n].rearrange("l p n -> (l p) n")).then_inc(unit_landed[n % RING], 16)

                    unit(0)
                    sp.dma_start(small[:, SMALL_FIRST:SMALL_W], parameters[:, SMALL_FIRST:SMALL_W]).then_inc(small_landed, 16)
                    for n in range(1, len(UNITS)):
                        unit(n)
                    sp.wait_ge(stored, 32)
                    sp.wait_ge(u_stored, 16)
                    sp.wait_ge(mix_stored, 32)
                    sp.wait_ge(cstored, 16 * MH)
                    sp.wait_ge(raw_stored, 32)
                    sp.wait_ge(nsa_stored, 48)

                @block.gpsimd
                def _(pool):
                    pool.dma_start(oldwin_out[bass.ds(layer, 1)].rearrange("l b n -> (l b) n"),
                                   cwin_in[bass.ds(layer, 1)].rearrange("l b n -> (l b) n")[:, DECT * 2 * P:PAST * 2 * P]).then_inc(stored, 16)

                    def load_c0(h):
                        pool.dma_start(Cst[:, h % 2, :, :].rearrange("p b e -> p (b e)"),
                                       c0_in[bass.ds(layer, 1), h].rearrange("l p n -> (l p) n")).then_inc(c0_landed[h % 2], 16)

                    load_c0(0)
                    load_c0(1)
                    pool.wait_ge(small_landed, 16)
                    pool.memset(upad[:, :, 0:CONV - 1], 0.0)
                    us = upad[:, :, CONV - 1 + SEQ:UW].rearrange("p c (b t) -> p c b t", b=DECB)
                    cs = sml("cs", "p (c b t) -> p c b t", c=4, b=DECB)
                    for c in range(4):
                        last = pool.tensor_copy(us[:, c, :, 0:CONV - 1], cs[:, c])
                    last.then_inc(history_ready, 1)
                    pool.wait_ge(history_ready, 1)
                    for m in range(4):
                        read_out(pool, ("u", m))
                    pool.dma_start(u_out[bass.ds(layer, 1)].rearrange("l p c n -> (l p) c n"), upad[:, :, SEQ:UW]).then_inc(u_stored, 16)
                    pool.wait_ge(rows_ready, 1)
                    pool.dma_start(m_out[bass.ds(layer, 1)].rearrange("l p n -> (l p) n"), row(M_)).then_inc(mix_stored, 16)
                    def values_by_seq(h):
                        if h >= 1:
                            pool.wait_ge(cs_done, h)
                        v = vtm[0:NS, TT, h * MD:(h + 1) * MD]
                        pool.tensor_tensor(vb[0:NS], bc(v.unsqueeze(1), [NS, DECB, MD]), bc(con("blk")[0:NS, :].unsqueeze(2), [NS, DECB, MD]),
                                           ALU.mult).then_inc(vb_ready, 1)

                    pool.wait_ge(mix_stored, 16)
                    pool.wait_ge(wexp_ready, 1)
                    for i in range(TT):
                        read_out(pool, ("kw", i))
                    pool.tensor_tensor(kwsum, kw[:, 0, :], kw[:, 1, :], ALU.add).then_inc(kw_summed, 1)
                    for i in range(2, TT):
                        pool.wait_ge(kw_summed, i - 1)
                        pool.tensor_tensor(kwsum, kwsum, kw[:, i, :], ALU.add).then_inc(kw_summed, 1)
                    read_out(pool, ("tm", TT))
                    pool.wait_ge(const_landed, 16)
                    values_by_seq(0)
                    for h in range(MH):
                        pool.wait_ge(bc_ready, 2 * h + 2)
                        pool.wait_ge(c0_landed[h % 2], 16 * (h // 2 + 1))
                        pool.wait_ge(nd_done, (h + 1) * (TT + 1))
                        C = Cst[:, h % 2]
                        dec = per_seq(inter[:, h % 2, :])[:, :, DECT - 1:DECT]
                        pool.tensor_tensor(C, C, bc(dec, [P, DECB, MD]), ALU.mult).then_inc(c_decayed, 1)
                        if h + 1 < MH:
                            values_by_seq(h + 1)
                        pool.wait_ge(head_fin, h + 1)
                        pool.dma_start(sC_out[bass.ds(layer, 1), h].rearrange("l p n -> (l p) n"),
                                       Cst[:, h % 2, :, :].rearrange("p b e -> p (b e)")).then_inc(cstored, 16)
                        if h + 2 < MH:
                            pool.wait_ge(cstored, 16 * (h + 1))
                            load_c0(h + 2)
                    pool.wait_ge(cstored, 16 * MH)
                    pool.wait_ge(pc_ready, 1)
                    pool.wait_ge(pn_ready, 1)
                    pool.dma_start(pC_out[bass.ds(layer, 1)].rearrange("l p n -> (l p) n"),
                                   pCs.rearrange("p h e -> p (h e)")).then_inc(mix_stored, 16)
                    pool.dma_start(pn_out[bass.ds(layer, 1)].rearrange("l p n -> (l p) n"),
                                   nstat[:, :, :].rearrange("p h b -> p (h b)")).then_inc(stored, 16)
                    pool.wait_ge(mix_stored, 32)
                    pool.wait_ge(ha_ready, MH)
                    pes = sml("pe", "p (v h l) -> p v l h", v=2, h=2)
                    for v in range(2):
                        last = pool.tensor_copy(raw[:, v, :, NBLK:NBLK + 2], pes[:, v])
                    last.then_inc(raw_ready, 1)

                    pool.wait_ge(table_landed, 16)

                    def page_of(n):
                        page = pool.value_load(table[0:1, n:n + 1], min_val=0, max_val=pages_in.shape[1] - 1)
                        return pages_in[bass.ds(layer, 1), bass.ds(page, 1)].rearrange("l a p n -> (l a p) n")

                    for n in range(DECB * NPG):
                        if n >= 4:
                            pool.wait_ge(page_arranged, n - 3)
                        pool.dma_start(stage[:, n % 4, :, :], page_of(n)[:, 0:2 * PAGE].rearrange("p (v s) -> p v s", v=2)).then_inc(page_landed[n % 4], 16)
                    pool.wait_ge(pair_done, ATTN_AT)
                    pool.memset(qb[:, :, :, :], 0.0).then_inc(qb_cleared, 1)
                    pool.wait_ge(w1_used, 8)
                    pool.wait_ge(rope_ready, 6)
                    pool.dma_start(raw_out[bass.ds(layer, 1)].rearrange("l p v i n -> (l p) (v i) n"),
                                   raw[:, :, :, 0:PBLK].rearrange("p v l n -> p (v l) n")).then_inc(raw_stored, 16)
                    pool.dma_start(knew_out[bass.ds(layer, 1)].rearrange("l p v n -> (l p) v n"), knew).then_inc(raw_stored, 16)
                    pool.wait_ge(raw_stored, 32)
                    pool.dma_start(winp, win_in[bass.ds(layer, 1)].rearrange("l p (b v j s) -> (l p) b v j s", b=DECB, v=2, j=NPG)).then_inc(win_landed, 16)
                    pool.wait_ge(cmp_ready, 1)
                    for n in range(DECB * NPG):
                        b, j = divmod(n, NPG)
                        pool.dma_start(selp[:, b, j, :, :],
                                       page_of(n)[:, 2 * PAGE:4 * PAGE].rearrange("p (v s) -> p v s", v=2)).then_inc(sel_landed, 16)
                    pool.dma_start(fm_out[bass.ds(layer, 1)].rearrange("l p v n -> (l p) v n"), kT).then_inc(nsa_stored, 16)
                    tmo = tm_out[bass.ds(layer, 1)].rearrange("l p i n -> (l p) i n")
                    pool.dma_start(tmo[:, 0:TT, :], vkv[:, 0:TT, :]).then_inc(nsa_stored, 16)
                    pool.dma_start(tmo[0:NS, TT, :], vkv[0:NS, TT, :]).then_inc(nsa_stored, 16)
                    pool.wait_ge(stored, 32)
                    pool.wait_ge(nsa_stored, 48)
                    pool.wait_ge(win_landed, 16)
                    pool.wait_ge(sel_landed, 16 * DECB * NPG)
                    pool.dma_reset()

                @block.tensor
                def _(pe):
                    def landed(key):
                        n = UNIT[key]
                        pe.wait_ge(unit_landed[n % RING], 16 * (n // RING + 1))
                        return ring[:, n % RING, :]

                    def begin(key):
                        q = GROUP[key]
                        if q >= 4:
                            pe.wait_ge(pair_free[q % 4], q // 4)
                        return pair(q)

                    def drained(q):
                        for s in range(4):
                            pe.wait_ge(pair_free[s], (q - s + 3) // 4)

                    def product(key, unit_key, src, kcs, ready=None):
                        w = landed(unit_key).rearrange("p (k m) -> p k m", m=P)
                        out = begin(key)
                        for k in range(kcs):
                            if ready is not None:
                                pe.wait_ge(ready[0], ready[1] + k + 1)
                            for a in range(2):
                                mm = pe.matmul(out[:, a, :], w[:, k, :], src[:, k, a * NHALF:(a + 1) * NHALF],
                                               start=(k == 0), stop=(k == kcs - 1))
                        return mm

                    def norm_sum(key, base):
                        out = begin(key)
                        if base is not None:
                            pe.wait_ge(sq_used, base + KC - 1)
                        for a in range(2):
                            mm = pe.matmul(out[:, a, :], ones[:, :], acc[:, a * NHALF:(a + 1) * NHALF], start=True, stop=True)
                        mm.then_inc(pair_done, 1)

                    def product3(key, unit_key, hi, lo, ready=None):
                        n = SPLIT[unit_key]
                        pe.wait_ge(wl_ready, n + 1)
                        out = begin(key)
                        for k in range(KC):
                            if ready is not None:
                                pe.wait_ge(ready[0], ready[1] + k + 1)
                            mm = passes(out, n, k, hi[:, k, :], lo[:, k, :], k == 0, k == KC - 1)
                        return mm

                    def branch_product(kind, m, hi, lo, first, ready):
                        n = SPLIT[("ab", m)]
                        pe.wait_ge(wl_ready, n + 1)
                        out = begin((kind, m))
                        for k in range(4):
                            pe.wait_ge(ready, k + 1)
                            mm = passes(out, n, first + k, hi[k], lo[:, k, :], k == 0, k == 3)
                        return mm

                    def passes(out, n, k, hi, lo, first, last):
                        wh, wl, _ = split_weights(n)
                        for w, x, start, stop in ((wh, hi, first, False), (wh, lo, False, False), (wl, hi, False, last)):
                            for a in range(2):
                                mm = pe.matmul(out[:, a, :], w[:, k * P:(k + 1) * P], x[:, a * NHALF:(a + 1) * NHALF],
                                               start=start, stop=stop)
                        return mm

                    norm_sum(("n1", 0), None)
                    def fm(kind, m, src=hT, kcs=KC, ready=None):
                        product((kind, m), (kind, m), src, kcs, ready=ready).then_inc(pair_done, 1)

                    for m in range(4):
                        fm("u", m, ready=(h_ready, 0))
                    for i in range(TT + 1):
                        rows = P if i < TT else NS
                        q = GROUP[("tm", i)]
                        begin(("tm", i))
                        s = 2 * (q % 4)
                        for k in range(KC):
                            w = landed(("tm", k))
                            x = hT[:, k, i * P:i * P + rows]
                            pe.matmul(ps[0:rows, s, :], x, w[:, 0:512], start=(k == 0), stop=(k == KC - 1))
                            mm = pe.matmul(ps[0:rows, s + 1, 0:280], x, w[:, 512:TMC], start=(k == 0), stop=(k == KC - 1))
                            if i == TT and k < KC - 1:
                                mm.then_inc(tm_used, 1)
                        mm.then_inc(pair_done, 1)

                    w = landed(("if", 0)).rearrange("p (k m) -> p k m", k=KC)
                    out = begin(("if", 0))
                    for k in range(KC):
                        for a in range(2):
                            mm = pe.matmul(out[0:64, a, :], w[:, k, 0:64], hT[:, k, a * NHALF:(a + 1) * NHALF],
                                           start=(k == 0), stop=(k == KC - 1))
                    mm.then_inc(pair_done, 1)
                    def fm3(kind, m):
                        product3((kind, m), (kind, m), xh, xl).then_inc(pair_done, 1)

                    for m in range(4):
                        product3(("o", m), ("o", m), xh, xl, (xl_ready, 0)).then_inc(pair_done, 1)
                    pe.wait_ge(small_landed, 16)
                    for h in range(MH):
                        for name in ("mq", "mk"):
                            w = sml("w" + name, "p (h m) -> p h m", h=MH)[:, h, :]
                            out = begin((name, h))
                            pe.wait_ge(c_ready, h + 1)
                            for a in range(2):
                                mm = pe.matmul(out[:, a, :], w, cT[:, h, a * NHALF:(a + 1) * NHALF], start=True, stop=True)
                            mm.then_inc(pair_done, 1)
                    pe.wait_ge(const_landed, 16)
                    begin(("aw", 0))
                    s = 2 * (GROUP[("aw", 0)] % 4)
                    aw = ps[:, s, 0:(TT + 1) * 2 * MH].rearrange("p (i a h) -> p i a h", i=TT + 1, a=2)
                    pe.wait_ge(wexp_ready, 1)
                    for i in range(TT + 1):
                        rows = P if i < TT else NS
                        for a, r in enumerate((A_, W_)):
                            mm = pe.transpose(aw[0:rows, i, a, :], row(r)[:, i * P:i * P + rows], ident[0:MH, 0:MH])
                    mm.then_inc(pair_done, 1)
                    for i in range(TT + 1):
                        rows = P if i < TT else NS
                        begin(("kw", i))
                        s = 2 * (GROUP[("kw", i)] % 4)
                        wk = sml("wmk", "p (h m) -> p h m", h=MH)
                        for h in range(MH):
                            mm = pe.matmul(ps[0:rows, s, h * MD:(h + 1) * MD], cT[:, h, i * P:i * P + rows], wk[:, h, :],
                                           start=True, stop=True)
                        mm.then_inc(pair_done, 1)
                    drained(CORE_AT)

                    def spread(h, which):
                        x = 2 * h + which
                        if x >= 1:
                            pe.wait_ge(bc_ready, x)
                        r = row(G_) if which == 0 else row(EN_)
                        for a in range(2):
                            mm = pe.matmul(ps[:, 6 + a, 0:NHALF], sel4[0:MH, h, :], r[:, a * NHALF:(a + 1) * NHALF],
                                           start=True, stop=True)
                        if which == 1:
                            mm = pe.matmul(ps[:, 6, NHALF:NHALF + NS], sel4[0:MH, h, :], introw, start=True, stop=True)
                        mm.then_inc(bc_done, 1)

                    def scores(k):
                        h, j = divmod(k, TT + 1)
                        if k >= 2:
                            pe.wait_ge(st_ready, k - 1)
                        if j < TT:
                            mm = pe.matmul(ps[:, k % 2, 0:SEQ - j * P], km[:, h, j * P:(j + 1) * P], qm[:, h, j * P:SEQ],
                                           start=True, stop=True)
                        else:
                            mm = pe.matmul(ps[0:NS, k % 2, 0:NS], km[:, h, SEQ:N], qm[:, h, SEQ:N], start=True, stop=True)
                        mm.then_inc(ms_done, 1)

                    def numden(k):
                        h, j = divmod(k, TT + 1)
                        if j == 0 and h >= 1:
                            pe.wait_ge(num_copied, h)
                            pe.wait_ge(den_read, h)
                        pe.wait_ge(st_ready, k + 1)
                        if j < TT:
                            s = St[:, k % 2, 0:SEQ - j * P]
                            pe.matmul(ps[:, 2, j * P:SEQ], vtm[:, j, h * MD:(h + 1) * MD], s, start=(j == 0), stop=(j == TT - 1))
                            mm = pe.matmul(ps[:, 3, j * P:SEQ], ones[:, :], s, start=(j == 0), stop=(j == TT - 1))
                        else:
                            s = St[0:NS, k % 2, 0:NS]
                            pe.matmul(ps[:, 4, 0:NS], vtm[0:NS, TT, h * MD:(h + 1) * MD], s, start=True, stop=False)
                            pe.wait_ge(qi_ready, h + 1)
                            pe.wait_ge(c0_landed[h % 2], 16 * (h // 2 + 1))
                            for b in range(DECB):
                                pe.matmul(ps[:, 4, b * DECT:(b + 1) * DECT], Cst[:, h % 2, b, :], qi[:, 0, b * DECT:(b + 1) * DECT],
                                          start=False, stop=(b == DECB - 1))
                            pe.matmul(ps[:, 4, NS:2 * NS], ones[0:NS, :], s, start=True, stop=False)
                            mm = pe.matmul(ps[:, 4, NS:2 * NS], ones[:, :], qi[:, 1, :], start=False, stop=True)
                        mm.then_inc(nd_done, 1)

                    def new_state(h):
                        pe.wait_ge(vb_ready, h + 1)
                        pe.wait_ge(bc_ready, min(2 * h + 4, 2 * MH))
                        k = kw[0:NS, TT, h * MD:(h + 1) * MD]
                        for a in range(2):
                            pe.matmul(ps[:, 6 + a, :], k, vb[0:NS, 4 * a:4 * a + 4, :], start=True, stop=True)
                        mm = pe.matmul(ps[:, 5, 0:DECB], k, con("blk")[0:NS, :], start=True, stop=True)
                        mm.then_inc(cs_done, 1)

                    nk = MH * (TT + 1)
                    spread(0, 0)
                    spread(0, 1)
                    scores(0)
                    for k in range(nk):
                        h, j = divmod(k, TT + 1)
                        if k + 1 < nk:
                            scores(k + 1)
                        if j == 2 and h + 1 < MH:
                            if h >= 1:
                                pe.wait_ge(head_fin, h)
                            spread(h + 1, 0)
                            spread(h + 1, 1)
                        numden(k)
                        if j == TT:
                            new_state(h)
                    pe.wait_ge(st_ready, nk)
                    pe.wait_ge(kw_summed, TT - 1)
                    for h in range(MH):
                        hd = slice(h * MD, (h + 1) * MD)
                        for i in range(TT):
                            pe.matmul(ps[:, 0, hd], kw[:, i, hd], vtm[:, i, hd], start=(i == 0), stop=(i == TT - 1))
                        mm = pe.matmul(ps[:, 1, h:h + 1], kwsum[:, hd], ones[:, 0:1], start=True, stop=True)
                    mm.then_inc(pc_done, 1)
                    pe.wait_ge(head_fin, MH)
                    pe.wait_ge(pc_ready, 1)
                    pe.wait_ge(pn_ready, 1)
                    for h in range(MH):
                        q = GROUP[("mn", h)]
                        begin(("mn", h))
                        pe.wait_ge(msq_ready, h + 1)
                        for a in range(2):
                            mm = pe.matmul(pair(q)[:, a, :], ones[:, :], sq[:, h % 2, a * NHALF:(a + 1) * NHALF], start=True, stop=True)
                        mm.then_inc(pair_done, 1)
                    for m in range(4):
                        fm3("q", m)
                    for kind, n in QK_TAIL:
                        if kind == "k":
                            fm3("k", n)
                            continue
                        out = begin(("rope", n))
                        src = qT[:, n, :] if n < 4 else kT[:, n - 4, :]
                        read_out(pe, ("q", n) if n < 4 else ("k", n - 2))
                        for a in range(2):
                            mm = pe.matmul(out[:, a, :], rot, src[:, a * NHALF:(a + 1) * NHALF], start=True, stop=True)
                        mm.then_inc(pair_done, 1)

                    def att_scores(k):
                        i, g, r0, heads, brs, _ = STEPS[k]
                        if before(k) is not None:
                            pe.wait_ge(exp_done, before(k) + 1)
                        hd = slice(g * HD, (g + 1) * HD)
                        out = score(k).rearrange("p (r b) n -> p r b n", r=heads)
                        for r in range(heads):
                            if brs == (0,):
                                mm = pe.matmul(out[:, r, 0, :], qT[hd, r0 + r, i * P:(i + 1) * P], kcT[hd, 0:NCP], start=True, stop=True)
                            else:
                                mm = pe.matmul(out[:, r], qrT[hd, r0 + r, i * P:(i + 1) * P], kT[hd, brs[0] - 1:brs[-1], 0:(i + 1) * P],
                                               start=True, stop=True)
                        mm.then_inc(s_done, 1)

                    def att_turn(k):
                        _, _, _, heads, brs, _ = STEPS[k]
                        if own_total(k):
                            pe.wait_ge(p_ready, scaled_through(k))
                        else:
                            pe.wait_ge(cp_ready, k + 1 - scaled_through(k))
                        rows = NCP if brs == (0,) else P
                        for x, blocks in chunks_of(k):
                            if x >= 2:
                                pe.wait_ge(t_free[x % 2], x // 2)
                            at = 0
                            for br, j in blocks:
                                for r in range(heads):
                                    part = prob(k)[:, r * len(brs) + brs.index(br), j * P:j * P + rows]
                                    mm = pe.transpose(ps[0:rows, 5 + x % 2, at:at + P], part, ident)
                                    at += P
                            mm.then_inc(t_done, 1)

                    def att_out(k):
                        i, g, r0, heads, brs, _ = STEPS[k]
                        if k and k - 1 in ENDS:
                            pe.wait_ge(hb_ready, outputs_before(k))
                        hd = slice(g * HD, (g + 1) * HD)
                        out = ps[hd, 7, r0 * P:(r0 + 2) * P]
                        for x, blocks in chunks_of(k):
                            pe.wait_ge(t_free[x % 2], x // 2 + 1)
                            for c, (br, j) in enumerate(blocks):
                                if br == 0:
                                    for h in range(0, R, 2):
                                        mm = pe.matmul(ps[hd, 7, h * P:(h + 2) * P], vcp[0:NCP, hd], PT[0:NCP, x % 2, h * P:(h + 2) * P],
                                                       start=False, stop=(h == R - 2))
                                else:
                                    mm = pe.matmul(out, vkv[:, j, (br - 1) * P + g * HD:(br - 1) * P + (g + 1) * HD],
                                                   PT[:, x % 2, 2 * c * P:2 * (c + 1) * P], start=(br == 1 and j == 0 and r0 == 0), stop=False)
                            mm.then_inc(o_done, 1)

                    def samp_scores(k):
                        _, hb, _, _, (br,), _ = STEPS[k]
                        pe.wait_ge(exp_done, before(k) + 1)
                        if br == 1:
                            pe.wait_ge(qb_ready, 1)
                            pe.wait_ge(sel_landed, 16 * DECB * NPG)
                        elif br == 2:
                            pe.wait_ge(win_landed, 16)
                        for b4 in range(4):
                            b = 4 * hb + b4
                            o = ps[32 * b4:32 * b4 + 32, (0, 1, 3)[br], :]
                            if br == 0:
                                mm = pe.matmul(o[:, 0:P], qb[:, 0, b, :], kcT[:, PBLK:NBLK], start=True, stop=True)
                            else:
                                past = selp[:, b, :, 0, :] if br == 1 else winp[:, b, 0, :, :]
                                pe.matmul(o[:, 0:PAST], qb[:, 1, b, :], past, start=True, stop=True)
                                mm = pe.matmul(o[:, PAST:PAST + NS], qb[:, 1, b, :], kT[:, br - 1, SEQ:N], start=True, stop=True)
                        mm.then_inc(s_done, 1)

                    def samp_turn(k):
                        br = STEPS[k][4][0]
                        x = chunks_of(k)[0][0]
                        pe.wait_ge(p_ready, scaled_through(k))
                        pe.wait_ge(t_free[x % 2], x // 2)
                        for j in range(1 if br == 0 else 3):
                            rows = NS if j == 2 else P
                            mm = pe.transpose(ps[0:rows, 5 + x % 2, j * P:(j + 1) * P], prob(k)[:, 0, j * P:j * P + rows], ident)
                        mm.then_inc(t_done, 1)

                    def samp_out(k):
                        _, hb, _, _, (br,), _ = STEPS[k]
                        x = chunks_of(k)[0][0]
                        if k - 1 in ENDS:
                            pe.wait_ge(hb_ready, outputs_before(k))
                        pe.wait_ge(t_free[x % 2], x // 2 + 1)
                        if br == 0:
                            mm = pe.matmul(ps[:, 7, 0:P], vcs, PT[:, x % 2, 0:P], start=False, stop=True)
                        else:
                            pe.matmul(ps[:, 7, 0:P], vkv[0:NS, TT, (br - 1) * P:br * P], PT[0:NS, x % 2, 2 * P:3 * P], start=(br == 1), stop=False)
                            for b4 in range(4):
                                b = 4 * hb + b4
                                for j in range(NPG):
                                    v = selp[:, b, j, 1, :] if br == 1 else winp[:, b, 1, j, :]
                                    mm = pe.matmul(ps[:, 7, 32 * b4:32 * b4 + 32], v, PT[:, x % 2, j * P + 32 * b4:j * P + 32 * b4 + 32],
                                                   start=False, stop=False)
                        mm.then_inc(o_done, 1)

                    def compress(v):
                        for u in range(4):
                            w = landed(("w1", 4 * v + u)).rearrange("p (l e) -> p l e", e=HID)
                            for l8 in range(8):
                                l = 8 * u + l8
                                second, l16 = divmod(l, STRIDE)
                                for g in range(NKV):
                                    x = raw[g * HD:(g + 1) * HD, v, l16, second:second + NBLK + 1]
                                    mm = pe.matmul(ps[:, HIDDEN_BANK[v][g], 0:NBLK + 1], w[g * HD:(g + 1) * HD, l8, :], x,
                                                   start=(l == 0), stop=(l == CLEN - 1))
                            mm.then_inc(w1_used, 1)

                    read_out(pe, ("rope", 2))
                    read_out(pe, ("k", 0))
                    pe.wait_ge(raw_ready, 1)
                    pe.wait_ge(page_arranged, DECB * NPG)
                    compress(0)
                    drained(ATTN_AT)
                    for hb in range(2):
                        mm = pe.matmul(ps[:, 7, hb * 24:(hb + 1) * 24], tsel[0:NS, hb, :], gate[0:NS, TT, :], start=True, stop=True)
                    mm.then_inc(gs_done, 1)
                    pe.wait_ge(rope_ready, 6)
                    att_scores(0)
                    att_scores(1)
                    pe.wait_ge(gs_read, 1)
                    compress(1)
                    w2 = sml("w2", "p (v f) -> p v f", v=2)
                    pe.wait_ge(hid_ready, 1)
                    for g in range(NKV):
                        pe.matmul(ps[g * HD:(g + 1) * HD, 0, 0:NBLK], w2[:, 0, :], hid[:, 0, g, :], start=True, stop=True)
                    pe.wait_ge(hid_ready, 2)
                    for g in range(NKV):
                        pe.matmul(ps[0:NCP, 5, g * HD:(g + 1) * HD], hid[:, 1, g, 0:NCP], w2[:, 1, :], start=True, stop=True)
                        mm = pe.matmul(ps[:, 5, P + g * HD:P + (g + 1) * HD], hid[:, 1, g, PBLK:NBLK], w2[:, 1, :], start=True, stop=True)
                    mm.then_inc(cmp_done, 1)
                    pe.wait_ge(cmp_ready, 1)
                    att_scores(2)
                    for k in range(NSTEP):
                        (samp_turn if STEPS[k][0] is None else att_turn)(k)
                        if k + 3 < NSTEP:
                            (samp_scores if STEPS[k + 3][0] is None else att_scores)(k + 3)
                        (samp_out if STEPS[k][0] is None else att_out)(k)
                    pe.wait_ge(exp_done, NSTEP)
                    pe.wait_ge(hb_ready, len(ENDS))
                    for m in range(KC):
                        product3(("ga", m), ("ga", m), xh, xl).then_inc(pair_done, 1)
                        product3(("gb", m), ("gb", m), xh, xl).then_inc(pair_done, 1)
                        branch_product("a", m, ha_high, ha_low, 0, ha_low_ready).then_inc(pair_done, 1)
                        branch_product("b", m, hb_high, hb_low, MH, hb_low_ready).then_inc(pair_done, 1)
                    for m in range(KC):
                        product3(("out", m), ("out", m), mh, ml, (merged_ready, 0)).then_inc(pair_done, 1)
                    norm_sum(("n2", 0), 0)
                    for f in range(2):
                        for m in range(f * NFH, (f + 1) * NFH):
                            for w in ("fg", "fu"):
                                product3((w, m), (w, m), xh, xl, (xl_ready, KC)).then_inc(pair_done, 1)
                        for m in range(KC):
                            out = begin(("dn", f * KC + m))
                            for k in range(NFH):
                                u, c = divmod(m * NFH + k, 8)
                                n = SPLIT[("dn", f * NFH + u)]
                                pe.wait_ge(wl_ready, n + 1)
                                pe.wait_ge(act_ready, f * NFH + k + 1)
                                mm = passes(out, n, c, ah[:, k, :], al(k), k == 0, k == NFH - 1)
                                if c == 7 and u < NFH - 1:
                                    mm.then_inc(dn_used, 1)
                            mm.then_inc(pair_done, 1)

                @block.scalar
                def _(act):
                    steps = [0]

                    def link(ins):
                        steps[0] += 1
                        ins.then_inc(act_step, 1)
                        act.wait_ge(act_step, steps[0])

                    def done(key):
                        q = GROUP[key]
                        act.wait_ge(pair_done, q + 1)
                        return pair(q), pair_free[q % 4]

                    def square(k, base):
                        if k == 0:
                            act.activation(acc[:, :], xT[:, 0, :], ACT.Square).then_inc(sq_ready, 1)
                            return
                        if k >= 3:
                            act.wait_ge(sq_used, base + k - 2)
                        act.activation(sq[:, k % 2, :], xT[:, k, :], ACT.Square).then_inc(sq_ready, 1)

                    def split_high(n):
                        if n >= len(SPLITS):
                            return
                        hi, _, slots = split_weights(n)
                        if n not in (0, 1, QSPLIT, QSPLIT + 1, LSPLIT, LSPLIT + 1, LSPLIT + 2):
                            split_used(act, n - slots)
                        u = UNIT[SPLITS[n]]
                        act.wait_ge(unit_landed[u % RING], 16 * (u // RING + 1))
                        act.copy(hi, ring[:, u % RING, :]).then_inc(wh_ready, 1)

                    def root(key):
                        out, free = done(key)
                        act.activation(halves(rstd[:, :]), out, ACT.Sqrt, bias=eps[:, :], scale=1.0 / D).then_inc(free, 1)

                    root(("n1", 0))
                    for m in range(4):
                        out, free = done(("u", m))
                        act.copy(upad[:, m, 3:3 + NHALF], out[:, 0, :])
                        act.copy(upad[:, m, 3 + NHALF:3 + SEQ], out[:, 1, 0:SEQ - NHALF])
                        us = upad[:, m, 3 + SEQ:UW].rearrange("p (b t) -> p b t", b=DECB)
                        act.copy(us[:, :, 3:7], out[:, 1, SEQ - NHALF:NHALF].rearrange("p (b t) -> p b t", b=DECB)).then_inc(free, 1)
                    for k in range(KC):
                        act.wait_ge(h_ready, k + 1)
                        act.copy(xh[:, k, :], hT[:, k, :]).then_inc(xh_ready, 1)
                    for i in range(TT + 1):
                        rows = P if i < TT else NS
                        done(("tm", i))
                        q = GROUP[("tm", i)]
                        s = 2 * (q % 4)
                        act.activation(gate[0:rows, i, :], ps[0:rows, s + 1, 2 * P:2 * P + 24], ACT.Sigmoid)
                        act.copy(vkv[0:rows, i, :], ps[0:rows, s + 1, 0:2 * P])
                        act.copy(vtm[0:rows, i, :], ps[0:rows, s, :]).then_inc(pair_free[q % 4], 1)
                        if i < 4:
                            act.wait_ge(conv_ready, i + 1)
                            act.activation(cT[:, i, :], ctmp[:, i % 2, :], ACT.Silu).then_inc(c_ready, 1)
                    split_high(0)
                    split_high(1)
                    out, free = done(("if", 0))
                    act.wait_ge(small_landed, 16)
                    act.activation(halves(row(I_)), out[0:MH], ACT.Identity, bias=sml("bi")[0:MH, :])
                    act.copy(halves(row(A_)), out[32:32 + MH]).then_inc(free, 1)
                    read_out(act, ("if", 0))
                    link(act.activation(row(Z_), row(A_), ACT.Identity, bias=sml("bf")[0:MH, :]))
                    link(act.activation(row(L_), row(Z_), ACT.Abs))
                    link(act.activation(row(A_), row(L_), ACT.Exp, scale=-1.0))
                    act.activation(row(L_), row(A_), ACT.Ln, bias=ones[0:MH, 0:1]).then_inc(ln_ready, 1)
                    for m in range(4):
                        if m < 2:
                            split_high(m + 2)
                        out, free = done(("o", m))
                        act.activation(halves(haT[:, m, :]), out, ACT.Sigmoid).then_inc(free, 1)
                    act.wait_ge(rows_ready, 1)
                    act.activation(row(W_)[:, 0:SEQ], row(A_)[:, 0:SEQ], ACT.Exp, bias=row(G_)[:, SEQ - 1:SEQ])
                    act.activation(row(W_)[:, SEQ:N], tmprow, ACT.Exp)
                    act.activation(row(EN_), row(M_), ACT.Exp, scale=-1.0)
                    act.activation(introw, introw, ACT.Exp).then_inc(wexp_ready, 1)
                    for h in range(MH):
                        for name, dst, scale in (("mq", qm, 1.0), ("mk", km, MD ** -0.5)):
                            out, free = done((name, h))
                            act.activation(halves(dst[:, h, :]), out, ACT.Copy, scale=scale).then_inc(free, 1)
                    act.wait_ge(pair_done, CORE_AT)
                    act.wait_ge(u_stored, 16)
                    read_out(act, ("aw", 0))

                    def spread(h):
                        if h >= 2:
                            act.wait_ge(head_fin, h - 1)
                        act.wait_ge(bc_done, 2 * h + 1)
                        act.copy(halves(gbc[:, h % 2, :]), ps[:, 6:8, 0:NHALF]).then_inc(bc_ready, 1)
                        act.wait_ge(bc_done, 2 * h + 2)
                        act.copy(inter[:, h % 2, :], ps[:, 6, NHALF:NHALF + NS])
                        act.copy(halves(enm[:, h % 2, :]), ps[:, 6:8, 0:NHALF]).then_inc(bc_ready, 1)

                    def copy_num(h):
                        act.wait_ge(nd_done, (h + 1) * (TT + 1))
                        act.copy(qm[:, h, 0:SEQ], ps[:, 2, :]).then_inc(num_copied, 1)

                    spread(0)
                    for k in range(MH * (TT + 1)):
                        h, j = divmod(k, TT + 1)
                        if j == 1 and h >= 1:
                            copy_num(h - 1)
                        if j == 3 and h + 1 < MH:
                            spread(h + 1)
                        if k >= 2:
                            act.wait_ge(st_ready, k - 1)
                        act.wait_ge(gm_ready, k + 1)
                        if j < TT:
                            if j < TT - 1:
                                act.wait_ge(bc_ready, 2 * h + 1)
                                act.activation(Et[:, k % 2, P:SEQ - j * P], gbc[:, h % 2, (j + 1) * P:SEQ], ACT.Exp, bias=awt[:, j, 0, h:h + 1])
                            act.activation(Et[:, k % 2, 0:P], gmask[:, k % 2, :], ACT.Exp, bias=awt[:, j, 0, h:h + 1]).then_inc(e_ready, 1)
                        else:
                            act.activation(Et[0:NS, k % 2, 0:NS], gmask[0:NS, k % 2, 0:NS], ACT.Exp, bias=awt[0:NS, j, 0, h:h + 1]).then_inc(e_ready, 1)
                    copy_num(MH - 1)
                    act.wait_ge(pc_done, 1)
                    act.copy(pCs, ps[:, 0, :].rearrange("p (h e) -> p h e", h=MH)).then_inc(pc_ready, 1)
                    split_high(QSPLIT)
                    split_high(QSPLIT + 1)
                    for h in range(MH):
                        if h >= 2:
                            act.wait_ge(pair_done, GROUP[("mn", h - 2)] + 1)
                        act.wait_ge(num_ready, h + 1)
                        act.activation(sq[:, h % 2, :], qm[:, h, :], ACT.Square).then_inc(msq_ready, 1)
                    for h in range(MH):
                        out, free = done(("mn", h))
                        if h >= 1:
                            act.wait_ge(ha_ready, h)
                        act.activation(halves(rstd[:, :]), out, ACT.Sqrt, bias=eps[:, :], scale=1.0 / MD).then_inc(free, 1)
                        if h:
                            split_high(QSPLIT + 1 + h)
                    act.wait_ge(ha_ready, MH)
                    act.wait_ge(mix_stored, 32)
                    act.wait_ge(cstored, 16 * MH)
                    for m in range(4):
                        if m == 1:
                            split_high(QSPLIT + 5)
                        out, free = done(("q", m))
                        act.activation(halves(qT[:, m, :]), out, ACT.Copy, scale=HD ** -0.5).then_inc(free, 1)
                    for n, m in enumerate(K_ORDER):
                        if n < 2:
                            split_high(QSPLIT + 6 + n)
                        out, free = done(("k", m))
                        if m < 2:
                            chunks = raw[:, m, :, :].rearrange("p l n -> p n l")
                            act.copy(chunks[:, 0:NHALF // STRIDE, :], out[:, 0, :].rearrange("p (n l) -> p n l", l=STRIDE))
                            act.copy(chunks[:, NHALF // STRIDE:PBLK, :], out[:, 1, 0:SEQ - NHALF].rearrange("p (n l) -> p n l", l=STRIDE))
                            act.copy(knew[:, m, :], out[:, 1, SEQ - NHALF:NHALF]).then_inc(free, 1)
                        else:
                            act.copy(halves(kT[:, m - 2, :]), out).then_inc(free, 1)
                    def att_exp(k):
                        act.wait_ge(max_ready, k + 1)
                        if before(k) is not None:
                            act.wait_ge(t_done, pieces_through(before(k)))
                        for r in range(parts_of(k)):
                            ins = act.activation(prob(k)[:, r, :], score(k)[:, r, :], ACT.Exp, bias=stat[:, k % 3, r:r + 1],
                                                 accum_out=stat[:, 3 + k % 3, r:r + 1] if own_total(k) else None)
                        ins.then_inc(exp_done, 1)

                    def att_scale(k):
                        if not own_total(k):
                            return
                        act.wait_ge(weight_ready, scaled_through(k))
                        for r in range(parts_of(k)):
                            ins = act.activation(prob(k)[:, r, :], prob(k)[:, r, :], ACT.Copy, scale=stat[:, 8 + k % 3, r:r + 1])
                        ins.then_inc(p_ready, 1)

                    def outputs(k):
                        i, g, _, _, _, _ = STEPS[k]
                        act.wait_ge(o_done, pieces_through(k))
                        if i is not None:
                            act.copy(hbT[g * HD:(g + 1) * HD, :, i * P:(i + 1) * P],
                                     ps[g * HD:(g + 1) * HD, 7, :].rearrange("p (r t) -> p r t", r=R)).then_inc(hb_ready, 1)
                        else:
                            for kv in range(NKV):
                                o = ps[kv * HD:(kv + 1) * HD, 7, 0:P].rearrange("p (b g r t) -> p b g r t", b=4, g=NKV, r=R)
                                d = hbT[kv * HD:(kv + 1) * HD, :, SEQ + 16 * g:SEQ + 16 * g + 16].rearrange("p r (b t) -> p b r t", b=4)
                                for b4 in range(4):
                                    ins = act.copy(d[:, b4], o[:, b4, kv])
                            ins.then_inc(hb_ready, 1)

                    for h in range(MH):
                        act.copy(ha_high[h], haT[:, h, :]).then_inc(ha_high_ready, 1)
                    att_exp(0)
                    att_exp(1)
                    att_scale(0)
                    for v in range(2):
                        act.wait_ge(w1_used, 4 * (v + 1))
                        link(act.copy(hbias[:, v:v + 1], ps[:, HIDDEN_BANK[v][0], NBLK:NBLK + 1]))
                        for g in range(NKV):
                            ins = act.activation(hid[:, v, g, :], ps[:, HIDDEN_BANK[v][g], 0:NBLK], ACT.Gelu_apprx_tanh, bias=hbias[:, v:v + 1])
                        ins.then_inc(hid_ready, 1)
                    act.wait_ge(cmp_done, 1)
                    act.copy(kcT, ps[:, 0, 0:NBLK])
                    act.copy(vcp[0:NCP, :], ps[0:NCP, 5, 0:P])
                    act.copy(vcs, ps[:, 5, P:2 * P]).then_inc(cmp_ready, 1)

                    att_exp(2)
                    for k in range(NSTEP):
                        if k and k - 1 in ENDS:
                            outputs(k - 1)
                        if k + 1 < NSTEP:
                            att_scale(k + 1)
                        for x, blocks in chunks_of(k):
                            if evac_on_act(x):
                                rows, cols = evac_shape(k, blocks)
                                act.wait_ge(t_done, x + 1)
                                if x >= 2:
                                    act.wait_ge(o_done, x - 1)
                                if STEPS[k][0] is not None or blocks[0][0] == 0:
                                    act.copy(PT[0:rows, x % 2, 0:cols], ps[0:rows, 5 + x % 2, 0:cols]).then_inc(t_free[x % 2], 1)
                                else:
                                    act.copy(PT[:, x % 2, 0:2 * P], ps[:, 5 + x % 2, 0:2 * P])
                                    act.copy(PT[0:NS, x % 2, 2 * P:3 * P], ps[0:NS, 5 + x % 2, 2 * P:3 * P]).then_inc(t_free[x % 2], 1)
                        for n in range(3, NSTEP):
                            if exp_turn(n) == k:
                                att_exp(n)
                        if k in (LAST_PROMPT + 1, LAST_PROMPT + 2):
                            act.wait_ge(s_done, LAST_PROMPT + 1)
                            act.wait_ge(qb_ready, 1)
                            split_high(LSPLIT + k - LAST_PROMPT - 1)
                    outputs(NSTEP - 1)
                    act.wait_ge(nsa_stored, 48)
                    split_high(LSPLIT + 2)
                    act.wait_ge(hb_ready, len(ENDS))
                    for r in range(R):
                        act.copy(hb_high[r], hbT[:, r, :]).then_inc(hb_high_ready, 1)
                    for what, key in late_events():
                        name, m = key
                        if what == "unit":
                            split_high(SPLIT[key] + SRING)
                        elif name in ("ga", "gb"):
                            out, free = done(key)
                            n = 0 if name == "ga" else 1
                            if m >= 1:
                                read_out(act, (("a", "b")[n], m - 1))
                            act.activation(halves(sg[:, n, :]), out, ACT.Sigmoid).then_inc(free, 1)
                        elif name == "out":
                            read_out(act, key)
                            square(m, 0)
                            if m == KC - 1:
                                root(("n2", 0))
                                for k in range(KC):
                                    act.wait_ge(t_ready, k + 1)
                                    act.copy(xh[:, k, :], tbuf[:, k % 2, :]).then_inc(th_ready, 1)
                        elif name == "dn" and m >= KC:
                            read_out(act, key)
                            square(m - KC, KC - 1)
                        elif name == "fg":
                            out, free = done(key)
                            if m >= 2:
                                read_out(act, ("fu", m - 2))
                            act.activation(halves(sg[:, m % 2, :]), out, ACT.Silu).then_inc(free, 1)

                @block.vector
                def _(dve):
                    steps = [0]

                    def link(ins):
                        steps[0] += 1
                        ins.then_inc(dve_step, 1)
                        dve.wait_ge(dve_step, steps[0])

                    def done(key):
                        q = GROUP[key]
                        dve.wait_ge(pair_done, q + 1)
                        return pair(q), pair_free[q % 4]

                    def add_square(k, time):
                        dve.wait_ge(sq_ready, time * KC + k + 1)
                        if time or k > 1:
                            dve.wait_ge(sq_used, time * (KC - 1) + k - 1)
                        dve.tensor_tensor(acc[:, :], acc[:, :], sq[:, k % 2, :], ALU.add).then_inc(sq_used, 1)

                    def split_low(n):
                        if n >= len(SPLITS):
                            return
                        u = UNIT[SPLITS[n]]
                        dve.wait_ge(wh_ready, n + 1)
                        hi, lo, _ = split_weights(n)
                        dve.tensor_tensor(lo, ring[:, u % RING, :], hi.bitcast(F32),
                                          ALU.subtract).then_inc(wl_ready, 1)

                    def split(t, hi, lo, ready):
                        link(dve.tensor_copy(hi, t))
                        dve.tensor_tensor(lo, t, hi.bitcast(F32), ALU.subtract).then_inc(ready, 1)

                    dve.wait_ge(scales_landed, 16)
                    read_out(dve, ("n1", 0))
                    link(dve.reciprocal(rstd[:, :], rstd[:, :]))
                    for k in range(KC):
                        dve.scalar_tensor_tensor(out=hT[:, k, :], in0=xT[:, k, :], scalar=sml("n1g")[:, k:k + 1], in1=rstd[:, :],
                                                 op0=ALU.mult, op1=ALU.mult).then_inc(h_ready, 1)
                    dve.wait_ge(history_ready, 1)
                    cw = sml("cw", "p (c j) -> p c j", c=4)
                    for m in range(4):
                        read_out(dve, ("u", m))
                        if m >= 2:
                            dve.wait_ge(c_ready, m - 1)
                        us = upad[:, m, 3 + SEQ:UW].rearrange("p (b t) -> p b t", b=DECB)
                        up, dp = upad[:, m, 0:3 + SEQ], ctmp[:, m % 2, 0:SEQ]
                        dsm = ctmp[:, m % 2, SEQ:N].rearrange("p (b t) -> p b t", b=DECB)
                        dve.tensor_scalar(dp, up[:, 0:SEQ], cw[:, m, 0:1], sml("cb")[:, m:m + 1], ALU.mult, ALU.add)
                        link(dve.tensor_scalar(dsm, us[:, :, 0:DECT], cw[:, m, 0:1], sml("cb")[:, m:m + 1], ALU.mult, ALU.add))
                        for j in range(1, CONV):
                            dve.scalar_tensor_tensor(out=dp, in0=up[:, j:j + SEQ], scalar=cw[:, m, j:j + 1], in1=dp, op0=ALU.mult, op1=ALU.add)
                            ins = dve.scalar_tensor_tensor(out=dsm, in0=us[:, :, j:j + DECT], scalar=cw[:, m, j:j + 1], in1=dsm,
                                                           op0=ALU.mult, op1=ALU.add)
                            if j < CONV - 1:
                                link(ins)
                            else:
                                ins.then_inc(conv_ready, 1)
                    split_low(0)
                    split_low(1)
                    dve.wait_ge(pair_done, GROUP[("if", 0)] + 1)
                    for k in range(KC):
                        dve.wait_ge(xh_ready, k + 1)
                        dve.tensor_tensor(xl[:, k, :], hT[:, k, :], xh[:, k, :].bitcast(F32), ALU.subtract).then_inc(xl_ready, 1)
                    dve.wait_ge(small_landed, 16)
                    dve.wait_ge(ln_ready, 1)
                    lf = row(Z_)
                    link(dve.scalar_tensor_tensor(out=lf, in0=row(Z_), scalar=0.0, in1=row(L_), op0=ALU.min, op1=ALU.subtract))
                    dve.memset(row(A_), 1.0)
                    m0 = sml("m0")[0:MH, :]
                    fs, ms, ls, is_ = (per_seq(r[:, SEQ:N]) for r in (row(F_), row(M_), lf, row(I_)))
                    link(dve.tensor_tensor_scan(out=row(M_)[:, 0:SEQ], data0=lf[:, 0:SEQ], data1=row(I_)[:, 0:SEQ], initial=0.0,
                                                op0=ALU.add, op1=ALU.max))
                    dve.tensor_tensor_scan(out=row(F_)[:, 0:SEQ], data0=row(A_)[:, 0:SEQ], data1=lf[:, 0:SEQ], initial=0.0,
                                           op0=ALU.mult, op1=ALU.add)
                    for t in range(DECT):
                        link(dve.tensor_tensor(ms[:, :, t], m0 if t == 0 else ms[:, :, t - 1], ls[:, :, t], ALU.add))
                        dve.tensor_tensor(ms[:, :, t], ms[:, :, t], is_[:, :, t], ALU.max)
                        link(dve.tensor_copy(fs[:, :, t], ls[:, :, t]) if t == 0 else
                             dve.tensor_tensor(fs[:, :, t], fs[:, :, t - 1], ls[:, :, t], ALU.add))
                    dve.tensor_tensor(row(A_), row(I_), row(F_), ALU.subtract)
                    link(dve.tensor_tensor(row(G_), row(F_), row(M_), ALU.subtract))
                    gs = per_seq(row(G_)[:, SEQ:N])
                    dve.tensor_tensor(per_seq(introw), gs, bc(m0.unsqueeze(2), [MH, DECB, DECT]), ALU.add)
                    dve.tensor_tensor(per_seq(tmprow), per_seq(row(A_)[:, SEQ:N]), bc(gs[:, :, DECT - 1:DECT], [MH, DECB, DECT]),
                                      ALU.add).then_inc(rows_ready, 1)
                    split_low(2)
                    split_low(3)
                    q = GROUP[("aw", 0)]
                    done(("aw", 0))
                    dve.tensor_copy(awt[:, 0:TT].rearrange("p i a h -> p (i a h)"), ps[:, 2 * (q % 4), 0:TT * 2 * MH])
                    dve.tensor_copy(awt[0:NS, TT].rearrange("p a h -> p (a h)"),
                                    ps[0:NS, 2 * (q % 4), TT * 2 * MH:(TT + 1) * 2 * MH]).then_inc(pair_free[q % 4], 1)
                    read_out(dve, ("aw", 0))
                    for i in range(TT + 1):
                        rows = P if i < TT else NS
                        done(("kw", i))
                        q = GROUP[("kw", i)]
                        for h in range(MH):
                            ins = dve.tensor_scalar(kw[0:rows, i, h * MD:(h + 1) * MD], ps[0:rows, 2 * (q % 4), h * MD:(h + 1) * MD],
                                                    awt[0:rows, i, 1, h:h + 1], MD ** -0.5, ALU.mult, ALU.mult)
                        ins.then_inc(pair_free[q % 4], 1)
                    for name in ("mq", "mk"):
                        for h in range(MH):
                            read_out(dve, (name, h))

                    dve.wait_ge(const_landed, 16)

                    def masked(k):
                        h, j = divmod(k, TT + 1)
                        dve.wait_ge(bc_ready, 2 * h + 1)
                        if k >= 2:
                            dve.wait_ge(e_ready, k - 1)
                        if j < TT:
                            dve.tensor_tensor(gmask[:, k % 2, :], gbc[:, h % 2, j * P:(j + 1) * P], con("sneg"), ALU.add).then_inc(gm_ready, 1)
                        else:
                            dve.tensor_tensor(gmask[0:NS, k % 2, 0:NS], gbc[0:NS, h % 2, SEQ:N], con("m32")[0:NS, :], ALU.add).then_inc(gm_ready, 1)

                    def new_states(h):
                        dve.wait_ge(cs_done, h + 1)
                        dve.wait_ge(c_decayed, h + 1)
                        C = Cst[:, h % 2]
                        n0 = sml("n0", "p (h b) -> p h b", h=MH)[:, h, :]
                        dec = per_seq(inter[:, h % 2, :])[:, :, DECT - 1:DECT]
                        link(dve.tensor_tensor(nstat[:, h, 1:1 + DECB], n0, dec.rearrange("p b o -> p (b o)"), ALU.mult))
                        dve.tensor_tensor(nstat[:, h, 1:1 + DECB], nstat[:, h, 1:1 + DECB], ps[:, 5, 0:DECB], ALU.add)
                        dve.tensor_tensor(C.rearrange("p (a b) e -> p a (b e)", a=2), C.rearrange("p (a b) e -> p a (b e)", a=2),
                                          ps[:, 6:8, :], ALU.add).then_inc(head_fin, 1)

                    def quotient(h):
                        dve.wait_ge(den_read, h + 1)
                        link(dve.reciprocal(enm[:, h % 2, :], enm[:, h % 2, :]))
                        dve.wait_ge(num_copied, h + 1)
                        dve.tensor_tensor(qm[:, h, :], qm[:, h, :], enm[:, h % 2, :], ALU.mult).then_inc(num_ready, 1)

                    masked(0)
                    masked(1)
                    for k in range(MH * (TT + 1)):
                        h, j = divmod(k, TT + 1)
                        if j == 0:
                            if h >= 1:
                                dve.wait_ge(nd_done, h * (TT + 1))
                            dve.wait_ge(bc_ready, 2 * h + 2)
                            link(dve.tensor_tensor(qi[:, 0, :], qm[:, h, SEQ:N], inter[:, h % 2, :], ALU.mult))
                            n0 = sml("n0", "p (h b) -> p h b", h=MH)[:, h, :]
                            dve.tensor_tensor(per_seq(qi[:, 1, :]), per_seq(qi[:, 0, :]), bc(n0.unsqueeze(2), [P, DECB, DECT]),
                                              ALU.mult).then_inc(qi_ready, 1)
                        dve.wait_ge(e_ready, k + 1)
                        dve.wait_ge(ms_done, k + 1)
                        if k >= 2:
                            dve.wait_ge(nd_done, k - 1)
                        if j < TT:
                            w = SEQ - j * P
                            dve.tensor_tensor(St[:, k % 2, 0:w], ps[:, k % 2, 0:w], Et[:, k % 2, 0:w], ALU.mult).then_inc(st_ready, 1)
                        else:
                            dve.tensor_tensor(St[0:NS, k % 2, 0:NS], ps[0:NS, k % 2, 0:NS], Et[0:NS, k % 2, 0:NS], ALU.mult).then_inc(st_ready, 1)
                        if k + 2 < MH * (TT + 1):
                            masked(k + 2)
                        if j == 0 and h >= 1:
                            quotient(h - 1)
                        if j == 1 and h >= 1:
                            new_states(h - 1)
                        if j == TT:
                            dve.wait_ge(nd_done, (h + 1) * (TT + 1))
                            parts = ((ps[:, 3, :], enm[:, h % 2, 0:SEQ]), (ps[:, 4, NS:2 * NS], enm[:, h % 2, SEQ:N]))
                            for den, en in parts:
                                ins = dve.scalar_tensor_tensor(out=en, in0=den, scalar=-1.0, in1=en, op0=ALU.mult, op1=ALU.max)
                            link(ins)
                            for den, en in parts:
                                dve.tensor_tensor(en, den, en, ALU.max)
                            dve.tensor_copy(qm[:, h, SEQ:N], ps[:, 4, 0:NS]).then_inc(den_read, 1)
                    quotient(MH - 1)
                    new_states(MH - 1)
                    dve.wait_ge(pc_done, 1)
                    dve.tensor_copy(nstat[:, :, 0], ps[:, 1, 0:MH]).then_inc(pn_ready, 1)
                    split_low(QSPLIT)
                    split_low(QSPLIT + 1)
                    for h in range(MH):
                        read_out(dve, ("mn", h))
                        link(dve.reciprocal(rstd[:, :], rstd[:, :]))
                        link(dve.scalar_tensor_tensor(out=qm[:, h, :], in0=qm[:, h, :], scalar=sml("mng")[:, h:h + 1], in1=rstd[:, :],
                                                      op0=ALU.mult, op1=ALU.mult))
                        dve.tensor_tensor(haT[:, h, :], haT[:, h, :], qm[:, h, :], ALU.mult).then_inc(ha_ready, 1)
                        if h:
                            split_low(QSPLIT + 1 + h)
                    def arrange(n):
                        dve.wait_ge(page_landed[n % 4], 16 * (n // 4 + 1))
                        at = (SEQ + n * PAGE) // STRIDE
                        for v in range(2):
                            ins = dve.tensor_copy(raw[:, v, :, at:at + PAGE // STRIDE].rearrange("p l n -> p n l"),
                                                  stage[:, n % 4, v, :].rearrange("p (n l) -> p n l", l=STRIDE))
                        ins.then_inc(page_arranged, 1)

                    split_low(QSPLIT + 5)
                    for n in range(10):
                        arrange(n)
                    for turned, n in enumerate(ROPE_ORDER):
                        out, free = done(("rope", n))
                        src = qT[:, n, :] if n < 4 else kT[:, n - 4, :]
                        dst = qrT[:, n, :] if n < 4 else kT[:, n - 4, :]
                        if turned:
                            dve.wait_ge(rope_ready, turned)
                        dve.tensor_tensor(halves(rtmp[:, 0, :]), out, halves(sin), ALU.mult).then_inc(free, 1)
                        link(dve.tensor_tensor(rtmp[:, 1, :], src, cos, ALU.mult))
                        dve.tensor_tensor(dst, rtmp[:, 0, :], rtmp[:, 1, :], ALU.add).then_inc(rope_ready, 1)
                        if turned < 2:
                            split_low(QSPLIT + 6 + turned)
                        arrange(10 + turned)
                    dve.wait_ge(rope_ready, 6)
                    dve.wait_ge(qb_cleared, 1)
                    for a, src in enumerate((qT, qrT)):
                        for g in range(NKV):
                            for r in range(R):
                                ins = dve.tensor_copy(qb[g * HD:(g + 1) * HD, a, :, g * 16 + r * 4:g * 16 + r * 4 + 4],
                                                      per_seq(src[g * HD:(g + 1) * HD, r, SEQ:N]))
                    ins.then_inc(qb_ready, 1)

                    dve.wait_ge(gs_done, 1)
                    for hb in range(2):
                        gall = ps[:, 7, hb * 24:(hb + 1) * 24].rearrange("p (h b) -> p b h", b=3)
                        link(dve.tensor_tensor(gtmp[:, :, :], gall, bc(con("rowm").unsqueeze(1), [P, 3, NH]), ALU.mult))
                        ins = dve.tensor_reduce(gsel[:, hb, :], gtmp[:, :, :], AX.X, ALU.add)
                        link(ins) if hb == 0 else ins.then_inc(gs_read, 1)

                    def mask_of(k):
                        i, g, _, _, brs, _ = STEPS[k]
                        if i is None:
                            return (kneg[:, g, :], 0) if brs == (0,) else (nneg[:, g, :], PAST)
                        return (cneg[:, i, :], 0) if brs == (0,) else (con("qneg"), i * P)

                    def gates_of(k):
                        i, g, r0, heads, brs, _ = STEPS[k]
                        if i is None:
                            return gsel[:, g, brs[0]:brs[0] + 1].unsqueeze(1)
                        return gate[:, i, :].rearrange("p (h b) -> p h b", b=3)[:, g * R + r0:g * R + r0 + heads, brs[0]:brs[-1] + 1]

                    def masked_scores(k):
                        dve.wait_ge(s_done, k + 1)
                        mask, lo = mask_of(k)
                        t = score(k)[:, :, lo:width_of(k)]
                        return dve.tensor_tensor(t, t, bc(mask.unsqueeze(1), [P, parts_of(k), width_of(k) - lo]), ALU.add)

                    def att_max(k):
                        dve.tensor_reduce(stat[:, k % 3, 0:parts_of(k)], score(k), AX.X, ALU.max, negate=True).then_inc(max_ready, 1)

                    def weight_and_max(k, m):
                        ins = None
                        if k is not None:
                            n, brs = parts_of(k), len(STEPS[k][4])
                            dve.wait_ge(exp_done, k + 1)
                            total = stat[:, 3 + k % 3, 0:n]
                            if not own_total(k):
                                link(dve.tensor_tensor(prob(k), prob(k), bc(c01[:, STEPS[k][0], :].unsqueeze(1), [P, n, NCP]), ALU.mult))
                                link(dve.tensor_reduce(total, prob(k), AX.X, ALU.add))
                            ins = dve.tensor_scalar(stat[:, 6, 0:n], total, TINY, None, ALU.max)
                        if m is not None:
                            ins = masked_scores(m)
                        link(ins)
                        if k is not None:
                            ins = dve.reciprocal(stat[:, 7, 0:n], stat[:, 6, 0:n])
                            if STEPS[k][0] is None:
                                dve.wait_ge(gs_read, 1)
                            if k >= 3:
                                dve.wait_ge(p_ready, scaled_through(k - 3))
                            link(ins)
                            ins = dve.tensor_tensor(stat[:, 8 + k % 3, 0:n].rearrange("p (h b) -> p h b", b=brs),
                                              stat[:, 7, 0:n].rearrange("p (h b) -> p h b", b=brs), gates_of(k), ALU.mult)
                            if own_total(k):
                                ins.then_inc(weight_ready, 1)
                            else:
                                link(ins)
                                dve.tensor_tensor(prob(k), prob(k), bc(stat[:, 8 + k % 3, 0:n].unsqueeze(2), [P, n, NCP]),
                                                  ALU.mult).then_inc(cp_ready, 1)
                        if m is not None:
                            att_max(m)

                    weight_and_max(None, 0)
                    weight_and_max(None, 1)
                    weight_and_max(0, None)
                    for h in range(MH):
                        dve.wait_ge(ha_high_ready, h + 1)
                        dve.tensor_tensor(ha_low[:, h, :], haT[:, h, :], ha_high[h].bitcast(F32), ALU.subtract).then_inc(ha_low_ready, 1)
                    weight_and_max(1, 2)
                    for k in range(NSTEP):
                        if 1 < k + 1 < NSTEP and exp_turn(k + 1) == k - 1:
                            weight_and_max(k + 1, None)
                        for x, blocks in chunks_of(k):
                            if not evac_on_act(x):
                                rows, cols = evac_shape(k, blocks)
                                dve.wait_ge(t_done, x + 1)
                                if x >= 2:
                                    dve.wait_ge(o_done, x - 1)
                                dve.tensor_copy(PT[0:rows, x % 2, 0:cols], ps[0:rows, 5 + x % 2, 0:cols]).then_inc(t_free[x % 2], 1)
                        early = k + 2 if k + 2 < NSTEP and exp_turn(k + 2) < k else None
                        later = k + 3 if k + 3 < NSTEP else None
                        if early is not None or later is not None:
                            weight_and_max(early, later)
                        if k in (LAST_PROMPT + 1, LAST_PROMPT + 2):
                            split_low(LSPLIT + k - LAST_PROMPT - 1)
                    dve.wait_ge(hb_ready, len(ENDS))
                    dve.wait_ge(nsa_stored, 48)
                    split_low(LSPLIT + 2)
                    for r in range(R):
                        dve.wait_ge(hb_high_ready, r + 1)
                        dve.tensor_tensor(hb_low[:, r, :], hbT[:, r, :], hb_high[r].bitcast(F32), ALU.subtract).then_inc(hb_low_ready, 1)
                    for what, key in late_events():
                        name, m = key
                        if what == "unit":
                            split_low(SPLIT[key] + SRING)
                        elif name in ("a", "b"):
                            n = 0 if name == "a" else 1
                            if m and n == 0:
                                dve.wait_ge(merged_ready, m)
                            read_out(dve, (("ga", "gb")[n], m))
                            out, free = done(key)
                            dve.tensor_tensor(halves(mt[:, n, :]), out, halves(sg[:, n, :]), ALU.mult).then_inc(free, 1)
                            if n == 1:
                                read_out(dve, ("a", m))
                                read_out(dve, ("b", m))
                                link(dve.tensor_tensor(tbuf[:, 0, :], mt[:, 0, :], mt[:, 1, :], ALU.add))
                                split(tbuf[:, 0, :], mh[:, m, :], ml[:, m, :], merged_ready)
                        elif name in ("out", "dn"):
                            out, free = done(key)
                            c = m % KC
                            dve.tensor_tensor(halves(xT[:, c, :]), halves(xT[:, c, :]), out, ALU.add).then_inc(free, 1)
                            if name == "out" and m >= 1:
                                add_square(m, 0)
                            if name == "dn" and m > KC:
                                add_square(m - KC, 1)
                            if name == "out" and m == KC - 1:
                                read_out(dve, ("n2", 0))
                                link(dve.reciprocal(rstd[:, :], rstd[:, :]))

                                def scaled(k):
                                    if k >= 2:
                                        dve.wait_ge(xl_ready, KC + k - 1)
                                    dve.scalar_tensor_tensor(out=tbuf[:, k % 2, :], in0=xT[:, k, :], scalar=sml("n2g")[:, k:k + 1],
                                                             in1=rstd[:, :], op0=ALU.mult, op1=ALU.mult).then_inc(t_ready, 1)

                                dve.wait_ge(merged_ready, KC)
                                scaled(0)
                                for k in range(KC):
                                    if k + 1 < KC:
                                        scaled(k + 1)
                                    dve.wait_ge(th_ready, k + 1)
                                    dve.tensor_tensor(xl[:, k, :], tbuf[:, k % 2, :], xh[:, k, :].bitcast(F32),
                                                      ALU.subtract).then_inc(xl_ready, 1)
                        elif name == "fu":
                            read_out(dve, ("fg", m))
                            out, free = done(key)
                            if m >= 1:
                                dve.wait_ge(act_ready, m)
                            dve.tensor_tensor(halves(tbuf[:, 0, :]), out, halves(sg[:, m % 2, :]), ALU.mult).then_inc(free, 1)
                            read_out(dve, key)
                            if m % NFH == 0:
                                dve.wait_ge(pair_done, GROUP[key] + 1)
                            split(tbuf[:, 0, :], ah[:, m % NFH, :], al(m % NFH), act_ready)

            for s in layer_sems:
                nc.sync.sem_clear(s)
            nc.all_engine_barrier()

        yT = slab[:, MIX_AT:MIX_AT + KC * N].rearrange("p (k n) -> p k n", k=KC)
        fin_done = ctx.enter_context(nc.semaphore("fin_done"))
        fin_root = ctx.enter_context(nc.semaphore("fin_root"))
        fin_step = ctx.enter_context(nc.semaphore("fin_step"))
        fin_y = ctx.enter_context(nc.semaphore("fin_y"))
        fin_stored = ctx.enter_context(nc.semaphore("fin_stored"))
        with nc.Block() as block:
            @block.scalar
            def _(act):
                act.wait_ge(fin_done, 1)
                act.activation(halves(rstd[:, :]), ps[:, 0:2, 0:NHALF], ACT.Sqrt, bias=eps[:, :], scale=1.0 / D).then_inc(fin_root, 1)

            @block.tensor
            def _(pe):
                for a in range(2):
                    mm = pe.matmul(ps[:, a, 0:NHALF], ones[:, :], acc[:, a * NHALF:(a + 1) * NHALF], start=True, stop=True)
                mm.then_inc(fin_done, 1)

            @block.vector
            def _(dve):
                dve.wait_ge(fin_root, 1)
                dve.reciprocal(rstd[:, :], rstd[:, :]).then_inc(fin_step, 1)
                dve.wait_ge(fin_step, 1)
                fng = con("fng")
                for k in range(KC):
                    dve.scalar_tensor_tensor(out=yT[:, k, :], in0=xT[:, k, :], scalar=fng[:, k:k + 1], in1=rstd[:, :],
                                             op0=ALU.mult, op1=ALU.mult).then_inc(fin_y, 1)

            @block.sync
            def _(sp):
                for k in range(KC):
                    sp.wait_ge(fin_y, k + 1)
                    sp.dma_start(y_out[:, k, :], yT[:, k, :]).then_inc(fin_stored, 16)
                sp.wait_ge(fin_stored, 16 * KC)


def shape_constants():
    c = np.zeros((P, CONST_W), np.float32)

    def put(name, value):
        a, b = CONST[name]
        v = np.asarray(value, np.float32)
        v = v.reshape(v.shape[0], -1)
        c[:v.shape[0], a:b] = v

    pos = np.concatenate([np.arange(SEQ), np.tile(PAST + np.arange(DECT), DECB)]).astype(np.float32)
    half = HD // 8
    inv = (np.float32(500000.0) ** (-np.arange(half, dtype=np.float32) / np.float32(half))).astype(np.float32)
    ang = (pos[None, :] * inv[:, None]).astype(np.float32)
    cos, sin, rot = np.ones((P, N)), np.zeros((P, N)), np.zeros((P, P))
    for g in range(NKV):
        for a in range(2):
            cos[g * HD + a * half:g * HD + (a + 1) * half] = np.cos(ang.astype(np.float64))
            sin[g * HD + a * half:g * HD + (a + 1) * half] = np.sin(ang.astype(np.float64))
        for d in range(half):
            rot[g * HD + half + d, g * HD + d] = -1.0
            rot[g * HD + d, g * HD + half + d] = 1.0
    put("cos", cos)
    put("sin", sin)
    put("rot", rot)
    put("ident", np.eye(P))
    t = np.arange(P)
    put("qneg", np.where(t[None, :] <= t[:, None], 0.0, NEG))
    put("sneg", np.where(t[:, None] <= t[None, :], 0.0, NEG))
    q = t[:, None, None] + P * np.arange(TT)[None, :, None]
    seen = np.arange(NCP)[None, None, :] * STRIDE + CLEN - 1 <= q
    put("cneg", np.where(seen, 0.0, NEG))
    put("c01", seen)
    put("sel4", np.repeat(np.eye(MH)[:, :, None], P, 2))
    s = np.arange(NS)
    same = s[:, None] // DECT == s[None, :] // DECT
    put("m32", np.where(same & (s[:, None] <= s[None, :]), 0.0, NEG))
    put("blk", s[:, None] // DECT == np.arange(DECB)[None, :])
    b4, g, r, tok = t // 32, t // 16 % 2, t // 4 % 4, t % 4
    b = b4[:, None] + 4 * np.arange(2)[None, :]
    put("nneg", np.where((b[:, :, None] == s // DECT) & (s % DECT <= tok[:, None, None]), 0.0, NEG))
    put("kneg", np.where((b[:, :, None] == t // SBLK) & (t % SBLK < SBLK - 1), 0.0, NEG))
    put("tsel", s[:, None, None] == (b * DECT + tok[:, None]).T[None])
    put("rowm", (g * R + r)[:, None] == np.arange(NH)[None, :])
    return c


def chunked(a):
    return a.reshape(-1, P, a.shape[-1]).transpose(1, 0, 2)


def weight_units(l, w):
    w_in = w["w_in"][l]
    at = np.cumsum([0, 512, 512, 512, 4, 4, 512, 768, 24, D, D])
    u, v, o, ig, fg, q, kv, ng, ga, gb = (w_in[:, a:b] for a, b in zip(at[:-1], at[1:]))
    kv = kv.reshape(D, 6, P)
    q = q.reshape(D, NKV, R, HD).transpose(0, 2, 1, 3).reshape(D, 512)
    out = np.zeros((len(UNITS), P, UCOLS), np.float32)

    def put(key, a):
        a = np.ascontiguousarray(a).reshape(P, -1)
        out[UNIT[key], :, :a.shape[1]] = a

    tm = np.concatenate([v, kv[:, 3], kv[:, 5], ng], 1)
    for k in range(KC):
        put(("tm", k), tm[k * P:(k + 1) * P])
    gates = np.zeros((D, P), np.float32)
    gates[:, 0:MH] = ig
    gates[:, 32:32 + MH] = fg
    put(("if", 0), chunked(gates))
    kk = kv[:, [0, 1, 2, 4]].reshape(D, 512)
    for m in range(4):
        for name, a in (("u", u), ("o", o), ("q", q), ("k", kk)):
            put((name, m), chunked(a[:, m * P:(m + 1) * P]))
    for v2, name in enumerate(("cmp_w1_k", "cmp_w1_v")):
        w1 = w[name][l].transpose(1, 0, 2)
        w1 = np.concatenate([w1, w1], 0)
        for n in range(4):
            put(("w1", 4 * v2 + n), w1[:, 8 * n:8 * n + 8])
    wb = w["w_branch_b"][l].reshape(NKV, R, HD, D).transpose(1, 0, 2, 3).reshape(512, D)
    for m in range(KC):
        c = slice(m * P, (m + 1) * P)
        put(("ga", m), chunked(ga[:, c]))
        put(("gb", m), chunked(gb[:, c]))
        put(("ab", m), np.concatenate([chunked(w["w_branch_a"][l][:, c]), chunked(wb[:, c])], 1))
        put(("out", m), chunked(w["w_out"][l][:, c]))
    dn = w["w_ffn_down"][l].reshape(2, NFH, P, KC, P).transpose(0, 3, 1, 2, 4).reshape(2, NFH, 8, P, P)
    for n in range(2 * NFH):
        put(("dn", n), dn[n // NFH, n % NFH].transpose(1, 0, 2))
    for m in range(NFF):
        put(("fg", m), chunked(w["w_ffn_up"][l][:, m * P:(m + 1) * P]))
        put(("fu", m), chunked(w["w_ffn_up"][l][:, (NFF + m) * P:(NFF + m + 1) * P]))
    return out


def small_weights(l, w):
    out = np.zeros((P, SMALL_W), np.float32)

    def put(name, a):
        a = np.ascontiguousarray(a)
        a = a.reshape(a.shape[0], -1)
        lo, hi = SMALL[name]
        out[:a.shape[0], lo:lo + a.shape[1]] = a

    def vec(a):
        return a.reshape(-1, P).T

    put("n1g", vec(w["norm1_g"][l]))
    put("n2g", vec(w["norm2_g"][l]))
    put("mng", vec(w["mlstm_norm_g"][l]))
    put("cw", w["conv_w"][l].reshape(CONV, 4, P).transpose(2, 1, 0))
    put("cb", vec(w["conv_b"][l]))
    put("wmq", w["w_mq"][l].transpose(1, 0, 2))
    put("wmk", w["w_mk"][l].transpose(1, 0, 2))
    put("w2", np.stack([w["cmp_w2_k"][l], w["cmp_w2_v"][l]], 1))
    pe = np.stack([w["cmp_pe_k"][l].T, w["cmp_pe_v"][l].T], 1)
    put("pe", np.concatenate([pe, pe], 0))
    put("bi", w["b_gates"][l][:MH, None])
    put("bf", w["b_gates"][l][MH:, None])
    put("m0", w["state_mlstm_m"][l].T)
    put("n0", w["state_mlstm_n"][l].transpose(2, 1, 0))
    put("cs", w["state_mlstm_conv"][l].reshape(DECB, CONV - 1, 4, P).transpose(3, 2, 0, 1))
    return out


def kernel(**inputs):
    import concourse.bacc as bacc
    from concourse.bass_utils import run_bass_kernel_spmd

    w = {k: np.asarray(v) for k, v in inputs.items()}
    x = np.concatenate([w["x_prompt"].reshape(SEQ, D), w["x_sample"].reshape(NS, D)], 0)
    const = shape_constants()
    a, b = CONST["fng"]
    const[:, a:b] = w["final_norm_g"].reshape(KC, P).T
    pages = w["cache_kv_pages"]
    pool = pages.shape[1]
    pg = pages.reshape(DEPTH, pool, PAGE, 4, P)
    turned = pg[:, :, :, 0:3].transpose(0, 1, 4, 3, 2).reshape(DEPTH, pool, P, 3 * PAGE)
    packed = np.concatenate([turned, pg[:, :, :, 3]], 3)
    cw = w["cache_win"].reshape(DEPTH, DECB, PAST, 2, P)
    wk = cw[:, :, :, 0].transpose(0, 3, 1, 2)
    wv = cw[:, :, :, 1].reshape(DEPTH, DECB, NPG, P, P).transpose(0, 3, 1, 2, 4).reshape(DEPTH, P, DECB, PAST)
    win = np.stack([wk, wv], 3).reshape(DEPTH, P, DECB * 2 * PAST)
    arrays = {
        "xT": chunked(np.ascontiguousarray(x.T)),
        "W": np.stack([weight_units(l, w) for l in range(DEPTH)]),
        "small": np.stack([small_weights(l, w) for l in range(DEPTH)]),
        "consts": const,
        "c0": w["state_mlstm_C"].transpose(0, 2, 3, 1, 4).reshape(DEPTH, MH, P, DECB * MD),
        "pages": packed,
        "table": w["page_table"].reshape(1, -1).astype(np.int32),
        "win": win,
        "cwin": w["cache_win"].reshape(DEPTH, DECB, PAST * 2 * P),
    }
    outs = {
        "y": (P, KC, N), "fm": (DEPTH, P, 2, N), "raw": (DEPTH, P, 2, STRIDE, PBLK), "knew": (DEPTH, P, 2, NS), "tm": (DEPTH, P, TT + 1, 2 * P), "u": (DEPTH, P, 4, UW - SEQ),
        "pC": (DEPTH, P, MH * MD), "pn": (DEPTH, P, MH * (1 + DECB)), "m": (DEPTH, MH, N),
        "sC": (DEPTH, MH, P, DECB * MD), "oldwin": (DEPTH, DECB, (PAST - DECT) * 2 * P),
    }
    nc = bacc.Bacc("TRN2", target_bir_lowering=False, num_devices=1)
    ins, args = {}, []
    for name, v in arrays.items():
        v = np.ascontiguousarray(v)
        ins["in_" + name] = v
        args.append(nc.dram_tensor("in_" + name, v.shape, mybir.dt.from_np(v.dtype), kind="ExternalInput").ap())
    oap = {n: nc.dram_tensor("out_" + n, s, F32, kind="ExternalOutput").ap() for n, s in outs.items()}
    build_step(nc, *args, *(oap[n] for n in ("y", "fm", "raw", "knew", "tm", "u", "pC", "pn", "m", "sC", "oldwin")))
    got = run_bass_kernel_spmd(nc, [ins], core_ids=[0]).results[0]
    o = {n: np.asarray(got["out_" + n]) for n in outs}

    y = o["y"].transpose(2, 1, 0).reshape(N, D)
    fm, tmv = o["fm"], o["tm"]
    ks, kwin = (fm[:, :, n].transpose(0, 2, 1) for n in range(2))
    raw = o["raw"].transpose(0, 2, 4, 3, 1).reshape(DEPTH, 2, SEQ, P)
    raw = np.concatenate([raw, o["knew"].transpose(0, 2, 3, 1)], 2)
    kc, vc = raw[:, 0], raw[:, 1]
    tok = np.concatenate([tmv[:, :, :TT].transpose(0, 2, 1, 3).reshape(DEPTH, SEQ, 2 * P), tmv[:, :NS, TT]], 1)
    vs, vw = tok[..., :P], tok[..., P:]
    rows = np.stack([kc, vc, ks, vs], 2).reshape(DEPTH, N, 4, NKV, HD)
    wins = np.stack([kwin, vw], 2).reshape(DEPTH, N, 2, NKV, HD)
    old = o["oldwin"].reshape(DEPTH, DECB, PAST - DECT, 2, NKV, HD)
    u = o["u"]
    hist = CONV - 1
    p_conv = u[..., :hist].transpose(0, 3, 2, 1).reshape(DEPTH, 1, hist, 512)
    s_conv = u[..., hist:].reshape(DEPTH, P, 4, DECB, hist + DECT)[..., DECT:].transpose(0, 3, 4, 2, 1).reshape(DEPTH, DECB, hist, 512)
    n_ = o["pn"].reshape(DEPTH, P, MH, 1 + DECB).transpose(0, 3, 2, 1)
    m_ = o["m"]
    got = (
        y[:SEQ].reshape(1, SEQ, D), y[SEQ:].reshape(DECB, DECT, D),
        rows[:, None, :SEQ], wins[:, None, :SEQ],
        o["pC"].reshape(DEPTH, P, MH, MD).transpose(0, 2, 1, 3)[:, None], n_[:, 0:1], m_[:, None, :, SEQ - 1], p_conv,
        rows[:, SEQ:].reshape(DEPTH, DECB, DECT, 4, NKV, HD),
        np.concatenate([old, wins[:, SEQ:].reshape(DEPTH, DECB, DECT, 2, NKV, HD)], 2),
        o["sC"].reshape(DEPTH, MH, P, DECB, MD).transpose(0, 3, 1, 2, 4), n_[:, 1:],
        m_[:, :, SEQ:].reshape(DEPTH, MH, DECB, DECT)[..., -1].transpose(0, 2, 1), s_conv,
    )
    return tuple(np.ascontiguousarray(a) for a in got)
```
